# Optimizing a Trainium2 kernel written in Bass

```python
import jax
import jax.numpy as jnp
from jax import lax
import numpy as np

D_MODEL = 1024
BATCH = 1
SEQ = 2048
DEPTH = 2
DEC_BATCH = 8
DEC_SEQ = 4
PAST_LEN = 4096
PAGE_SIZE = 128

N_MIXERS = 2
N_A = (DEPTH + 1) // 2
N_B = DEPTH // 2
D_PLE = 256
EPS = 1e-6
D_RNN = D_MODEL
N_LRU_BLOCKS = 8
LRU_BLOCK = D_RNN // N_LRU_BLOCKS
CONV_W = 4
LRU_C = 8.0
HEAD_DIM = 64
N_HEADS = D_MODEL // HEAD_DIM
N_KV = N_HEADS // 4
GROUP = N_HEADS // N_KV
Q_W = N_HEADS * HEAD_DIM
KV_W = N_KV * HEAD_DIM
D_ATT = Q_W
WINDOW = 128
BLOCK = 128
ALIBI_MAX = 8.0
NEG_INF = -1e30

kernel_name = 'hybrid_rglru_swa_sink_decoder_step'

def _rmsnorm(x, g):
    xf = x.astype(jnp.float32)
    xf = xf * lax.rsqrt(jnp.mean(xf * xf, axis=-1, keepdims=True) + EPS)
    return (xf * g.astype(jnp.float32)).astype(x.dtype)

def _alibi_slopes():
    return jnp.exp2(-ALIBI_MAX * jnp.arange(1, N_HEADS + 1, dtype=jnp.float32) / N_HEADS)

def _causal_conv(x, prev, w, b):
    T = x.shape[1]
    xp = jnp.concatenate([prev.astype(x.dtype), x], axis=1)
    y = b
    for k in range(CONV_W):
        y = y + xp[:, k:k + T] * w[k]
    return y, xp[:, -(CONV_W - 1):]

def _block_diag(x, w, b):
    xb = x.reshape(x.shape[:-1] + (N_LRU_BLOCKS, LRU_BLOCK))
    return jnp.einsum('...nc,ncd->...nd', xb, w).reshape(x.shape) + b

def _rg_lru(xc, h0, wr, br, wi, bi, lam):
    xf = xc.astype(jnp.float32)
    r = jax.nn.sigmoid(_block_diag(xf, wr.astype(jnp.float32), br.astype(jnp.float32)))
    i = jax.nn.sigmoid(_block_diag(xf, wi.astype(jnp.float32), bi.astype(jnp.float32)))
    log_a = -LRU_C * r * jax.nn.softplus(-lam.astype(jnp.float32))
    a = jnp.exp(log_a)
    b = jnp.sqrt(-jnp.expm1(2.0 * log_a)) * (i * xf)
    b = b.at[:, 0].add(a[:, 0] * h0.astype(jnp.float32))

    def combine(left, right):
        return left[0] * right[0], right[0] * left[1] + right[1]

    _, h = lax.associative_scan(combine, (a, b), axis=1)
    return h, h[:, -1]

def _mixer_a(u, h0, conv_prev, w_in, cw, cb, wr, br, wi, bi, lam, w_out):
    xg = u @ w_in
    xb, gate = xg[..., :D_RNN], xg[..., D_RNN:]
    xc, conv_new = _causal_conv(xb, conv_prev, cw, cb)
    h, h_last = _rg_lru(xc, h0, wr, br, wi, bi, lam)
    y = (h.astype(u.dtype) * jax.nn.silu(gate)) @ w_out
    return y, h_last, conv_new

def _sink_attention(q, k, v, dist, valid, sinks, slopes):
    s = jnp.einsum('...qkgd,...skd->...kgqs', q.astype(jnp.float32), k.astype(jnp.float32)) * (HEAD_DIM ** -0.5)
    s = s - slopes[:, :, None, None] * dist.astype(jnp.float32)
    s = jnp.where(valid, s, NEG_INF)
    sink_col = jnp.broadcast_to(sinks.astype(jnp.float32)[:, :, None, None], s.shape[:-1] + (1,))
    p = jax.nn.softmax(jnp.concatenate([s, sink_col], axis=-1), axis=-1)[..., :-1]
    return jnp.einsum('...kgqs,...skd->...qkgd', p, v.astype(jnp.float32))

def _mixer_b(u, kbuf, vbuf, w_in, sinks, w_out):
    Bn, T, _ = u.shape
    proj = u @ w_in
    q = proj[..., :Q_W].reshape(Bn, T, N_KV, GROUP, HEAD_DIM)
    k = proj[..., Q_W:Q_W + KV_W].reshape(Bn, T, N_KV, HEAD_DIM)
    v = proj[..., Q_W + KV_W:Q_W + 2 * KV_W].reshape(Bn, T, N_KV, HEAD_DIM)
    gate = proj[..., Q_W + 2 * KV_W:]
    sink = sinks.reshape(N_KV, GROUP)
    slopes = _alibi_slopes().reshape(N_KV, GROUP)
    if kbuf is None:
        nb = T // BLOCK
        qb = q.reshape(Bn, nb, BLOCK, N_KV, GROUP, HEAD_DIM)
        kb = k.reshape(Bn, nb, BLOCK, N_KV, HEAD_DIM)
        vb = v.reshape(Bn, nb, BLOCK, N_KV, HEAD_DIM)

        def band(xb):
            prev = jnp.concatenate([jnp.zeros_like(xb[:, :1]), xb[:, :-1]], axis=1)
            return jnp.concatenate([prev, xb], axis=2)

        qi = jnp.arange(BLOCK)[:, None]
        si = jnp.arange(2 * BLOCK)[None, :]
        dist = BLOCK + qi - si
        blk = jnp.arange(nb)[:, None, None]
        valid = (dist >= 0) & (dist < WINDOW) & ((blk - 1) * BLOCK + si >= 0)
        o = _sink_attention(qb, band(kb), band(vb), dist, valid[:, None, None], sink, slopes)
        new_k, new_v = k[:, -WINDOW:], v[:, -WINDOW:]
    else:
        W = kbuf.shape[1]
        k_all = jnp.concatenate([kbuf.astype(k.dtype), k], axis=1)
        v_all = jnp.concatenate([vbuf.astype(v.dtype), v], axis=1)
        qi = jnp.arange(T)[:, None]
        si = jnp.arange(W + T)[None, :]
        dist = W + qi - si
        valid = (dist >= 0) & (dist < WINDOW)
        o = _sink_attention(q, k_all, v_all, dist, valid, sink, slopes)
        new_k, new_v = k_all[:, -WINDOW:], v_all[:, -WINDOW:]
    o = o.reshape(Bn, T, Q_W).astype(u.dtype)
    return (o * jax.nn.silu(gate)) @ w_out, new_k, new_v

def _trunk(x, p, lru_h, conv_st, kc, vc, weights):
    (norm_g, final_norm_g, ple_norm_g, w_ple_gate, w_ple_proj, w_in_a, conv_w_a, conv_b_a,
     w_rgate, b_rgate, w_igate, b_igate, lru_lambda, w_out_a, w_in_b, sinks, w_out_b) = weights
    Bn = x.shape[0]
    new_h, new_conv, new_k, new_v = [], [], [], []
    h = x
    for i in range(DEPTH):
        j = i // N_MIXERS
        u = _rmsnorm(h, norm_g[i])
        if i % N_MIXERS == 0:
            h0 = jnp.zeros((Bn, D_RNN), jnp.float32) if lru_h is None else lru_h[j]
            cprev = jnp.zeros((Bn, CONV_W - 1, D_RNN), x.dtype) if conv_st is None else conv_st[j]
            y, hl, cn = _mixer_a(u, h0, cprev, w_in_a[j], conv_w_a[j], conv_b_a[j], w_rgate[j], b_rgate[j],
                                 w_igate[j], b_igate[j], lru_lambda[j], w_out_a[j])
            new_h.append(hl)
            new_conv.append(cn)
        else:
            y, nk, nv = _mixer_b(u, None if kc is None else kc[j], None if vc is None else vc[j],
                                 w_in_b[j], sinks[j], w_out_b[j])
            new_k.append(nk)
            new_v.append(nv)
        h = h + y
        gate = jax.nn.sigmoid((_rmsnorm(h, ple_norm_g[i]) @ w_ple_gate[i]).astype(jnp.float32)).astype(h.dtype)
        h = h + gate * (p[i] @ w_ple_proj[i])
    return (_rmsnorm(h, final_norm_g), jnp.stack(new_h), jnp.stack(new_conv), jnp.stack(new_k), jnp.stack(new_v))

def setup_inputs(seed: int = 0) -> dict:
    key = jax.random.key(seed)
    ks = jax.random.split(key, 26)

    def nrm(k, shape, scale):
        return jax.random.normal(k, shape, jnp.float32) * scale

    a0 = jax.random.uniform(ks[20], (N_A, D_RNN), jnp.float32, 0.9, 0.999)
    s0 = a0 ** (1.0 / LRU_C)
    return {
        'x_prompt': nrm(ks[0], (BATCH, SEQ, D_MODEL), 1.0),
        'x_sample': nrm(ks[1], (DEC_BATCH, DEC_SEQ, D_MODEL), 1.0),
        'p_prompt': nrm(ks[2], (DEPTH, BATCH, SEQ, D_PLE), 1.0),
        'p_sample': nrm(ks[3], (DEPTH, DEC_BATCH, DEC_SEQ, D_PLE), 1.0),
        'state_lru_h': nrm(ks[4], (N_A, DEC_BATCH, D_RNN), 0.5),
        'state_conv': nrm(ks[5], (N_A, DEC_BATCH, CONV_W - 1, D_RNN), 1.0),
        'cache_k': nrm(ks[6], (N_B, DEC_BATCH, WINDOW, N_KV, HEAD_DIM), 1.0),
        'cache_v': nrm(ks[7], (N_B, DEC_BATCH, WINDOW, N_KV, HEAD_DIM), 1.0),
        'norm_g': 1.0 + nrm(ks[8], (DEPTH, D_MODEL), 0.02),
        'final_norm_g': 1.0 + nrm(ks[9], (D_MODEL,), 0.02),
        'ple_norm_g': 1.0 + nrm(ks[10], (DEPTH, D_MODEL), 0.02),
        'w_ple_gate': nrm(ks[11], (DEPTH, D_MODEL, D_MODEL), D_MODEL ** -0.5),
        'w_ple_proj': nrm(ks[12], (DEPTH, D_PLE, D_MODEL), D_PLE ** -0.5),
        'w_in_a': nrm(ks[13], (N_A, D_MODEL, 2 * D_RNN), D_MODEL ** -0.5),
        'conv_w_a': nrm(ks[14], (N_A, CONV_W, D_RNN), CONV_W ** -0.5),
        'conv_b_a': nrm(ks[15], (N_A, D_RNN), 0.01),
        'w_rgate': nrm(ks[16], (N_A, N_LRU_BLOCKS, LRU_BLOCK, LRU_BLOCK), LRU_BLOCK ** -0.5),
        'b_rgate': nrm(ks[17], (N_A, D_RNN), 0.01),
        'w_igate': nrm(ks[18], (N_A, N_LRU_BLOCKS, LRU_BLOCK, LRU_BLOCK), LRU_BLOCK ** -0.5),
        'b_igate': nrm(ks[19], (N_A, D_RNN), 0.01),
        'lru_lambda': jnp.log(s0) - jnp.log1p(-s0),
        'w_out_a': nrm(ks[21], (N_A, D_RNN, D_MODEL), D_RNN ** -0.5),
        'w_in_b': nrm(ks[22], (N_B, D_MODEL, Q_W + 2 * KV_W + D_ATT), D_MODEL ** -0.5),
        'sinks': nrm(ks[23], (N_B, N_HEADS), 0.5),
        'w_out_b': nrm(ks[24], (N_B, D_ATT, D_MODEL), D_ATT ** -0.5),
    }

def reference(x_prompt, x_sample, p_prompt, p_sample, state_lru_h, state_conv, cache_k, cache_v,
              norm_g, final_norm_g, ple_norm_g, w_ple_gate, w_ple_proj, w_in_a, conv_w_a, conv_b_a,
              w_rgate, b_rgate, w_igate, b_igate, lru_lambda, w_out_a, w_in_b, sinks, w_out_b):
    weights = (norm_g, final_norm_g, ple_norm_g, w_ple_gate, w_ple_proj, w_in_a, conv_w_a, conv_b_a,
               w_rgate, b_rgate, w_igate, b_igate, lru_lambda, w_out_a, w_in_b, sinks, w_out_b)
    y_prompt, h_p, conv_p, k_p, v_p = _trunk(x_prompt, p_prompt, None, None, None, None, weights)
    y_sample, h_s, conv_s, k_s, v_s = _trunk(x_sample, p_sample, state_lru_h, state_conv, cache_k, cache_v, weights)
    return (y_prompt, y_sample, h_p, conv_p, k_p, v_p, h_s, conv_s, k_s, v_s)


_drawn_inputs = setup_inputs


def setup_inputs(seed=0):
    import zlib

    import numpy as np

    out = dict(_drawn_inputs(seed))
    spreads = {}
    factors = {'final_norm_g': 8.11, 'ple_norm_g': 29.313, 'b_rgate': 8.0, 'b_igate': 8.0, 'sinks': 7.054}
    for name, (base, spread) in spreads.items():
        noise = np.random.default_rng([zlib.crc32(name.encode()), seed]).standard_normal(out[name].shape)
        drawn = base * np.exp(spread * noise) if base else spread * noise
        out[name] = jnp.asarray(drawn.astype(out[name].dtype))
    for name, factor in factors.items():
        out[name] = (out[name] * factor).astype(out[name].dtype)
    return out
```

```python
from contextlib import ExitStack

import concourse.bass as bass
from concourse import mybir

F32 = mybir.dt.float32
F32R = mybir.dt.float32r
ALU = mybir.AluOpType
ACT = mybir.ActivationFunctionType
AX_X = mybir.AxisListType.X

D = 1024
KT = D // 128
SEQ = 2048
GROUPS = 4
TP = SEQ // GROUPS
NSEQ, ST = 8, 4
SG = NSEQ // GROUPS
TS = SG * ST
T = TP + TS
C = T // 2
TB = C - TS
TAPS = 4
PREV = TAPS - 1
SEG = PREV + ST
PAD = 2
FLAT = TP + PAD + SG * SEG
XBW = FLAT + PREV
S0 = TP + PAD
NH, HD, NKV = 16, 64, 4
WIN = 128
BLK = 128
NB = TP // BLK
NU = NB * NKV
SW = WIN + ST
EPS = 1e-6
MASKED = 1e33

ORDER = [("X", 0), ("X", 1), ("X", 2)]
for _n in range(5):
    ORDER += [("G", _n), ("X", _n + 3)]
ORDER += [("G", 5), ("G", 6), ("G", 7)]
O0 = len(ORDER)
ORDER += [("O", m) for m in range(KT)]
Z0 = len(ORDER)
for _m in range(KT):
    ORDER += [("Z", _m), ("P", _m)]
L1 = len(ORDER)
ORDER += [("k", 0), ("k", 1), ("v", 0), ("v", 1)]
Q1 = len(ORDER)
ORDER += [("q", m) for m in range(KT)]
G1 = len(ORDER)
ORDER += [("g", m) for m in range(KT)]
O1 = len(ORDER)
ORDER += [("o", m) for m in range(KT)]
Z1 = len(ORDER)
for _m in range(KT):
    ORDER += [("z", _m), ("p", _m)]
NBLK = len(ORDER)
AT = {b: c for c, b in enumerate(ORDER)}
RING, STAGE = 3, 2
assert NBLK % RING == 0 and NBLK % STAGE == 0

RI_BEFORE = {2: 0, 3: 1}
RI_BEFORE.update({2 * n: n for n in range(2, KT)})

PAIR = []
_turn = 0
for _b in ORDER:
    if _b[0] in "Pp" or _b == ("v", 0):
        PAIR.append(3)
    else:
        PAIR.append(_turn)
        _turn ^= 1


def before_in_pair(c):
    return next(p for p in range(c - 1, c - NBLK - 1, -1) if PAIR[p % NBLK] == PAIR[c])


FREE_HEAD = 4


def is_small(c):
    return ORDER[c % NBLK][0] in "Pp"


def slope(head):
    return 2.0 ** (-8.0 * (head + 1) / NH)


V_G0, V_G1, V_P0, V_P1, V_FIN = 0, 8, 16, 24, 32
V_CW, V_CB, V_BR, V_BI, V_LAM, V_SINK, V_SINKS = 40, 72, 80, 88, 96, 104, 120
NVEC = 124

N_IN0, N_FIN, N_PL0, N_IN1, N_PL1 = range(5)
NORMS = 5

DVE_CHAIN, ACT_CHAIN = 146, 8


class Stage:

    def __init__(self, nc, ctx, name, per, head=0, step=1):
        self.sem = ctx.enter_context(nc.semaphore(name))
        self.per, self.head, self.step = per, head, step

    def at(self, g, n):
        if isinstance(g, tuple):
            g, n = g[0], n + g[1] * self.per
        assert (isinstance(g, int) and g) or self.head + n > 0
        return g * (self.per * self.step) + (self.head + n) * self.step


def build(nc, A):
    ctx = ExitStack()
    with ctx:
        base = 16512
        place = [base]

        def sb_at(name, shape, dt, offset):
            return nc.alloc_sbuf_tensor_at(name, [128] + list(shape), dt, offset=offset)

        def sb(name, shape, dt=F32):
            n = 4
            for s in shape:
                n *= s
            off = place[0]
            place[0] += (n + 31) // 32 * 32
            return sb_at(name, shape, dt, off)

        H = sb("resid", [KT, T])
        a_at = place[0]
        Ahi = sb("a_hi", [KT, T], F32R)
        Alo = sb("a_lo", [KT, T], F32R)
        Bhi = sb("b_hi", [KT, T], F32R)
        Blo = sb("b_lo", [KT, T], F32R)
        Q = sb_at("q", [KT, T], F32, a_at)
        LR = sb("lru_or_o", [4, FLAT])
        p_at = place[0]
        Phi = sb("p_hi", [2, T], F32R)
        Plo = sb("p_lo", [2, T], F32R)
        KS = sb_at("ks", [2, SG, SW], F32, p_at)
        KSX = sb_at("ks_swapped", [2, SG, SW], F32, p_at + 4 * 2 * SG * SW)
        VS = sb_at("vs", [SG, NKV * HD], F32, p_at + 8 * 2 * SG * SW)
        VN = sb_at("vs_new", [SG, NKV * HD], F32, p_at + 8 * 2 * SG * SW + 4 * SG * NKV * HD)
        assert 8 * 2 * SG * SW + 8 * SG * NKV * HD <= 16 * T
        WH = sb("w_hi", [RING, KT, 128], F32R)
        WL = sb("w_lo", [RING, KT, 128], F32R)
        WS = sb("w_stage", [STAGE, KT, 128])
        WRI = sb("w_ri", [2 * KT, 128])
        K = sb("k", [2, BLK + TP])
        KX = sb("k_swapped", [2, BLK + TP])
        V = sb("v", [1 + NB, NKV * HD])
        t_at = place[0]
        XB = sb("conv_in", [2, XBW])
        XC = sb("conv_out", [2, FLAT])
        TR = sb("gate_r", [FLAT])
        AA = sb("decay", [FLAT])
        TH = sb("decay_th", [FLAT])
        TI = sb("gate_i", [FLAT])
        SC = sb_at("scores", [3, 4, 2 * BLK], F32, t_at)
        PT = sb_at("probs_t", [2, 4 * BLK], F32, t_at + 12288)
        VT = sb_at("v_t", [2, T], F32, t_at)
        PS_ = sb_at("p_stage", [2, T], F32, t_at)
        XS = sb_at("x_stage", [2, T], F32, t_at + 8 * T)
        assert 16384 <= place[0] - t_at and 16 * T <= place[0] - t_at
        GH = sb("gate_half", [2, T])
        TG = sb("gate_tanh", [2, T])
        R = sb("inv_rms", [T])
        RN = sb("inv_rms_in0", [T])
        SQ = sb("square", [2, T])
        ACC = sb("square_sum", [T])
        ACCN = sb("square_sum_in0", [T])
        DIST = sb("dist", [2 * BLK])
        DIST0 = sb("dist_first", [2 * BLK])
        TBS = sb("bias_s", [2, SG * SW])
        IDN = sb("identity", [128])
        ONE = sb("ones", [128])
        VEC = sb("vec", [NVEC])
        C1 = sb("lru_c", [2, KT])
        EPT = sb("eps", [1])
        QS = sb("qs", [SG, NKV, 32])
        OS = sb("os", [KT, TS])
        HC = sb("h_carry", [KT])
        HST = sb("h_state", [KT, SG])
        HSO = sb("h_state_out", [KT, SG])
        CC = sb("conv_carry", [KT, PREV])
        CST = sb("conv_state", [KT, SG, PREV])
        CSO = sb("conv_state_out", [KT, SG, PREV])
        MX = sb("row_max", [4, 4])
        NM = sb("row_max_neg", [4, 4])
        ES = sb("sink_exp", [4, 4])
        DEN = sb("row_sum", [4, 4])
        SP = sb("softplus_tmp", [6, KT])
        assert place[0] <= nc.sbuf_usable_end, place[0]

        PSUM = ctx.enter_context(nc.psum_tensor("psum", [128, 8, 512], F32))

        def pair(p):
            return PSUM[:, 2 * p:2 * p + 2, 0:C]

        def halves(ap):
            return ap.rearrange("p (a c) -> p a c", a=2)

        def samples(ap):
            return ap.rearrange("p (s t) -> p s t", t=ST)

        def segments(ap):
            return ap.rearrange("p (s w) -> p s w", w=SEG)

        def stage(name, per, head=0, step=1):
            return Stage(nc, ctx, name, per, head, step)

        consts_in = stage("consts_in", 0, step=16)
        memset_done = stage("memset_done", 0)
        dve_setup = stage("dve_setup", 0)
        act_setup = stage("act_setup", 0)
        w_in = [stage(f"w_in{i}", NBLK // STAGE, step=16) for i in range(STAGE)]
        w_hi = stage("w_hi_done", NBLK)
        w_lo = stage("w_lo_done", NBLK)
        proj_done = stage("proj_done", NBLK, head=1)
        proj_free = stage("proj_free", NBLK, head=FREE_HEAD)
        x_in = [stage(f"x_in{i}", KT // 2, step=16) for i in range(2)]
        h_in = stage("h_in", 1, head=1, step=16)
        state_in = stage("state_in", 2, step=16)
        state_out = stage("state_out", 2, step=16)
        p_in = stage("p_in", 2, step=16)
        ks_in = stage("ks_in", 3, step=16)
        kv_out = stage("kv_out", 3, step=16)
        k_swapped = stage("k_swapped_in", 4, step=16)
        y_out = stage("y_out", 1, step=16)
        end_out = stage("end_out", 0, step=16)
        ops = ("in0", "y0", "pl0", "in1", "y1", "pl1")
        hi = {o: stage(o + "_hi", KT) for o in ops}
        lo = {o: stage(o + "_lo", KT) for o in ops}
        p_hi, p_lo = stage("p_hi_done", 2), stage("p_lo_done", 2)
        norms = ("in0", "fin", "pl0", "in1", "pl1")
        squared = {o: stage("sq_" + o, KT) for o in norms}
        added = {o: stage("add_" + o, KT - 1, head=int(o == "fin")) for o in norms}
        ms_done = stage("ms_done", NORMS)
        root_done = stage("root_done", NORMS)
        h_new = {o: stage("h_" + o, KT) for o in ("in1", "fin")}
        y_fin = stage("y_fin", KT)
        xc_done = stage("xc_done", KT)
        ri_done = stage("ri_done", KT)
        ri_read = stage("ri_read", KT)
        decay_done = stage("decay_done", KT)
        q2_done = stage("q2_done", KT)
        q2_root = stage("q2_root", KT)
        lru_done = stage("lru_done", KT)
        tanh_done = stage("tanh_done", 4 * KT)
        y_val = {o: stage(o + "_val", KT) for o in ("y0", "y1")}
        v_turned = stage("v_turned", 2)
        v_ready = stage("v_ready", 2)
        q_ready = stage("q_ready", 1)
        s_done = stage("s_done", NU + 1)
        s_read = stage("s_read", NU + 1)
        nm_ready = stage("nm_ready", NU + 1)
        exp_done = stage("exp_done", NU + 1)
        p_ready = stage("p_ready", NU + 1)
        t_done = stage("t_done", NU + 1)
        pt_ready = stage("pt_ready", NU + 1)
        o_done = stage("o_done", NU + 1)
        o_read = stage("o_read", NU)
        os_read = stage("os_read", 1)
        carry_done = stage("carry_done", 1)
        dve_chain = stage("dve_chain", DVE_CHAIN)
        act_chain = stage("act_chain", ACT_CHAIN)

        block = ctx.enter_context(nc.Block())

        @block.sync
        def _(sp):
            def load_weights(g, j):
                if not (isinstance(g, int) and j < STAGE):
                    sp.wait_ge(w_lo.sem, w_lo.at(g, j - STAGE + 1))
                c, s = j % NBLK, j % STAGE
                if is_small(c):
                    n = KT * (ORDER[c][0] == "p") + ORDER[c][1]
                    sp.dma_start(WS[:, s, 0:2, :], A["w_small"][n]).then_inc(w_in[s].sem, 16)
                else:
                    n = sum(not is_small(x) for x in range(c))
                    sp.dma_start(WS[:, s, :, :], A["w_big"][n]).then_inc(w_in[s].sem, 16)

            def group_of(ap, g):
                if isinstance(g, int):
                    return ap[g]
                v = ap[bass.ds(g, 1)]
                if len(ap.shape) == 3:
                    return v.rearrange("a p x -> (a p) x")
                if len(ap.shape) == 4:
                    return v.rearrange("a p x y -> (a p) x y")
                return v.rearrange("a p x y z -> (a p) x y z")

            def load_x(g, k, group):
                if k >= 2 or not isinstance(g, int):
                    sp.wait_ge(lo["in0"].sem, lo["in0"].at(g, k - 1))
                sp.dma_start(XS[:, k % 2, :], group_of(A["x"], group)[:, k, :]).then_inc(x_in[k % 2].sem, 16)

            load_x(0, 0, 0)
            load_x(0, 1, 0)
            for dst, src in ((VEC[:], A["vec"]), (DIST[:], A["dist"][0]), (DIST0[:], A["dist"][1]),
                             (TBS[:], A["bias_s"]), (IDN[:], A["ident"]), (WRI[:], A["w_ri"])):
                sp.dma_start(dst, src).then_inc(consts_in.sem, 16)
            load_weights(0, 0)
            load_weights(0, 1)
            sp.dma_start(H[:], A["x"][0]).then_inc(h_in.sem, 16)
            for k in range(2, KT):
                load_x(0, k, 0)

            with sp.Fori(0, GROUPS) as g:
                for c in range(NBLK):
                    load_weights(g, c + STAGE)
                    if c == 0:
                        sp.dma_start(CST[:], group_of(A["conv_state"], g)).then_inc(state_in.sem, 16)
                        sp.dma_start(HST[:], group_of(A["h_state"], g)).then_inc(state_in.sem, 16)
                    if c == 11:
                        sp.wait_ge(y_fin.sem, y_fin.at(g, KT))
                        sp.dma_start(group_of(A["y_out"], g), H[:]).then_inc(y_out.sem, 16)
                    if c == 14:
                        sp.wait_ge(y_out.sem, y_out.at(g, 1))
                        sp.dma_start(H[:], group_of(A["x"], g)).then_inc(h_in.sem, 16)
                    if c == O0 + 4:
                        sp.wait_ge(proj_done.sem, proj_done.at(g, O0 + 1))
                        sp.dma_start(PS_[:], group_of(A["p0"], g)).then_inc(p_in.sem, 16)
                        sp.dma_start(group_of(A["h_state_out"], g), HSO[:]).then_inc(state_out.sem, 16)
                        sp.dma_start(group_of(A["conv_state_out"], g), CSO[:]).then_inc(state_out.sem, 16)
                    if c == L1 + 3:
                        sp.wait_ge(proj_done.sem, proj_done.at(g, L1))
                        sp.dma_start(KS[:, :, :, 0:WIN], group_of(A["k_cache"], g)).then_inc(ks_in.sem, 16)
                        sp.dma_start(KSX[:, :, :, 0:WIN], group_of(A["k_cache_x"], g)).then_inc(ks_in.sem, 16)
                        sp.dma_start(VS[:], group_of(A["v_cache"], g)).then_inc(ks_in.sem, 16)
                    if c == Q1 + 1:
                        sp.wait_ge(proj_free.sem, proj_free.at(g, AT["k", 1] + 1))
                        for a in (0, 64):
                            b = 64 - a
                            sp.dma_start(KX[a:a + 64, :, BLK:], K[b:b + 64, :, BLK:]).then_inc(k_swapped.sem, 16)
                            sp.dma_start(KSX[a:a + 64, :, :, WIN:], KS[b:b + 64, :, :, WIN:]).then_inc(k_swapped.sem, 16)
                    if c == Q1 + 6:
                        sp.wait_ge(ks_in.sem, ks_in.at(g, 3))
                        sp.wait_ge(v_ready.sem, v_ready.at(g, 2))
                        sp.dma_start(group_of(A["ks_out"], g),
                                     KS[:, :, :, ST:]).then_inc(kv_out.sem, 16)
                        vo = group_of(A["vs_out"], g)
                        sp.dma_start(vo[0:WIN - ST], VS[ST:]).then_inc(kv_out.sem, 16)
                        sp.dma_start(vo[WIN - ST:], VN[0:ST]).then_inc(kv_out.sem, 16)
                    if c == O1 + 4:
                        sp.wait_ge(proj_done.sem, proj_done.at(g, O1 + 1))
                        sp.dma_start(PS_[:], group_of(A["p1"], g)).then_inc(p_in.sem, 16)
                    if c > Z1 and (c - Z1) % 2:
                        load_x((g, 1), (c - Z1) // 2, g + 1)

            sp.wait_ge(y_fin.sem, y_fin.at(GROUPS, KT))
            sp.dma_start(A["y_out"][GROUPS], H[:]).then_inc(end_out.sem, 16)
            sp.wait_ge(carry_done.sem, carry_done.at(GROUPS, 0))
            sp.dma_start(A["h_out"], HC[:]).then_inc(end_out.sem, 16)
            sp.dma_start(A["conv_out"], CC[:]).then_inc(end_out.sem, 16)
            sp.dma_start(A["k_out"], K[:, :, 0:BLK]).then_inc(end_out.sem, 16)
            sp.dma_start(A["v_out"], V[:, 0, :]).then_inc(end_out.sem, 16)
            sp.wait_ge(end_out.sem, 5 * 16)
            sp.wait_ge(y_out.sem, y_out.at(GROUPS, 0))
            sp.wait_ge(state_out.sem, state_out.at(GROUPS, 0))
            sp.wait_ge(kv_out.sem, kv_out.at(GROUPS, 0))
            for s in range(STAGE):
                sp.wait_ge(w_in[s].sem, w_in[s].at(GROUPS, 1))

        @block.gpsimd
        def _(pool):
            def split_low(g, j):
                n = 2 if is_small(j) else KT
                pool.wait_ge(w_hi.sem, w_hi.at(g, j + 1))
                nc.gpsimd.tensor_tensor(WL[:, j % RING, 0:n, :], WS[:, j % STAGE, 0:n, :],
                                        WH[:, j % RING, 0:n, :].bitcast(F32), ALU.subtract).then_inc(w_lo.sem, 1)

            def add_square(g, o, k):
                acc = ACCN if o == "in0" else ACC
                slot = {"fin": 0, "in0": 1}.get(o, k % 2)
                pool.wait_ge(squared[o].sem, squared[o].at(g, k + 1))
                if k >= 2:
                    pool.wait_ge(added[o].sem, added[o].at(g, k - 1))
                nc.gpsimd.tensor_tensor(acc[:], acc[:], SQ[:, slot, :], ALU.add).then_inc(added[o].sem, 1)

            nc.gpsimd.memset(ONE[:], 1.0).then_inc(memset_done.sem, 1)
            for t in (HC, CC, K, KX, V, QS):
                nc.gpsimd.memset(t[:], 0.0).then_inc(memset_done.sem, 1)
            nc.gpsimd.memset(ACC[:], 0.0).then_inc(added["fin"].sem, 1)
            nc.gpsimd.memset(EPT[:], EPS).then_inc(memset_done.sem, 1)
            split_low(0, 0)
            split_low(0, 1)
            for k in range(1, KT):
                add_square(0, "in0", k)

            with pool.Fori(0, GROUPS) as g:
                for c in range(NBLK):
                    kind, m = ORDER[c - 1] if c else ("", 0)
                    sum_first = m and kind in "Oo" or m == KT - 1
                    if not sum_first:
                        split_low(g, c + 2)
                    if m and kind in "Oo":
                        add_square(g, "pl0" if kind == "O" else "pl1", m)
                    if m and kind == "P":
                        add_square(g, "in1", m)
                    if m and kind == "p":
                        add_square(g, "fin", m)
                        add_square((g, 1), "in0", m)
                    if sum_first:
                        split_low(g, c + 2)
                add_square(g, "fin", KT - 1)
                add_square((g, 1), "in0", KT - 1)

        @block.scalar
        def _(act):
            chain = [0]

            def link(g, ins):
                chain[0] += 1
                ins.then_inc(act_chain.sem, 1)
                act.wait_ge(act_chain.sem, act_chain.at(g, chain[0]))

            def split_high(g, j):
                act.wait_ge(w_in[j % STAGE].sem, w_in[j % STAGE].at(g, j // STAGE + 1))
                if not (isinstance(g, int) and j < RING):
                    act.wait_ge(proj_done.sem, proj_done.at(g, j - RING + 1))
                n = 2 if is_small(j) else KT
                nc.scalar.activation(WH[:, j % RING, 0:n, :], WS[:, j % STAGE, 0:n, :], ACT.Copy).then_inc(w_hi.sem, 1)

            def square(g, o, k, src):
                acc = ACCN if o == "in0" else ACC
                slot = {"fin": 0, "in0": 1}.get(o, k % 2)
                back = 1 if o in ("fin", "in0") else 2
                if k > back:
                    act.wait_ge(added[o].sem, added[o].at(g, k - back))
                nc.scalar.activation(acc[:] if k == 0 else SQ[:, slot, :], src, ACT.Square).then_inc(squared[o].sem, 1)

            def scaled_high(g, o, k, dst, src, col):
                nc.scalar.activation(dst, src, ACT.Copy, scale=VEC[:, col:col + 1]).then_inc(hi[o].sem, 1)

            def x_tile(g, k):
                act.wait_ge(x_in[k % 2].sem, x_in[k % 2].at(g, k // 2 + 1))
                square(g, "in0", k, XS[:, k % 2, :])
                scaled_high(g, "in0", k, Ahi[:, k, :], XS[:, k % 2, :], V_G0 + k)

            def root(g, n, banks, dst):
                act.wait_ge(ms_done.sem, ms_done.at(g, n + 1))
                nc.scalar.activation(halves(dst), PSUM[:, banks:banks + 2, 0:C], ACT.Sqrt, scale=1.0 / D,
                                     bias=EPT[:, 0:1]).then_inc(root_done.sem, 1)

            def gate_tanh(g, c, slot):
                act.wait_ge(proj_free.sem, proj_free.at(g, c + 1))
                nc.scalar.activation(TG[:, slot, :], GH[:, slot, :], ACT.Tanh).then_inc(tanh_done.sem, 1)

            def gates(g, n):
                act.wait_ge(ri_done.sem, ri_done.at(g, n + 1))
                if n:
                    act.wait_ge(lru_done.sem, lru_done.at(g, n))
                hw = FLAT // 2
                two = lambda ap: ap.rearrange("p (a c) -> p a c", a=2)
                nc.scalar.activation(two(TI[:]), PSUM[:, 6:8, 0:hw], ACT.Tanh, scale=0.5,
                                     bias=VEC[:, V_BI + n:V_BI + n + 1])
                nc.scalar.activation(two(TR[:]), PSUM[:, 4:6, 0:hw], ACT.Tanh, scale=0.5,
                                     bias=VEC[:, V_BR + n:V_BR + n + 1]).then_inc(ri_read.sem, 1)
                act.wait_ge(ri_read.sem, ri_read.at(g, n + 1))
                nc.scalar.activation(TH[:], TR[:], ACT.Tanh, scale=C1[:, 1, n:n + 1], bias=C1[:, 1, n:n + 1])
                link(g, nc.scalar.activation(AA[:], TR[:], ACT.Exp, scale=C1[:, 0, n:n + 1], bias=C1[:, 0, n:n + 1]))
                nc.scalar.activation(TR[:], AA[:], ACT.Square).then_inc(decay_done.sem, 1)

            def decay_root(g, n):
                act.wait_ge(q2_done.sem, q2_done.at(g, n + 1))
                nc.scalar.activation(TR[:], TR[:], ACT.Sqrt, scale=0.25).then_inc(q2_root.sem, 1)

            def y_high(g, o, t, dst, slot):
                act.wait_ge(y_val[o].sem, y_val[o].at(g, t + 1))
                nc.scalar.activation(dst[:, t, :], TG[:, slot, :], ACT.Copy).then_inc(hi[o].sem, 1)

            def exps(g, ev, sc, width):
                s = ev if ev == 0 else 1 + (ev - 1) % 3
                act.wait_ge(nm_ready.sem, nm_ready.at(g, ev + 1))
                for i in range(4):
                    nc.scalar.activation(sc[:, i, 0:width], sc[:, i, 0:width], ACT.Exp, bias=NM[:, s, i:i + 1],
                                         accum_out=DEN[:, s, i:i + 1])
                nc.scalar.activation(ES[:, s, :], ES[:, s, :], ACT.Exp).then_inc(exp_done.sem, 1)

            act.wait_ge(consts_in.sem, 6 * 16)
            act.wait_ge(dve_setup.sem, 2)
            nc.scalar.activation(SP[:, 1, :], SP[:, 0, :], ACT.Exp, scale=-1.0).then_inc(act_setup.sem, 1)
            act.wait_ge(dve_setup.sem, 3)
            act.wait_ge(memset_done.sem, 8)
            split_high(0, 0)
            split_high(0, 1)
            for k in range(KT):
                x_tile(0, k)

            with act.Fori(0, GROUPS) as g:
                chain[0] = 0
                for c in range(NBLK):
                    kind, m = ORDER[c]
                    if kind == "g":
                        continue
                    split_high(g, c + 2)
                    if c == 1:
                        root(g, N_IN0, 4, RN[:])
                        root(g, N_FIN, 6, R[:])
                    if c in RI_BEFORE:
                        gates(g, RI_BEFORE[c])
                    if kind == "G":
                        gate_tanh(g, c, m % 2)
                    if c in RI_BEFORE:
                        decay_root(g, RI_BEFORE[c])
                    if kind == "G":
                        y_high(g, "y0", m, Bhi, m % 2)
                    if kind in "Oo":
                        o, V_P, dst = ("pl0", V_P0, Ahi) if kind == "O" else ("pl1", V_P1, Bhi)
                        act.wait_ge(proj_free.sem, proj_free.at(g, c + 1))
                        square(g, o, m, H[:, m, :])
                        scaled_high(g, o, m, dst[:, m, :], H[:, m, :], V_P + m)
                        if m == 6:
                            l = int(kind == "o")
                            act.wait_ge(p_in.sem, p_in.at(g, l + 1))
                            if l:
                                act.wait_ge(kv_out.sem, kv_out.at(g, 3))
                            nc.scalar.activation(Phi[:], PS_[:], ACT.Copy).then_inc(p_hi.sem, 1)
                    if c in (Z0, L1, Z1):
                        root(g, {Z0: N_PL0, L1: N_IN1, Z1: N_PL1}[c], 4, R[:])
                    if kind in "Zz":
                        gate_tanh(g, c, m % 2)
                        if kind == "z":
                            x_tile((g, 1), m)
                    if kind == "P":
                        act.wait_ge(h_new["in1"].sem, h_new["in1"].at(g, m + 1))
                        square(g, "in1", m, H[:, m, :])
                        scaled_high(g, "in1", m, Bhi[:, m, :], H[:, m, :], V_G1 + m)
                    if kind == "p":
                        act.wait_ge(h_new["fin"].sem, h_new["fin"].at(g, m + 1))
                        square(g, "fin", m, H[:, m, :])
                    if c in (Q1 + 1, Q1 + 2):
                        t = c - Q1 - 1
                        act.wait_ge(v_turned.sem, v_turned.at(g, t + 1))
                        nc.scalar.activation(V[:, 1:, t * 128:(t + 1) * 128],
                                             PSUM[:, 6 + t, :].rearrange("p (b f) -> p b f", f=128), ACT.Copy)
                        nc.scalar.activation(VN[0:ST, :, t * 128:(t + 1) * 128],
                                             PSUM[0:ST, 4 + t, 0:SG * 128].rearrange("p (s f) -> p s f", f=128),
                                             ACT.Copy).then_inc(v_ready.sem, 1)
                    if c == G1 - 1:
                        split_high(g, G1 + 2)
                        exps(g, 0, SC[:, 1].rearrange("p a b -> p (a b)")[:, 0:4 * SW].rearrange(
                            "p (i w) -> p i w", w=SW), SW)
                        gate_tanh(g, G1, 0)
                        act.wait_ge(t_done.sem, t_done.at(g, 1))
                        nc.scalar.activation(PT[:, 0, :], PSUM[:, 6, :], ACT.Copy)
                        nc.scalar.activation(PT[0:ST, 1, :], PSUM[0:ST, 7, :], ACT.Copy).then_inc(pt_ready.sem, 1)
                        exps(g, 1, SC[:, 0], 2 * BLK)
                        for u in range(NU):
                            kv, b = divmod(u, NB)
                            if u + 1 < NU:
                                exps(g, u + 2, SC[:, (u + 1) % 3], 2 * BLK)
                            act.wait_ge(t_done.sem, t_done.at(g, u + 2))
                            nc.scalar.activation(PT[:], PSUM[:, 6:8, :], ACT.Copy).then_inc(pt_ready.sem, 1)
                            if u % 2 == 0 and u // 2 + 1 < KT:
                                split_high(g, G1 + u // 2 + 3)
                            act.wait_ge(o_done.sem, o_done.at(g, u + 2))
                            s = 2 * (kv % 2)
                            nc.scalar.activation(LR[:, s:s + 2, b * BLK:(b + 1) * BLK],
                                                 PSUM[:, 6, 0:2 * BLK].rearrange("p (j q) -> p j q", j=2),
                                                 ACT.Copy).then_inc(o_read.sem, 1)
                            if b == NB - 1:
                                for t in (2 * kv, 2 * kv + 1):
                                    y_high(g, "y1", t, Ahi, t % 2)
                            if u % 2 and u // 2 + 1 < KT:
                                gate_tanh(g, G1 + u // 2 + 1, (u // 2 + 1) % 2)
                assert chain[0] == ACT_CHAIN, chain[0]
            act.wait_ge(ms_done.sem, ms_done.at(GROUPS, 1))
            nc.scalar.activation(halves(R[:]), PSUM[:, 6:8, 0:C], ACT.Sqrt, scale=1.0 / D,
                                 bias=EPT[:, 0:1]).then_inc(root_done.sem, 1)

        @block.vector
        def _(dve):
            v = nc.vector
            chain = [0]

            def link(g, ins):
                chain[0] += 1
                ins.then_inc(dve_chain.sem, 1)
                dve.wait_ge(dve_chain.sem, dve_chain.at(g, chain[0]))

            def product(g, c):
                dve.wait_ge(proj_done.sem, proj_done.at(g, c + 1))

            def low(g, o, k, dst_lo, dst_hi, src, col):
                dve.wait_ge(hi[o].sem, hi[o].at(g, k + 1))
                v.scalar_tensor_tensor(dst_lo[:, k, :], src, VEC[:, col:col + 1], dst_hi[:, k, :].bitcast(F32),
                                       ALU.mult, ALU.subtract).then_inc(lo[o].sem, 1)

            def y_low(g, o, k, dst_lo, dst_hi, slot):
                dve.wait_ge(hi[o].sem, hi[o].at(g, k + 1))
                v.tensor_tensor(dst_lo[:, k, :], TG[:, slot, :], dst_hi[:, k, :].bitcast(F32),
                                ALU.subtract).then_inc(lo[o].sem, 1)

            def inverse(g, n, dst):
                dve.wait_ge(root_done.sem, root_done.at(g, n + 1))
                link(g, v.reciprocal(dst, dst))

            def conv(g, n, p):
                xb = XB[:, n % 2, :]
                product(g, AT["X", n])
                seg = segments(xb[:, S0 + PREV:])
                if n == 0:
                    dve.wait_ge(state_in.sem, state_in.at(g, 2))
                v.tensor_copy(seg[:, :, 0:PREV], CST[:, n])
                v.tensor_copy(xb[:, 0:PREV], CC[:, n])
                v.tensor_tensor(xb[:, PREV:PREV + C], PSUM[:, 2 * p, 0:C], RN[:, 0:C], ALU.mult)
                v.tensor_tensor(xb[:, PREV + C:PREV + TP], PSUM[:, 2 * p + 1, 0:TB], RN[:, C:TP], ALU.mult)
                v.tensor_tensor(seg[:, :, PREV:], samples(PSUM[:, 2 * p + 1, TB:C]), samples(RN[:, TP:T]),
                                ALU.mult).then_inc(proj_free.sem, 1)
                dve.wait_ge(proj_free.sem, proj_free.at(g, AT["X", n] + 1))
                xc = XC[:, n % 2, :]
                link(g, v.tensor_scalar(xc, xb[:, 0:FLAT], VEC[:, V_CW + n:V_CW + n + 1],
                                        VEC[:, V_CB + n:V_CB + n + 1], ALU.mult, ALU.add))
                for k in range(1, TAPS):
                    w = V_CW + KT * k + n
                    ins = v.scalar_tensor_tensor(xc, xb[:, k:k + FLAT], VEC[:, w:w + 1], xc, ALU.mult, ALU.add)
                    if k < PREV:
                        link(g, ins)
                    else:
                        ins.then_inc(xc_done.sem, 1)
                v.tensor_copy(CC[:, n], xb[:, TP:TP + PREV])
                v.tensor_copy(CSO[:, n], seg[:, :, SEG - PREV:])

            def recur(g, n):
                dve.wait_ge(decay_done.sem, decay_done.at(g, n + 1))
                v.scalar_tensor_tensor(TR[:], TR[:], 1.0, TH[:], ALU.add, ALU.mult).then_inc(q2_done.sem, 1)
                dve.wait_ge(xc_done.sem, xc_done.at(g, n + 1))
                v.scalar_tensor_tensor(TI[:], TI[:], 1.0, XC[:, n % 2, :], ALU.add, ALU.mult)
                link(g, v.memset(segments(AA[:, S0:])[:, :, PREV - 1], 0.0))
                dve.wait_ge(q2_root.sem, q2_root.at(g, n + 1))
                link(g, v.tensor_tensor(TI[:], TI[:], TR[:], ALU.mult))
                link(g, v.tensor_copy(segments(TI[:, S0:])[:, :, PREV - 1], HST[:, n]))
                link(g, v.tensor_tensor_scan(LR[:, n % 4, :], AA[:], TI[:], HC[:, n:n + 1], ALU.mult, ALU.add))
                v.tensor_copy(HSO[:, n], segments(LR[:, n % 4, S0:])[:, :, SEG - 1])
                v.tensor_copy(HC[:, n:n + 1], LR[:, n % 4, TP - 1:TP]).then_inc(lru_done.sem, 1)

            def half_gate(g, c, slot, r):
                product(g, c)
                v.scalar_tensor_tensor(halves(GH[:, slot, :]), pair(PAIR[c]), 0.5, halves(r), ALU.mult,
                                       ALU.mult).then_inc(proj_free.sem, 1)

            def silu(g, i, slot):
                dve.wait_ge(tanh_done.sem, tanh_done.at(g, i + 1))
                link(g, v.scalar_tensor_tensor(TG[:, slot, :], TG[:, slot, :], 1.0, GH[:, slot, :], ALU.add, ALU.mult))

            def embed(g, c, i, m, o):
                s = m % 2
                dve.wait_ge(tanh_done.sem, tanh_done.at(g, i + 1))
                product(g, c + 1)
                v.scalar_tensor_tensor(halves(GH[:, s, :]), halves(TG[:, s, :]), 1.0, pair(3), ALU.add,
                                       ALU.mult).then_inc(proj_free.sem, 1)
                dve.wait_ge(proj_free.sem, proj_free.at(g, c + 2))
                v.scalar_tensor_tensor(H[:, m, :], GH[:, s, :], 0.5, H[:, m, :], ALU.mult, ALU.add)\
                 .then_inc(h_new[o].sem, 1)

            def final(g, k):
                v.scalar_tensor_tensor(H[:, k, :], H[:, k, :], VEC[:, V_FIN + k:V_FIN + k + 1], R[:], ALU.mult,
                                       ALU.mult).then_inc(y_fin.sem, 1)

            def row_max(g, ev, sc, sink):
                s = ev if ev == 0 else 1 + (ev - 1) % 3
                link(g, v.tensor_reduce(MX[:, s, :], sc, AX_X, ALU.max))
                link(g, v.tensor_tensor(MX[:, s, :], MX[:, s, :], VEC[:, sink:sink + 4], ALU.max))
                v.tensor_scalar(NM[:, s, :], MX[:, s, :], -1.0, None, ALU.mult)
                v.tensor_tensor(ES[:, s, :], VEC[:, sink:sink + 4], MX[:, s, :], ALU.subtract).then_inc(nm_ready.sem, 1)

            def scores(g, u):
                kv, b = divmod(u, NB)
                sc = SC[:, u % 3]
                dve.wait_ge(s_done.sem, s_done.at(g, u + 2))
                for i in range(4):
                    ins = v.scalar_tensor_tensor(sc[:, i, :], DIST[:] if b else DIST0[:],
                                                 -slope(4 * kv + 2 * (i % 2) + i // 2),
                                                 PSUM[:, 4 + i // 2, (i % 2) * 2 * BLK:(i % 2 + 1) * 2 * BLK],
                                                 ALU.mult, ALU.add)
                ins.then_inc(s_read.sem, 1)
                dve.wait_ge(s_read.sem, s_read.at(g, u + 2))
                row_max(g, u + 1, sc, V_SINK + 4 * kv)

            def divide(g, ev, sc, width):
                s = ev if ev == 0 else 1 + (ev - 1) % 3
                dve.wait_ge(exp_done.sem, exp_done.at(g, ev + 1))
                link(g, v.tensor_tensor(DEN[:, s, :], DEN[:, s, :], ES[:, s, :], ALU.add))
                link(g, v.reciprocal(DEN[:, s, :], DEN[:, s, :]))
                for i in range(4):
                    ins = v.tensor_scalar(sc[:, i, 0:width], sc[:, i, 0:width], DEN[:, s, i:i + 1], None, ALU.mult)
                ins.then_inc(p_ready.sem, 1)

            def gated(g, t):
                s = t % 2
                silu(g, 2 * KT + t, s)
                v.tensor_tensor(TG[:, s, 0:TP], TG[:, s, 0:TP], LR[:, t % 4, 0:TP], ALU.mult)
                v.tensor_tensor(TG[:, s, TP:T], TG[:, s, TP:T], OS[:, t, :], ALU.mult).then_inc(y_val["y1"].sem, 1)

            n_set = [0]

            def setup(ins):
                n_set[0] += 1
                ins.then_inc(dve_setup.sem, 1)
                dve.wait_ge(dve_setup.sem, n_set[0])

            dve.wait_ge(consts_in.sem, 6 * 16)
            dve.wait_ge(h_in.sem, 16)
            dve.wait_ge(memset_done.sem, 8)
            lam = VEC[:, V_LAM:V_LAM + KT]
            setup(v.tensor_scalar(SP[:, 5, :], lam, -1.0, None, ALU.mult))
            setup(v.tensor_tensor(SP[:, 0, :], lam, SP[:, 5, :], ALU.max))
            setup(v.tensor_scalar(VEC[:, V_BR:V_BR + 2 * KT], VEC[:, V_BR:V_BR + 2 * KT], 0.5, None, ALU.mult))
            dve.wait_ge(act_setup.sem, 1)
            y = SP[:, 1, :]
            setup(v.tensor_scalar(SP[:, 2, :], y, 2.0, None, ALU.add))
            setup(v.reciprocal(SP[:, 2, :], SP[:, 2, :]))
            setup(v.tensor_tensor(SP[:, 2, :], SP[:, 2, :], y, ALU.mult))
            z, z2, q = SP[:, 2, :], SP[:, 3, :], SP[:, 4, :]
            setup(v.tensor_tensor(z2, z, z, ALU.mult))
            setup(v.tensor_scalar(q, z2, 1.0 / 17, None, ALU.mult))
            for d in (15, 13, 11, 9, 7, 5, 3):
                setup(v.scalar_tensor_tensor(q, q, 1.0 / d, z2, ALU.add, ALU.mult))
            setup(v.scalar_tensor_tensor(q, q, 1.0, z, ALU.add, ALU.mult))
            setup(v.tensor_scalar(SP[:, 5, :], SP[:, 5, :], 0.0, None, ALU.max))
            setup(v.scalar_tensor_tensor(q, q, 2.0, SP[:, 5, :], ALU.mult, ALU.add))
            setup(v.tensor_scalar(C1[:, 0, :], q, -4.0, None, ALU.mult))
            setup(v.tensor_scalar(C1[:, 1, :], q, 4.0, None, ALU.mult))
            for n in range(FREE_HEAD):
                v.memset(SP[:, n, :], 0.0).then_inc(proj_free.sem, 1)
            for k in range(KT):
                low(0, "in0", k, Alo, Ahi, XS[:, k % 2, :], V_G0 + k)

            with dve.Fori(0, GROUPS) as g:
                chain[0] = 0
                dve.wait_ge(lo["in0"].sem, lo["in0"].at(g, KT))
                link(g, v.memset(XB[:, :, PREV + TP:PREV + S0], 0.0))
                for c in range(NBLK):
                    kind, m = ORDER[c]
                    if kind == "g":
                        continue
                    if c == 2:
                        recur(g, 0)
                    if c == 1:
                        inverse(g, N_IN0, RN[:])
                        conv(g, 0, PAIR[0])
                        conv(g, 1, PAIR[1])
                        inverse(g, N_FIN, R[:])
                    if kind == "X" and c > 1:
                        conv(g, m, PAIR[c])
                    if kind == "G":
                        half_gate(g, c, m % 2, RN[:])
                    if c in RI_BEFORE and c > 2:
                        recur(g, RI_BEFORE[c])
                    if kind == "G":
                        silu(g, m, m % 2)
                        v.tensor_tensor(TG[:, m % 2, 0:TP], TG[:, m % 2, 0:TP], LR[:, m % 4, 0:TP], ALU.mult)
                        v.tensor_tensor(samples(TG[:, m % 2, TP:T]), samples(TG[:, m % 2, TP:T]),
                                        segments(LR[:, m % 4, S0:])[:, :, PREV:], ALU.mult)\
                         .then_inc(y_val["y0"].sem, 1)
                        y_low(g, "y0", m, Blo, Bhi, m % 2)
                    if 3 <= c < 7:
                        final(g, 2 * (c - 3))
                        final(g, 2 * (c - 3) + 1)
                    if kind in "Oo":
                        o, V_P, dl, dh = ("pl0", V_P0, Alo, Ahi) if kind == "O" else ("pl1", V_P1, Blo, Bhi)
                        if c == O0:
                            dve.wait_ge(h_in.sem, h_in.at(g, 1))
                        product(g, c)
                        v.tensor_tensor(halves(H[:, m, :]), pair(PAIR[c]), halves(H[:, m, :]), ALU.add)\
                         .then_inc(proj_free.sem, 1)
                        if m:
                            low(g, o, m - 1, dl, dh, H[:, m - 1, :], V_P + m - 1)
                        if m == KT - 1:
                            low(g, o, m, dl, dh, H[:, m, :], V_P + m)
                            l = int(kind == "o")
                            dve.wait_ge(p_hi.sem, p_hi.at(g, l + 1))
                            v.tensor_tensor(Plo[:], PS_[:], Phi[:].bitcast(F32), ALU.subtract).then_inc(p_lo.sem, 1)
                    if kind in "Zz":
                        i = (KT if kind == "Z" else 3 * KT) + m
                        if m == 0:
                            inverse(g, N_PL0 if kind == "Z" else N_PL1, R[:])
                        half_gate(g, c, m % 2, R[:])
                        if kind == "Z" and m:
                            low(g, "in1", m - 1, Blo, Bhi, H[:, m - 1, :], V_G1 + m - 1)
                        if kind == "z" and m:
                            low((g, 1), "in0", m - 1, Alo, Ahi, XS[:, (m - 1) % 2, :], V_G0 + m - 1)
                        embed(g, c, i, m, "in1" if kind == "Z" else "fin")
                        if m == KT - 1 and kind == "Z":
                            low(g, "in1", m, Blo, Bhi, H[:, m, :], V_G1 + m)
                        if m == KT - 1 and kind == "z":
                            low((g, 1), "in0", m, Alo, Ahi, XS[:, m % 2, :], V_G0 + m)
                    if kind == "k":
                        if m == 0:
                            inverse(g, N_IN1, R[:])
                            dve.wait_ge(state_out.sem, state_out.at(g, 2))
                        p = PAIR[c]
                        product(g, c)
                        v.tensor_tensor(K[:, m, BLK:BLK + C], PSUM[:, 2 * p, 0:C], R[:, 0:C], ALU.mult)
                        v.tensor_tensor(K[:, m, BLK + C:], PSUM[:, 2 * p + 1, 0:TB], R[:, C:TP], ALU.mult)
                        v.tensor_tensor(KS[:, m, :, WIN:], samples(PSUM[:, 2 * p + 1, TB:C]), samples(R[:, TP:T]),
                                        ALU.mult).then_inc(proj_free.sem, 1)
                    if kind == "v":
                        product(g, c)
                        v.tensor_tensor(halves(VT[:, m, :]), pair(PAIR[c]), halves(R[:]), ALU.mult)\
                         .then_inc(proj_free.sem, 1)
                    if kind == "q":
                        product(g, c)
                        v.scalar_tensor_tensor(halves(Q[:, m, :]), pair(PAIR[c]), HD ** -0.5, halves(R[:]),
                                               ALU.mult, ALU.mult).then_inc(proj_free.sem, 1)
                        if m == KT - 1:
                            dve.wait_ge(proj_free.sem, proj_free.at(g, c + 1))
                            for s in range(SG):
                                ins = v.tensor_copy(
                                    QS[:, s, :, 0:2 * ST].rearrange("p k (j t) -> p k j t", t=ST),
                                    Q[:, :, TP + s * ST:TP + (s + 1) * ST].rearrange("p (k j) t -> p k j t", j=2))
                            ins.then_inc(q_ready.sem, 1)
                    if c == G1 - 1:
                        ss = SC[:, 1].rearrange("p a b -> p (a b)")[:, 0:4 * SW]
                        s4 = ss.rearrange("p (i w) -> p i w", w=SW)
                        dve.wait_ge(s_done.sem, s_done.at(g, 1))
                        v.tensor_tensor(ss.rearrange("p (a w) -> p a w", a=2), PSUM[:, 4:6, 0:SG * SW], TBS[:],
                                        ALU.add).then_inc(s_read.sem, 1)
                        dve.wait_ge(s_read.sem, s_read.at(g, 1))
                        row_max(g, 0, s4, V_SINKS)
                        half_gate(g, G1, 0, R[:])
                        divide(g, 0, s4, SW)
                        dve.wait_ge(o_done.sem, o_done.at(g, 1))
                        v.tensor_copy(OS[:].rearrange("p a b -> p (a b)"), PSUM[:, 6, 0:KT * TS]).then_inc(os_read.sem, 1)
                        scores(g, 0)
                        for u in range(NU):
                            kv, b = divmod(u, NB)
                            if u + 1 < NU:
                                scores(g, u + 1)
                            divide(g, u + 1, SC[:, u % 3], 2 * BLK)
                            if b == NB - 1:
                                dve.wait_ge(o_read.sem, o_read.at(g, u + 1))
                                for t in (2 * kv, 2 * kv + 1):
                                    gated(g, t)
                                    y_low(g, "y1", t, Alo, Ahi, t % 2)
                            if u % 2 and u // 2 + 1 < KT:
                                half_gate(g, G1 + u // 2 + 1, (u // 2 + 1) % 2, R[:])
                        for t in (K, KX):
                            v.tensor_copy(t[:, :, 0:BLK], t[:, :, TP:TP + BLK])
                        v.tensor_copy(V[:, 0, :], V[:, NB, :])
                        v.tensor_copy(DIST0[:], DIST[:]).then_inc(carry_done.sem, 1)
                assert chain[0] == DVE_CHAIN, chain[0]
            chain[0] = 0
            dve.wait_ge(root_done.sem, root_done.at(GROUPS, 1))
            link(GROUPS, v.reciprocal(R[:], R[:]))
            for k in range(KT):
                final(GROUPS, k)

        @block.tensor
        def _(pe):
            def project(g, c, hi_t, lo_t, ready, k0=0, k1=None):
                nk = 2 if is_small(c) else KT
                k1 = nk if k1 is None else k1
                if k0 == 0:
                    pe.wait_ge(w_lo.sem, w_lo.at(g, c + 1))
                    pe.wait_ge(proj_free.sem, proj_free.at(g, before_in_pair(c) + 1))
                s, p = c % RING, PAIR[c]
                for k in range(k0, k1):
                    if ready is not None:
                        pe.wait_ge(ready.sem, ready.at(g, k + 1))
                    for n, (w, x) in enumerate(((WH, hi_t), (WH, lo_t), (WL, hi_t))):
                        for a in range(2):
                            ins = nc.tensor.matmul(PSUM[:, 2 * p + a, 0:C], w[:, s, k, :], x[:, k, a * C:(a + 1) * C],
                                                   start=(k == 0 and n == 0), stop=(k == nk - 1 and n == 2))
                if k1 == nk:
                    ins.then_inc(proj_done.sem, 1)

            def mean_square(g, o, acc, roots):
                pe.wait_ge(added[o].sem, added[o].at(g, KT - 1))
                if roots:
                    pe.wait_ge(root_done.sem, root_done.at(g, roots))
                for a in range(2):
                    ins = nc.tensor.matmul(PSUM[:, 4 + a, 0:C], ONE[:], acc[:, a * C:(a + 1) * C], start=True, stop=True)
                ins.then_inc(ms_done.sem, 1)

            def final_sum(g):
                pe.wait_ge(added["fin"].sem, added["fin"].at(g, 0))
                pe.wait_ge(proj_free.sem, proj_free.at(g, 0))
                for a in range(2):
                    ins = nc.tensor.matmul(PSUM[:, 6 + a, 0:C], ONE[:], ACC[:, a * C:(a + 1) * C], start=True, stop=True)
                ins.then_inc(ms_done.sem, 1)

            def static_wait():
                pe.wait_ge(memset_done.sem, 8)

            def gate_products(g, n):
                pe.wait_ge(xc_done.sem, xc_done.at(g, n + 1))
                if n == 0:
                    pe.wait_ge(root_done.sem, root_done.at(g, N_FIN + 1))
                else:
                    pe.wait_ge(ri_read.sem, ri_read.at(g, n))
                hw = FLAT // 2
                for w in range(2):
                    for a in range(2):
                        ins = nc.tensor.matmul(PSUM[:, 4 + 2 * w + a, 0:hw], WRI[:, w * KT + n, :],
                                               XC[:, n % 2, a * hw:(a + 1) * hw], start=True, stop=True)
                ins.then_inc(ri_done.sem, 1)

            def turn_values(g, t):
                pe.wait_ge(proj_free.sem, proj_free.at(g, AT["v", t] + 1))
                if t == 0:
                    pe.wait_ge(root_done.sem, root_done.at(g, N_IN1 + 1))
                for b in range(NB):
                    nc.tensor.transpose(PSUM[:, 6 + t, b * 128:(b + 1) * 128], VT[:, t, b * BLK:(b + 1) * BLK], IDN[:])
                for s in range(SG):
                    ins = nc.tensor.matmul(PSUM[0:ST, 4 + t, s * 128:(s + 1) * 128],
                                           VT[:, t, TP + s * ST:TP + (s + 1) * ST], IDN[:], start=True, stop=True)
                ins.then_inc(v_turned.sem, 1)

            def key_half(kv, par):
                return kv % 2 == par

            def unit_scores(g, u):
                kv, b = divmod(u, NB)
                pe.wait_ge(s_read.sem, s_read.at(g, u + 1))
                for j in range(2):
                    for par in range(2):
                        h0 = 64 * par
                        keys = K if key_half(kv, par) else KX
                        ins = nc.tensor.matmul(PSUM[:, 4 + par, j * 2 * BLK:(j + 1) * 2 * BLK],
                                               Q[h0:h0 + 64, 2 * kv + j, b * BLK:(b + 1) * BLK],
                                               keys[h0:h0 + 64, kv // 2, b * BLK:(b + 2) * BLK], start=True, stop=True)
                ins.then_inc(s_done.sem, 1)

            def unit_turn(g, u):
                pe.wait_ge(p_ready.sem, p_ready.at(g, u + 2))
                if u:
                    pe.wait_ge(o_read.sem, o_read.at(g, u))
                else:
                    pe.wait_ge(os_read.sem, os_read.at(g, 1))
                for h in range(2):
                    for i in range(4):
                        ins = nc.tensor.transpose(PSUM[:, 6 + h, i * BLK:(i + 1) * BLK],
                                                  SC[:, u % 3, i, h * BLK:(h + 1) * BLK], IDN[:])
                ins.then_inc(t_done.sem, 1)

            def unit_values(g, u):
                kv, b = divmod(u, NB)
                pe.wait_ge(pt_ready.sem, pt_ready.at(g, u + 2))
                static_wait()
                for par in range(2):
                    for h in range(2):
                        ins = nc.tensor.matmul(PSUM[64 * par:64 * par + 64, 6, 0:2 * BLK],
                                               V[:, b + h, kv * HD:(kv + 1) * HD],
                                               PT[:, h, 2 * par * BLK:2 * (par + 1) * BLK], start=(h == 0), stop=(h == 1))
                ins.then_inc(o_done.sem, 1)

            def sample_scores(g):
                for kv in range(NKV):
                    for s in range(SG):
                        for par in range(2):
                            h0 = 64 * par
                            keys = KS if key_half(kv, par) else KSX
                            ins = nc.tensor.matmul(PSUM[32 * kv:32 * kv + 32, 4 + par, s * SW:(s + 1) * SW],
                                                   QS[h0:h0 + 64, s, kv, :], keys[h0:h0 + 64, kv // 2, s, :],
                                                   start=True, stop=True)
                ins.then_inc(s_done.sem, 1)

            def sample_turn(g):
                pe.wait_ge(p_ready.sem, p_ready.at(g, 1))
                ss = SC[:, 1].rearrange("p a b -> p (a b)")
                for i in range(4):
                    nc.tensor.transpose(PSUM[:, 6, i * 128:(i + 1) * 128], ss[:, i * SW:i * SW + WIN], IDN[:])
                for i in range(4):
                    ins = nc.tensor.matmul(PSUM[0:ST, 7, i * 128:(i + 1) * 128], ss[:, i * SW + WIN:(i + 1) * SW],
                                           IDN[:], start=True, stop=True)
                ins.then_inc(t_done.sem, 1)

            def sample_values(g):
                pe.wait_ge(pt_ready.sem, pt_ready.at(g, 1))
                static_wait()
                out = PSUM[:, 6, 0:KT * TS].rearrange("p (m s t) -> p m s t", m=KT, s=SG)
                for par in range(2):
                    for s in range(SG):
                        for kv in range(NKV):
                            i = SG * par + s
                            o = out[64 * par:64 * par + 64, 2 * kv:2 * kv + 2, s, :]
                            cols = slice(i * 128 + 32 * kv, i * 128 + 32 * kv + 2 * ST)
                            nc.tensor.matmul(o, VS[:, s, kv * HD:(kv + 1) * HD], PT[:, 0, cols], start=True, stop=False)
                            ins = nc.tensor.matmul(o, VN[0:ST, s, kv * HD:(kv + 1) * HD], PT[0:ST, 1, cols],
                                                   start=False, stop=True)
                ins.then_inc(o_done.sem, 1)

            pe.wait_ge(consts_in.sem, 6 * 16)
            pe.wait_ge(memset_done.sem, 8)
            nc.tensor.matmul(PSUM[:, 0, 0:128], ONE[:], ONE[:], start=True, stop=True).then_inc(proj_done.sem, 1)
            with pe.Fori(0, GROUPS) as g:
                for c in range(NBLK):
                    kind, m = ORDER[c]
                    if c == 1:
                        mean_square(g, "in0", ACCN, 0)
                        final_sum(g)
                    if c in RI_BEFORE:
                        gate_products(g, RI_BEFORE[c])
                    if c == G1 - 1:
                        pe.wait_ge(k_swapped.sem, k_swapped.at(g, 4))
                        pe.wait_ge(ks_in.sem, ks_in.at(g, 3))
                        pe.wait_ge(v_ready.sem, v_ready.at(g, 2))
                    if kind in "XG":
                        project(g, c, Ahi, Alo, lo["in0"] if c == 0 else None)
                    elif kind == "O":
                        project(g, c, Bhi, Blo, lo["y0"] if m == 0 else None)
                    elif kind == "o":
                        project(g, c, Ahi, Alo, lo["y1"] if m == 0 else None)
                    elif kind in "Pp":
                        if m == 0:
                            pe.wait_ge(p_lo.sem, p_lo.at(g, 1 + (kind == "p")))
                        project(g, c, Phi, Plo, None)
                    elif kind in "Zzkvq":
                        a, b, o = (Ahi, Alo, "pl0") if kind == "Z" else (Bhi, Blo, "pl1" if kind == "z" else "in1")
                        if c in (Z0, L1, Z1):
                            project(g, c, a, b, lo[o])
                            n = {Z0: N_PL0, L1: N_IN1, Z1: N_PL1}[c]
                            mean_square(g, o, ACC, n)
                        else:
                            project(g, c, a, b, None)
                    if c == Q1:
                        turn_values(g, 0)
                    if c == Q1 + 1:
                        turn_values(g, 1)
                    if c == G1 - 1:
                        project(g, G1, Bhi, Blo, None, 0, KT // 2)
                        pe.wait_ge(q_ready.sem, q_ready.at(g, 1))
                        project(g, G1, Bhi, Blo, None, KT // 2)
                        sample_scores(g)
                        project(g, G1 + 1, Bhi, Blo, None, 0, KT // 2)
                        sample_turn(g)
                        sample_values(g)
                        unit_scores(g, 0)
                        unit_scores(g, 1)
                        for u in range(NU):
                            if u + 2 < NU:
                                unit_scores(g, u + 2)
                            unit_turn(g, u)
                            j = G1 + 1 + (u + 1) // 2
                            if j < O1:
                                if u % 2 == 0:
                                    project(g, j, Bhi, Blo, None, KT // 2)
                                else:
                                    project(g, j, Bhi, Blo, None, 0, KT // 2)
                            unit_values(g, u)
            final_sum(GROUPS)


def kernel(**inputs):
    import numpy as np
    import concourse.bacc as bacc
    from concourse.bass_utils import run_bass_kernel_spmd

    i = {k: np.ascontiguousarray(v) for k, v in inputs.items()}

    def by_group(prompt, sample, extra=0):
        f = prompt.shape[-1]
        out = np.zeros((GROUPS + extra, T, f), np.float32)
        out[:GROUPS, :TP] = prompt.reshape(GROUPS, TP, f)
        out[:GROUPS, TP:] = sample.reshape(GROUPS, TS, f)
        return np.ascontiguousarray(out.reshape(-1, T, f // 128, 128).transpose(0, 3, 2, 1))

    def w_block(w, m):
        return w[:, m * 128:(m + 1) * 128].reshape(-1, 128, 128).transpose(1, 0, 2)

    win_a, win_b = i["w_in_a"][0], i["w_in_b"][0]
    take = {"X": (win_a, 0), "G": (win_a, KT), "O": (i["w_out_a"][0], 0), "Z": (i["w_ple_gate"][0], 0),
            "P": (i["w_ple_proj"][0], 0), "q": (win_b, 0), "k": (win_b, KT), "v": (win_b, KT + 2),
            "g": (win_b, KT + 4), "o": (i["w_out_b"][0], 0), "z": (i["w_ple_gate"][1], 0),
            "p": (i["w_ple_proj"][1], 0)}
    big = np.stack([w_block(take[k][0], take[k][1] + m) for k, m in ORDER if k not in "Pp"])
    small = np.stack([w_block(take[k][0], m) for k in "Pp" for m in range(KT)])

    def cols(v):
        return v.reshape(KT, 128).T

    heads = np.array([4 * kv + 2 * j + par for kv in range(NKV) for par in range(2) for j in range(2)])
    sinks = i["sinks"][0]
    row_head = np.zeros((128, 2), np.int64)
    bias_s = np.zeros((128, 2, SG, SW), np.float32)
    key = np.arange(SW)
    for kv in range(NKV):
        for j in range(2):
            for t in range(ST):
                r = 32 * kv + ST * j + t
                dist = WIN + t - key
                for par in range(2):
                    h = 4 * kv + 2 * j + par
                    row_head[r, par] = h
                    bias_s[r, par] = np.where((dist >= 0) & (dist < WIN), -slope(h) * dist, -1e30)
    vec = np.concatenate(
        [cols(i["norm_g"][0]), cols(i["norm_g"][1]), cols(i["ple_norm_g"][0]), cols(i["ple_norm_g"][1]),
         cols(i["final_norm_g"])] + [cols(i["conv_w_a"][0][k]) for k in range(TAPS)]
        + [cols(i[n][0]) for n in ("conv_b_a", "b_rgate", "b_igate", "lru_lambda")]
        + [np.broadcast_to(sinks[heads], (128, NH)), np.repeat(sinks[row_head], SG, axis=1)], axis=1)
    q, s = np.arange(BLK)[:, None], np.arange(2 * BLK)[None]
    d = BLK + q - s
    dist = np.where((d >= 0) & (d < WIN), d, MASKED).astype(np.float32)
    first = np.where(s < BLK, MASKED, dist).astype(np.float32)
    w_ri = np.concatenate([i["w_rgate"][0], i["w_igate"][0]]).transpose(1, 0, 2)
    ck, cv = (i[n][0].reshape(GROUPS, SG, WIN, NKV * HD) for n in ("cache_k", "cache_v"))
    k_cache = ck.reshape(GROUPS, SG, WIN, 2, 128).transpose(0, 4, 3, 1, 2)
    arrays = {
        "x": by_group(i["x_prompt"][0], i["x_sample"], 1),
        "p0": by_group(i["p_prompt"][0, 0], i["p_sample"][0]),
        "p1": by_group(i["p_prompt"][1, 0], i["p_sample"][1]),
        "w_big": big, "w_small": small, "w_ri": w_ri, "vec": vec,
        "dist": np.stack([dist, first]), "bias_s": bias_s.reshape(128, 2, SG * SW),
        "ident": np.eye(128, dtype=np.float32),
        "h_state": i["state_lru_h"][0].reshape(GROUPS, SG, KT, 128).transpose(0, 3, 2, 1),
        "conv_state": i["state_conv"][0].reshape(GROUPS, SG, PREV, KT, 128).transpose(0, 4, 3, 1, 2),
        "k_cache": k_cache, "k_cache_x": np.roll(k_cache, 64, axis=1),
        "v_cache": cv.transpose(0, 2, 1, 3),
    }
    arrays = {k: np.ascontiguousarray(v) for k, v in arrays.items()}
    outs = {
        "y_out": (GROUPS + 1, 128, KT, T), "h_out": (128, KT), "conv_out": (128, KT, PREV),
        "k_out": (128, 2, BLK), "v_out": (BLK, NKV * HD), "h_state_out": (GROUPS, 128, KT, SG),
        "conv_state_out": (GROUPS, 128, KT, SG, PREV), "ks_out": (GROUPS, 128, 2, SG, WIN),
        "vs_out": (GROUPS, WIN, SG, NKV * HD),
    }
    nc = bacc.Bacc("TRN2", target_bir_lowering=False, num_devices=1)
    aps = {k: nc.dram_tensor(k, v.shape, F32, kind="ExternalInput").ap() for k, v in arrays.items()}
    aps.update({k: nc.dram_tensor(k, v, F32, kind="ExternalOutput").ap() for k, v in outs.items()})
    build(nc, aps)
    r = run_bass_kernel_spmd(nc, [arrays], core_ids=[0]).results[0]
    y = r["y_out"][1:].transpose(0, 3, 2, 1).reshape(GROUPS, T, D)
    return (
        y[:, :TP].reshape(1, SEQ, D),
        y[:, TP:].reshape(NSEQ, ST, D),
        r["h_out"].T.reshape(1, 1, D),
        r["conv_out"].transpose(2, 1, 0).reshape(1, 1, PREV, D),
        r["k_out"].transpose(2, 1, 0).reshape(1, 1, WIN, NKV, HD),
        r["v_out"].reshape(1, 1, WIN, NKV, HD),
        r["h_state_out"].transpose(0, 3, 2, 1).reshape(1, NSEQ, D),
        r["conv_state_out"].transpose(0, 3, 4, 2, 1).reshape(1, NSEQ, PREV, D),
        r["ks_out"].transpose(0, 3, 4, 2, 1).reshape(1, NSEQ, WIN, NKV, HD),
        r["vs_out"].transpose(0, 2, 1, 3).reshape(1, NSEQ, WIN, NKV, HD),
    )
```

```python
from contextlib import ExitStack

import concourse.bass as bass
from concourse import mybir

F32 = mybir.dt.float32
F32R = mybir.dt.float32r
ALU = mybir.AluOpType
ACT = mybir.ActivationFunctionType
AX_X = mybir.AxisListType.X

D = 1024
KT = D // 128
SEQ = 2048
GROUPS = 4
TP = SEQ // GROUPS
NSEQ, ST = 8, 4
SG = NSEQ // GROUPS
TS = SG * ST
T = TP + TS
C = T // 2
TB = C - TS
TAPS = 4
PREV = TAPS - 1
SEG = PREV + ST
PAD = 2
FLAT = TP + PAD + SG * SEG
XBW = FLAT + PREV
S0 = TP + PAD
NH, HD, NKV = 16, 64, 4
WIN = 128
BLK = 128
NB = TP // BLK
NU = NB * NKV
SW = WIN + ST
EPS = 1e-6
MASKED = 1e33

ORDER = [("X", 0), ("X", 1), ("X", 2)]
for _n in range(5):
    ORDER += [("G", _n), ("X", _n + 3)]
ORDER += [("G", 5), ("G", 6), ("G", 7)]
O0 = len(ORDER)
ORDER += [("O", m) for m in range(KT)]
Z0 = len(ORDER)
for _m in range(KT):
    ORDER += [("Z", _m), ("P", _m)]
L1 = len(ORDER)
ORDER += [("k", 0), ("k", 1), ("v", 0), ("v", 1)]
Q1 = len(ORDER)
ORDER += [("q", m) for m in range(KT)]
G1 = len(ORDER)
ORDER += [("g", m) for m in range(KT)]
O1 = len(ORDER)
ORDER += [("o", m) for m in range(KT)]
Z1 = len(ORDER)
for _m in range(KT):
    ORDER += [("z", _m), ("p", _m)]
NBLK = len(ORDER)
AT = {b: c for c, b in enumerate(ORDER)}
RING, STAGE = 4, 2
AHEAD = RING - 1
assert NBLK % RING == 0 and NBLK % STAGE == 0

FILL = (KT - 2) * KT // NU
WHOLE = {max(0, -(-KT * (j - 1) // FILL) - 1): j for j in range(1, KT)}

RI_BEFORE = {2: 0, 3: 1}
RI_BEFORE.update({2 * n: n for n in range(2, KT)})

PAIR = []
_turn = 0
for _b in ORDER:
    if _b[0] in "Pp" or _b == ("v", 0):
        PAIR.append(3)
    else:
        PAIR.append(_turn)
        _turn ^= 1


def before_in_pair(c):
    return next(p for p in range(c - 1, c - NBLK - 1, -1) if PAIR[p % NBLK] == PAIR[c])


FREE_HEAD = 4


def is_small(c):
    return ORDER[c % NBLK][0] in "Pp"


def slope(head):
    return 2.0 ** (-8.0 * (head + 1) / NH)


V_G0, V_G1, V_P0, V_P1, V_FIN = 0, 8, 16, 24, 32
V_CW, V_CB, V_BR, V_BI, V_LAM, V_SINK, V_SINKS = 40, 72, 80, 88, 96, 104, 120
NVEC = 124

N_IN0, N_FIN, N_PL0, N_IN1, N_PL1 = range(5)
NORMS = 5

DVE_CHAIN, ACT_CHAIN = 130, 8


class Stage:

    def __init__(self, nc, ctx, name, per, head=0, step=1):
        self.sem = ctx.enter_context(nc.semaphore(name))
        self.per, self.head, self.step = per, head, step

    def at(self, g, n):
        if isinstance(g, tuple):
            g, n = g[0], n + g[1] * self.per
        assert (isinstance(g, int) and g) or self.head + n > 0
        return g * (self.per * self.step) + (self.head + n) * self.step


def build(nc, A):
    ctx = ExitStack()
    with ctx:
        base = 16512
        place = [base]

        def sb_at(name, shape, dt, offset):
            return nc.alloc_sbuf_tensor_at(name, [128] + list(shape), dt, offset=offset)

        def sb(name, shape, dt=F32):
            n = 4
            for s in shape:
                n *= s
            off = place[0]
            place[0] += (n + 31) // 32 * 32
            return sb_at(name, shape, dt, off)

        H = sb("resid", [KT, T])
        a_at = place[0]
        Ahi = sb("a_hi", [KT, T], F32R)
        Alo = sb("a_lo", [KT, T], F32R)
        Bhi = sb("b_hi", [KT, T], F32R)
        Blo = sb("b_lo", [KT, T], F32R)
        Q = sb_at("q", [KT, T], F32, a_at)
        LR = sb("lru_or_o", [4, FLAT])
        p_at = place[0]
        Phi = sb("p_hi", [2, T], F32R)
        Plo = sb("p_lo", [2, T], F32R)
        KS = sb_at("ks", [2, SG, SW], F32, p_at)
        KSX = sb_at("ks_swapped", [2, SG, SW], F32, p_at + 4 * 2 * SG * SW)
        VS = sb_at("vs", [SG, NKV * HD], F32, p_at + 8 * 2 * SG * SW)
        VN = sb_at("vs_new", [SG, NKV * HD], F32, p_at + 8 * 2 * SG * SW + 4 * SG * NKV * HD)
        assert 8 * 2 * SG * SW + 8 * SG * NKV * HD <= 16 * T
        WH = sb("w_hi", [RING, KT, 128], F32R)
        WL = sb("w_lo", [RING, KT, 128], F32R)
        WS = sb("w_stage", [STAGE, KT, 128])
        WRI = sb("w_ri", [2 * KT, 128])
        K = sb("k", [2, BLK + TP])
        KX = sb("k_swapped", [2, BLK + TP])
        V = sb("v", [1 + NB, NKV * HD])
        t_at = place[0]
        XB = sb("conv_in", [2, XBW])
        XC = sb("conv_out", [2, FLAT])
        TR = sb("gate_r", [FLAT])
        AA = sb("decay", [FLAT])
        TH = sb("decay_th", [FLAT])
        TI = sb("gate_i", [FLAT])
        SC = sb_at("scores", [3, 4, 2 * BLK], F32, t_at)
        PT = sb_at("probs_t", [2, 4 * BLK], F32, t_at + 12288)
        VT = sb_at("v_t", [2, T], F32, t_at)
        PS_ = sb_at("p_stage", [2, T], F32, t_at)
        XS = sb_at("x_stage", [2, T], F32, t_at + 8 * T)
        assert 16384 <= place[0] - t_at and 16 * T <= place[0] - t_at
        GH = sb("gate_half", [2, T])
        TG = sb("gate_tanh", [3, T])
        R = sb("inv_rms", [T])
        RN = sb("inv_rms_in0", [T])
        SQ = sb("square", [2, T])
        ACC = sb("square_sum", [T])
        ACCN = sb("square_sum_in0", [T])
        DIST = sb("dist", [2 * BLK])
        DIST0 = sb("dist_first", [2 * BLK])
        TBS = sb("bias_s", [2, SG * SW])
        IDN = sb("identity", [128])
        ONE = sb("ones", [128])
        VEC = sb("vec", [NVEC])
        C1 = sb("lru_c", [2, KT])
        EPT = sb("eps", [1])
        QS = sb("qs", [SG, NKV, 32])
        OS = sb("os", [KT, TS])
        HC = sb("h_carry", [KT])
        HST = sb("h_state", [KT, SG])
        HSO = sb("h_state_out", [KT, SG])
        CC = sb("conv_carry", [KT, PREV])
        CST = sb("conv_state", [KT, SG, PREV])
        CSO = sb("conv_state_out", [KT, SG, PREV])
        MX = sb("row_max", [4, 4])
        NM = sb("row_max_neg", [4, 4])
        ES = sb("sink_exp", [4, 4])
        DEN = sb("row_sum", [4, 4])
        SP = sb("softplus_tmp", [6, KT])
        assert place[0] <= nc.sbuf_usable_end, place[0]

        PSUM = ctx.enter_context(nc.psum_tensor("psum", [128, 8, 512], F32))

        def pair(p):
            return PSUM[:, 2 * p:2 * p + 2, 0:C]

        def halves(ap):
            return ap.rearrange("p (a c) -> p a c", a=2)

        def samples(ap):
            return ap.rearrange("p (s t) -> p s t", t=ST)

        def segments(ap):
            return ap.rearrange("p (s w) -> p s w", w=SEG)

        def stage(name, per, head=0, step=1):
            return Stage(nc, ctx, name, per, head, step)

        consts_in = stage("consts_in", 0, step=16)
        memset_done = stage("memset_done", 0)
        dve_setup = stage("dve_setup", 0)
        act_setup = stage("act_setup", 0)
        w_in = [stage(f"w_in{i}", NBLK // STAGE, step=16) for i in range(STAGE)]
        w_hi = stage("w_hi_done", NBLK)
        w_lo = stage("w_lo_done", NBLK)
        proj_done = stage("proj_done", NBLK, head=1)
        proj_free = stage("proj_free", NBLK, head=FREE_HEAD)
        x_in = [stage(f"x_in{i}", KT // 2, step=16) for i in range(2)]
        h_in = stage("h_in", 1, head=1, step=16)
        state_in = stage("state_in", 2, step=16)
        state_out = stage("state_out", 2, step=16)
        p_in = stage("p_in", 2, step=16)
        ks_in = stage("ks_in", 3, step=16)
        kv_out = stage("kv_out", 3, step=16)
        k_swapped = stage("k_swapped_in", 4, step=16)
        y_out = stage("y_out", 1, step=16)
        end_out = stage("end_out", 0, step=16)
        ops = ("in0", "y0", "pl0", "in1", "y1", "pl1")
        hi = {o: stage(o + "_hi", KT) for o in ops}
        lo = {o: stage(o + "_lo", KT) for o in ops}
        p_hi, p_lo = stage("p_hi_done", 2), stage("p_lo_done", 2)
        norms = ("in0", "fin", "pl0", "in1", "pl1")
        squared = {o: stage("sq_" + o, KT) for o in norms}
        added = {o: stage("add_" + o, KT - 1, head=int(o == "fin")) for o in norms}
        ms_done = stage("ms_done", NORMS)
        root_done = stage("root_done", NORMS)
        h_new = {o: stage("h_" + o, KT) for o in ("in1", "fin")}
        y_fin = stage("y_fin", KT)
        xc_done = stage("xc_done", KT)
        ri_done = stage("ri_done", KT)
        ri_read = stage("ri_read", KT)
        decay_done = stage("decay_done", KT)
        q2_done = stage("q2_done", KT)
        q2_root = stage("q2_root", KT)
        lru_done = stage("lru_done", KT)
        tanh_done = stage("tanh_done", 4 * KT)
        y_val = {o: stage(o + "_val", KT) for o in ("y0", "y1")}
        v_turned = stage("v_turned", 2)
        v_ready = stage("v_ready", 2)
        q_ready = stage("q_ready", 1)
        s_done = stage("s_done", NU + 1)
        s_read = stage("s_read", NU + 1)
        nm_ready = stage("nm_ready", NU + 1)
        exp_done = stage("exp_done", NU + 1)
        p_ready = stage("p_ready", NU + 1)
        t_done = stage("t_done", NU + 1)
        pt_ready = stage("pt_ready", NU + 1)
        o_done = stage("o_done", NU + 1)
        o_read = stage("o_read", NU)
        silu_done = stage("silu_done", 2 * KT)
        os_read = stage("os_read", 1)
        carry_done = stage("carry_done", 1)
        dve_chain = stage("dve_chain", DVE_CHAIN)
        act_chain = stage("act_chain", ACT_CHAIN)

        block = ctx.enter_context(nc.Block())

        @block.sync
        def _(sp):
            def load_weights(g, j):
                if not (isinstance(g, int) and j < STAGE):
                    sp.wait_ge(w_lo.sem, w_lo.at(g, j - STAGE + 1))
                c, s = j % NBLK, j % STAGE
                if is_small(c):
                    n = KT * (ORDER[c][0] == "p") + ORDER[c][1]
                    sp.dma_start(WS[:, s, 0:2, :], A["w_small"][n]).then_inc(w_in[s].sem, 16)
                else:
                    n = sum(not is_small(x) for x in range(c))
                    sp.dma_start(WS[:, s, :, :], A["w_big"][n]).then_inc(w_in[s].sem, 16)

            def group_of(ap, g):
                if isinstance(g, int):
                    return ap[g]
                v = ap[bass.ds(g, 1)]
                if len(ap.shape) == 3:
                    return v.rearrange("a p x -> (a p) x")
                if len(ap.shape) == 4:
                    return v.rearrange("a p x y -> (a p) x y")
                return v.rearrange("a p x y z -> (a p) x y z")

            def load_x(g, k, group):
                if k >= 2 or not isinstance(g, int):
                    sp.wait_ge(lo["in0"].sem, lo["in0"].at(g, k - 1))
                sp.dma_start(XS[:, k % 2, :], group_of(A["x"], group)[:, k, :]).then_inc(x_in[k % 2].sem, 16)

            load_x(0, 0, 0)
            load_x(0, 1, 0)
            for dst, src in ((VEC[:], A["vec"]), (DIST[:], A["dist"][0]), (DIST0[:], A["dist"][1]),
                             (TBS[:], A["bias_s"]), (IDN[:], A["ident"]), (WRI[:], A["w_ri"])):
                sp.dma_start(dst, src).then_inc(consts_in.sem, 16)
            for j in range(STAGE):
                load_weights(0, j)
            sp.dma_start(H[:], A["x"][0]).then_inc(h_in.sem, 16)
            for k in range(2, KT):
                load_x(0, k, 0)
            for j in range(STAGE, AHEAD):
                load_weights(0, j)

            with sp.Fori(0, GROUPS) as g:
                for c in range(NBLK):
                    load_weights(g, c + AHEAD)
                    if c == 0:
                        sp.dma_start(CST[:], group_of(A["conv_state"], g)).then_inc(state_in.sem, 16)
                        sp.dma_start(HST[:], group_of(A["h_state"], g)).then_inc(state_in.sem, 16)
                    if c == 11:
                        sp.wait_ge(y_fin.sem, y_fin.at(g, KT))
                        sp.dma_start(group_of(A["y_out"], g), H[:]).then_inc(y_out.sem, 16)
                    if c == 14:
                        sp.wait_ge(y_out.sem, y_out.at(g, 1))
                        sp.dma_start(H[:], group_of(A["x"], g)).then_inc(h_in.sem, 16)
                    if c == O0 + 4:
                        sp.wait_ge(proj_done.sem, proj_done.at(g, O0 + 1))
                        sp.dma_start(PS_[:], group_of(A["p0"], g)).then_inc(p_in.sem, 16)
                        sp.dma_start(group_of(A["h_state_out"], g), HSO[:]).then_inc(state_out.sem, 16)
                        sp.dma_start(group_of(A["conv_state_out"], g), CSO[:]).then_inc(state_out.sem, 16)
                    if c == L1 + 3:
                        sp.wait_ge(proj_done.sem, proj_done.at(g, L1))
                        sp.dma_start(KS[:, :, :, 0:WIN], group_of(A["k_cache"], g)).then_inc(ks_in.sem, 16)
                        sp.dma_start(KSX[:, :, :, 0:WIN], group_of(A["k_cache_x"], g)).then_inc(ks_in.sem, 16)
                        sp.dma_start(VS[:], group_of(A["v_cache"], g)).then_inc(ks_in.sem, 16)
                    if c == Q1 + 1:
                        sp.wait_ge(proj_free.sem, proj_free.at(g, AT["k", 1] + 1))
                        for a in (0, 64):
                            b = 64 - a
                            sp.dma_start(KX[a:a + 64, :, BLK:], K[b:b + 64, :, BLK:]).then_inc(k_swapped.sem, 16)
                            sp.dma_start(KSX[a:a + 64, :, :, WIN:], KS[b:b + 64, :, :, WIN:]).then_inc(k_swapped.sem, 16)
                    if c == Q1 + 6:
                        sp.wait_ge(ks_in.sem, ks_in.at(g, 3))
                        sp.wait_ge(v_ready.sem, v_ready.at(g, 2))
                        sp.dma_start(group_of(A["ks_out"], g),
                                     KS[:, :, :, ST:]).then_inc(kv_out.sem, 16)
                        vo = group_of(A["vs_out"], g)
                        sp.dma_start(vo[0:WIN - ST], VS[ST:]).then_inc(kv_out.sem, 16)
                        sp.dma_start(vo[WIN - ST:], VN[0:ST]).then_inc(kv_out.sem, 16)
                    if c == O1 + 4:
                        sp.wait_ge(proj_done.sem, proj_done.at(g, O1 + 1))
                        sp.dma_start(PS_[:], group_of(A["p1"], g)).then_inc(p_in.sem, 16)
                    if c == O1 + 5:
                        load_x((g, 1), 0, g + 1)
                        load_x((g, 1), 1, g + 1)
                    if c > Z1 and (c - Z1) % 2 and (c - Z1) // 2 + 2 < KT:
                        load_x((g, 1), (c - Z1) // 2 + 2, g + 1)

            sp.wait_ge(y_fin.sem, y_fin.at(GROUPS, KT))
            sp.dma_start(A["y_out"][GROUPS], H[:]).then_inc(end_out.sem, 16)
            sp.wait_ge(carry_done.sem, carry_done.at(GROUPS, 0))
            sp.dma_start(A["h_out"], HC[:]).then_inc(end_out.sem, 16)
            sp.dma_start(A["conv_out"], CC[:]).then_inc(end_out.sem, 16)
            sp.dma_start(A["k_out"], K[:, :, 0:BLK]).then_inc(end_out.sem, 16)
            sp.dma_start(A["v_out"], V[:, 0, :]).then_inc(end_out.sem, 16)
            sp.wait_ge(end_out.sem, 5 * 16)
            sp.wait_ge(y_out.sem, y_out.at(GROUPS, 0))
            sp.wait_ge(state_out.sem, state_out.at(GROUPS, 0))
            sp.wait_ge(kv_out.sem, kv_out.at(GROUPS, 0))
            for j in range(AHEAD):
                sp.wait_ge(w_in[j % STAGE].sem, w_in[j % STAGE].at(GROUPS, j // STAGE + 1))

        @block.gpsimd
        def _(pool):
            def split_low(g, j):
                n = 2 if is_small(j) else KT
                pool.wait_ge(w_hi.sem, w_hi.at(g, j + 1))
                nc.gpsimd.tensor_tensor(WL[:, j % RING, 0:n, :], WS[:, j % STAGE, 0:n, :],
                                        WH[:, j % RING, 0:n, :].bitcast(F32), ALU.subtract).then_inc(w_lo.sem, 1)

            def add_square(g, o, k):
                acc = ACCN if o == "in0" else ACC
                slot = {"fin": 0, "in0": 1}.get(o, k % 2)
                pool.wait_ge(squared[o].sem, squared[o].at(g, k + 1))
                if k >= 2:
                    pool.wait_ge(added[o].sem, added[o].at(g, k - 1))
                nc.gpsimd.tensor_tensor(acc[:], acc[:], SQ[:, slot, :], ALU.add).then_inc(added[o].sem, 1)

            def y_value(g, o, i, t):
                pool.wait_ge(silu_done.sem, silu_done.at(g, i + 1))
                tg = TG[:, t % 3]
                if o == "y0":
                    nc.gpsimd.tensor_tensor(tg[:, 0:TP], tg[:, 0:TP], LR[:, t % 4, 0:TP], ALU.mult)
                    ins = nc.gpsimd.tensor_tensor(samples(tg[:, TP:T]), samples(tg[:, TP:T]),
                                                  segments(LR[:, t % 4, S0:])[:, :, PREV:], ALU.mult)
                else:
                    pool.wait_ge(o_read.sem, o_read.at(g, 4 * (t // 2) + NB))
                    nc.gpsimd.tensor_tensor(tg[:, 0:TP], tg[:, 0:TP], LR[:, t % 4, 0:TP], ALU.mult)
                    ins = nc.gpsimd.tensor_tensor(tg[:, TP:T], tg[:, TP:T], OS[:, t, :], ALU.mult)
                ins.then_inc(y_val[o].sem, 1)

            def y_low(g, o, t, dst_lo, dst_hi):
                pool.wait_ge(hi[o].sem, hi[o].at(g, t + 1))
                nc.gpsimd.tensor_tensor(dst_lo[:, t, :], TG[:, t % 3, :], dst_hi[:, t, :].bitcast(F32),
                                        ALU.subtract).then_inc(lo[o].sem, 1)

            nc.gpsimd.memset(ONE[:], 1.0).then_inc(memset_done.sem, 1)
            for t in (HC, CC, K, KX, V, QS):
                nc.gpsimd.memset(t[:], 0.0).then_inc(memset_done.sem, 1)
            nc.gpsimd.memset(ACC[:], 0.0).then_inc(added["fin"].sem, 1)
            nc.gpsimd.memset(EPT[:], EPS).then_inc(memset_done.sem, 1)
            for j in range(STAGE):
                split_low(0, j)
            for k in range(1, KT):
                add_square(0, "in0", k)
            for j in range(STAGE, AHEAD):
                split_low(0, j)

            with pool.Fori(0, GROUPS) as g:
                for c in range(NBLK):
                    kind, m = ORDER[c - 1] if c else ("", 0)
                    if kind == "G":
                        y_value(g, "y0", m, m)
                        split_low(g, c + AHEAD)
                        y_low(g, "y0", m, Blo, Bhi)
                        continue
                    if kind == "g":
                        split_low(g, c + AHEAD)
                        if m in (1, 3, 4, 6):
                            kv = (1, 3, 4, 6).index(m)
                            for t in (2 * kv, 2 * kv + 1):
                                y_value(g, "y1", KT + t, t)
                            for t in (2 * kv, 2 * kv + 1):
                                y_low(g, "y1", t, Alo, Ahi)
                        continue
                    sum_first = m and kind in "Oo" or kind in "Pp"
                    if not kind or not sum_first:
                        split_low(g, c + AHEAD)
                    if m and kind in "Oo":
                        add_square(g, "pl0" if kind == "O" else "pl1", m)
                    if kind == "P" and m > 1:
                        add_square(g, "in1", m - 1)
                    if kind == "P" and m == KT - 1:
                        add_square(g, "in1", m)
                    if kind == "p":
                        if m > 1:
                            add_square(g, "fin", m - 1)
                        if m < KT - 1:
                            add_square((g, 1), "in0", m + 1)
                    if kind and sum_first:
                        split_low(g, c + AHEAD)
                add_square(g, "fin", KT - 2)
                add_square(g, "fin", KT - 1)

        @block.scalar
        def _(act):
            chain = [0]

            def link(g, ins):
                chain[0] += 1
                ins.then_inc(act_chain.sem, 1)
                act.wait_ge(act_chain.sem, act_chain.at(g, chain[0]))

            def split_high(g, j):
                act.wait_ge(w_in[j % STAGE].sem, w_in[j % STAGE].at(g, j // STAGE + 1))
                if not (isinstance(g, int) and j < RING):
                    act.wait_ge(proj_done.sem, proj_done.at(g, j - RING + 1))
                n = 2 if is_small(j) else KT
                nc.scalar.activation(WH[:, j % RING, 0:n, :], WS[:, j % STAGE, 0:n, :], ACT.Copy).then_inc(w_hi.sem, 1)

            def square(g, o, k, src):
                acc = ACCN if o == "in0" else ACC
                slot = {"fin": 0, "in0": 1}.get(o, k % 2)
                back = 1 if o in ("fin", "in0") else 2
                if k > back:
                    act.wait_ge(added[o].sem, added[o].at(g, k - back))
                nc.scalar.activation(acc[:] if k == 0 else SQ[:, slot, :], src, ACT.Square).then_inc(squared[o].sem, 1)

            def scaled_high(g, o, k, dst, src, col):
                nc.scalar.activation(dst, src, ACT.Copy, scale=VEC[:, col:col + 1]).then_inc(hi[o].sem, 1)

            def x_tile(g, k):
                act.wait_ge(x_in[k % 2].sem, x_in[k % 2].at(g, k // 2 + 1))
                square(g, "in0", k, XS[:, k % 2, :])
                scaled_high(g, "in0", k, Ahi[:, k, :], XS[:, k % 2, :], V_G0 + k)

            def root(g, n, banks, dst):
                act.wait_ge(ms_done.sem, ms_done.at(g, n + 1))
                nc.scalar.activation(halves(dst), PSUM[:, banks:banks + 2, 0:C], ACT.Sqrt, scale=1.0 / D,
                                     bias=EPT[:, 0:1]).then_inc(root_done.sem, 1)

            def gate_tanh(g, c, o=None):
                t = ORDER[c][1]
                act.wait_ge(proj_free.sem, proj_free.at(g, c + 1))
                if o and t >= 3:
                    act.wait_ge(lo[o].sem, lo[o].at(g, t - 2))
                nc.scalar.activation(TG[:, t % 3 if o else t % 2, :], GH[:, t % 2, :], ACT.Tanh).then_inc(tanh_done.sem, 1)

            def gates(g, n):
                act.wait_ge(ri_done.sem, ri_done.at(g, n + 1))
                if n:
                    act.wait_ge(lru_done.sem, lru_done.at(g, n))
                hw = FLAT // 2
                two = lambda ap: ap.rearrange("p (a c) -> p a c", a=2)
                nc.scalar.activation(two(TI[:]), PSUM[:, 6:8, 0:hw], ACT.Tanh, scale=0.5,
                                     bias=VEC[:, V_BI + n:V_BI + n + 1])
                nc.scalar.activation(two(TR[:]), PSUM[:, 4:6, 0:hw], ACT.Tanh, scale=0.5,
                                     bias=VEC[:, V_BR + n:V_BR + n + 1]).then_inc(ri_read.sem, 1)
                act.wait_ge(ri_read.sem, ri_read.at(g, n + 1))
                nc.scalar.activation(TH[:], TR[:], ACT.Tanh, scale=C1[:, 1, n:n + 1], bias=C1[:, 1, n:n + 1])
                link(g, nc.scalar.activation(AA[:], TR[:], ACT.Exp, scale=C1[:, 0, n:n + 1], bias=C1[:, 0, n:n + 1]))
                nc.scalar.activation(TR[:], AA[:], ACT.Square).then_inc(decay_done.sem, 1)

            def decay_root(g, n):
                act.wait_ge(q2_done.sem, q2_done.at(g, n + 1))
                nc.scalar.activation(TR[:], TR[:], ACT.Sqrt, scale=0.25).then_inc(q2_root.sem, 1)

            def y_high(g, o, t, dst):
                act.wait_ge(y_val[o].sem, y_val[o].at(g, t + 1))
                nc.scalar.activation(dst[:, t, :], TG[:, t % 3, :], ACT.Copy).then_inc(hi[o].sem, 1)

            def exps(g, ev, sc, width):
                s = ev if ev == 0 else 1 + (ev - 1) % 3
                act.wait_ge(nm_ready.sem, nm_ready.at(g, ev + 1))
                for i in range(4):
                    nc.scalar.activation(sc[:, i, 0:width], sc[:, i, 0:width], ACT.Exp, bias=NM[:, s, i:i + 1],
                                         accum_out=DEN[:, s, i:i + 1])
                nc.scalar.activation(ES[:, s, :], ES[:, s, :], ACT.Exp).then_inc(exp_done.sem, 1)

            act.wait_ge(consts_in.sem, 6 * 16)
            act.wait_ge(dve_setup.sem, 2)
            nc.scalar.activation(SP[:, 1, :], SP[:, 0, :], ACT.Exp, scale=-1.0).then_inc(act_setup.sem, 1)
            act.wait_ge(dve_setup.sem, 3)
            act.wait_ge(memset_done.sem, 8)
            for j in range(STAGE):
                split_high(0, j)
            for k in range(KT):
                x_tile(0, k)
            for j in range(STAGE, AHEAD):
                split_high(0, j)

            with act.Fori(0, GROUPS) as g:
                chain[0] = 0
                for c in range(NBLK):
                    kind, m = ORDER[c]
                    if kind == "g":
                        continue
                    split_high(g, c + AHEAD)
                    if c == 0:
                        root(g, N_IN0, 4, RN[:])
                    if c == 1:
                        root(g, N_FIN, 6, R[:])
                    if c in RI_BEFORE:
                        gates(g, RI_BEFORE[c])
                        decay_root(g, RI_BEFORE[c])
                    if c and ORDER[c - 1][0] == "G":
                        y_high(g, "y0", ORDER[c - 1][1], Bhi)
                    if kind == "G":
                        gate_tanh(g, c, "y0")
                    if kind in "Oo":
                        o, V_P, dst = ("pl0", V_P0, Ahi) if kind == "O" else ("pl1", V_P1, Bhi)
                        act.wait_ge(proj_free.sem, proj_free.at(g, c + 1))
                        square(g, o, m, H[:, m, :])
                        scaled_high(g, o, m, dst[:, m, :], H[:, m, :], V_P + m)
                        if m == 6:
                            l = int(kind == "o")
                            act.wait_ge(p_in.sem, p_in.at(g, l + 1))
                            if l:
                                act.wait_ge(kv_out.sem, kv_out.at(g, 3))
                            nc.scalar.activation(Phi[:], PS_[:], ACT.Copy).then_inc(p_hi.sem, 1)
                    if c in (Z0, L1, Z1):
                        root(g, {Z0: N_PL0, L1: N_IN1, Z1: N_PL1}[c], 4, R[:])
                    if kind in "Zz":
                        if kind == "z":
                            if m == 0:
                                x_tile((g, 1), 0)
                            if m < KT - 1:
                                x_tile((g, 1), m + 1)
                        gate_tanh(g, c)
                    if kind == "P":
                        act.wait_ge(h_new["in1"].sem, h_new["in1"].at(g, m + 1))
                        square(g, "in1", m, H[:, m, :])
                        scaled_high(g, "in1", m, Bhi[:, m, :], H[:, m, :], V_G1 + m)
                    if kind == "p":
                        act.wait_ge(h_new["fin"].sem, h_new["fin"].at(g, m + 1))
                        square(g, "fin", m, H[:, m, :])
                    if c in (Q1 + 1, Q1 + 2):
                        t = c - Q1 - 1
                        act.wait_ge(v_turned.sem, v_turned.at(g, t + 1))
                        nc.scalar.activation(V[:, 1:, t * 128:(t + 1) * 128],
                                             PSUM[:, 6 + t, :].rearrange("p (b f) -> p b f", f=128), ACT.Copy)
                        nc.scalar.activation(VN[0:ST, :, t * 128:(t + 1) * 128],
                                             PSUM[0:ST, 4 + t, 0:SG * 128].rearrange("p (s f) -> p s f", f=128),
                                             ACT.Copy).then_inc(v_ready.sem, 1)
                    if c == G1 - 1:
                        split_high(g, G1 + AHEAD)
                        exps(g, 0, SC[:, 2].rearrange("p a b -> p (a b)")[:, 0:4 * SW].rearrange(
                            "p (i w) -> p i w", w=SW), SW)
                        gate_tanh(g, G1, "y1")
                        exps(g, 1, SC[:, 0], 2 * BLK)
                        act.wait_ge(t_done.sem, t_done.at(g, 1))
                        nc.scalar.activation(PT[:, 0, :], PSUM[:, 6, :], ACT.Copy)
                        nc.scalar.activation(PT[0:ST, 1, :], PSUM[0:ST, 7, :], ACT.Copy).then_inc(pt_ready.sem, 1)
                        for u in range(NU):
                            kv, b = divmod(u, NB)
                            if u + 1 < NU:
                                exps(g, u + 2, SC[:, (u + 1) % 3], 2 * BLK)
                            act.wait_ge(t_done.sem, t_done.at(g, u + 2))
                            nc.scalar.activation(PT[:], PSUM[:, 6:8, :], ACT.Copy).then_inc(pt_ready.sem, 1)
                            if u in WHOLE:
                                split_high(g, G1 + WHOLE[u] + AHEAD)
                            act.wait_ge(o_done.sem, o_done.at(g, u + 2))
                            s = 2 * (kv % 2)
                            nc.scalar.activation(LR[:, s:s + 2, b * BLK:(b + 1) * BLK],
                                                 PSUM[:, 6, 0:2 * BLK].rearrange("p (j q) -> p j q", j=2),
                                                 ACT.Copy).then_inc(o_read.sem, 1)
                            if b == 0 and u:
                                for t in (2 * kv - 2, 2 * kv - 1):
                                    y_high(g, "y1", t, Ahi)
                            if u in WHOLE:
                                gate_tanh(g, G1 + WHOLE[u], "y1")
                        y_high(g, "y1", KT - 2, Ahi)
                        y_high(g, "y1", KT - 1, Ahi)
                assert chain[0] == ACT_CHAIN, chain[0]
            act.wait_ge(ms_done.sem, ms_done.at(GROUPS, 1))
            nc.scalar.activation(halves(R[:]), PSUM[:, 6:8, 0:C], ACT.Sqrt, scale=1.0 / D,
                                 bias=EPT[:, 0:1]).then_inc(root_done.sem, 1)

        @block.vector
        def _(dve):
            v = nc.vector
            chain = [0]

            def link(g, ins):
                chain[0] += 1
                ins.then_inc(dve_chain.sem, 1)
                dve.wait_ge(dve_chain.sem, dve_chain.at(g, chain[0]))

            def product(g, c):
                dve.wait_ge(proj_done.sem, proj_done.at(g, c + 1))

            def low(g, o, k, dst_lo, dst_hi, src, col):
                dve.wait_ge(hi[o].sem, hi[o].at(g, k + 1))
                v.scalar_tensor_tensor(dst_lo[:, k, :], src, VEC[:, col:col + 1], dst_hi[:, k, :].bitcast(F32),
                                       ALU.mult, ALU.subtract).then_inc(lo[o].sem, 1)

            def inverse(g, n, dst):
                dve.wait_ge(root_done.sem, root_done.at(g, n + 1))
                link(g, v.reciprocal(dst, dst))

            def conv(g, n, p):
                xb = XB[:, n % 2, :]
                product(g, AT["X", n])
                seg = segments(xb[:, S0 + PREV:])
                if n == 0:
                    dve.wait_ge(state_in.sem, state_in.at(g, 2))
                    inverse(g, N_IN0, RN[:])
                v.tensor_copy(seg[:, :, 0:PREV], CST[:, n])
                v.tensor_copy(xb[:, 0:PREV], CC[:, n])
                v.tensor_tensor(xb[:, PREV:PREV + C], PSUM[:, 2 * p, 0:C], RN[:, 0:C], ALU.mult)
                v.tensor_tensor(xb[:, PREV + C:PREV + TP], PSUM[:, 2 * p + 1, 0:TB], RN[:, C:TP], ALU.mult)
                v.tensor_tensor(seg[:, :, PREV:], samples(PSUM[:, 2 * p + 1, TB:C]), samples(RN[:, TP:T]),
                                ALU.mult).then_inc(proj_free.sem, 1)
                dve.wait_ge(proj_free.sem, proj_free.at(g, AT["X", n] + 1))
                xc = XC[:, n % 2, :]
                link(g, v.tensor_scalar(xc, xb[:, 0:FLAT], VEC[:, V_CW + n:V_CW + n + 1],
                                        VEC[:, V_CB + n:V_CB + n + 1], ALU.mult, ALU.add))
                for k in range(1, TAPS):
                    w = V_CW + KT * k + n
                    ins = v.scalar_tensor_tensor(xc, xb[:, k:k + FLAT], VEC[:, w:w + 1], xc, ALU.mult, ALU.add)
                    if k < PREV:
                        link(g, ins)
                    else:
                        ins.then_inc(xc_done.sem, 1)
                v.tensor_copy(CC[:, n], xb[:, TP:TP + PREV])
                v.tensor_copy(CSO[:, n], seg[:, :, SEG - PREV:])

            def recur(g, n):
                dve.wait_ge(decay_done.sem, decay_done.at(g, n + 1))
                v.scalar_tensor_tensor(TR[:], TR[:], 1.0, TH[:], ALU.add, ALU.mult).then_inc(q2_done.sem, 1)
                dve.wait_ge(xc_done.sem, xc_done.at(g, n + 1))
                v.scalar_tensor_tensor(TI[:], TI[:], 1.0, XC[:, n % 2, :], ALU.add, ALU.mult)
                link(g, v.memset(segments(AA[:, S0:])[:, :, PREV - 1], 0.0))
                dve.wait_ge(q2_root.sem, q2_root.at(g, n + 1))
                link(g, v.tensor_tensor(TI[:], TI[:], TR[:], ALU.mult))
                link(g, v.tensor_copy(segments(TI[:, S0:])[:, :, PREV - 1], HST[:, n]))
                if n >= 4:
                    dve.wait_ge(y_val["y0"].sem, y_val["y0"].at(g, n - 3))
                link(g, v.tensor_tensor_scan(LR[:, n % 4, :], AA[:], TI[:], HC[:, n:n + 1], ALU.mult, ALU.add))
                v.tensor_copy(HSO[:, n], segments(LR[:, n % 4, S0:])[:, :, SEG - 1])
                v.tensor_copy(HC[:, n:n + 1], LR[:, n % 4, TP - 1:TP]).then_inc(lru_done.sem, 1)

            def half_gate(g, c, slot, r):
                product(g, c)
                v.scalar_tensor_tensor(halves(GH[:, slot, :]), pair(PAIR[c]), 0.5, halves(r), ALU.mult,
                                       ALU.mult).then_inc(proj_free.sem, 1)

            def silu(g, i):
                dve.wait_ge(tanh_done.sem, tanh_done.at(g, (i if i < KT else i + KT) + 1))
                tg = TG[:, i % KT % 3, :]
                v.scalar_tensor_tensor(tg, tg, 1.0, GH[:, i % 2, :], ALU.add, ALU.mult)\
                 .then_inc(silu_done.sem, 1)

            def embed(g, c, i, m, o):
                s = m % 2
                dve.wait_ge(tanh_done.sem, tanh_done.at(g, i + 1))
                product(g, c + 1)
                v.scalar_tensor_tensor(halves(GH[:, s, :]), halves(TG[:, s, :]), 1.0, pair(3), ALU.add,
                                       ALU.mult).then_inc(proj_free.sem, 1)
                dve.wait_ge(proj_free.sem, proj_free.at(g, c + 2))
                v.scalar_tensor_tensor(H[:, m, :], GH[:, s, :], 0.5, H[:, m, :], ALU.mult, ALU.add)\
                 .then_inc(h_new[o].sem, 1)

            def final(g, k):
                v.scalar_tensor_tensor(H[:, k, :], H[:, k, :], VEC[:, V_FIN + k:V_FIN + k + 1], R[:], ALU.mult,
                                       ALU.mult).then_inc(y_fin.sem, 1)

            def row_max(g, ev, sc, sink):
                s = ev if ev == 0 else 1 + (ev - 1) % 3
                link(g, v.tensor_reduce(MX[:, s, :], sc, AX_X, ALU.max))
                link(g, v.tensor_tensor(MX[:, s, :], MX[:, s, :], VEC[:, sink:sink + 4], ALU.max))
                v.tensor_scalar(NM[:, s, :], MX[:, s, :], -1.0, None, ALU.mult)
                v.tensor_tensor(ES[:, s, :], VEC[:, sink:sink + 4], MX[:, s, :], ALU.subtract).then_inc(nm_ready.sem, 1)

            def scores(g, u):
                kv, b = divmod(u, NB)
                sc = SC[:, u % 3]
                dve.wait_ge(s_done.sem, s_done.at(g, u + 2))
                for i in range(4):
                    ins = v.scalar_tensor_tensor(sc[:, i, :], DIST[:] if b else DIST0[:],
                                                 -slope(4 * kv + 2 * (i % 2) + i // 2),
                                                 PSUM[:, 4 + i // 2, (i % 2) * 2 * BLK:(i % 2 + 1) * 2 * BLK],
                                                 ALU.mult, ALU.add)
                ins.then_inc(s_read.sem, 1)
                dve.wait_ge(s_read.sem, s_read.at(g, u + 2))
                row_max(g, u + 1, sc, V_SINK + 4 * kv)

            def divide(g, ev, sc, width):
                s = ev if ev == 0 else 1 + (ev - 1) % 3
                dve.wait_ge(exp_done.sem, exp_done.at(g, ev + 1))
                link(g, v.tensor_tensor(DEN[:, s, :], DEN[:, s, :], ES[:, s, :], ALU.add))
                link(g, v.reciprocal(DEN[:, s, :], DEN[:, s, :]))
                for i in range(4):
                    ins = v.tensor_scalar(sc[:, i, 0:width], sc[:, i, 0:width], DEN[:, s, i:i + 1], None, ALU.mult)
                ins.then_inc(p_ready.sem, 1)

            n_set = [0]

            def setup(ins):
                n_set[0] += 1
                ins.then_inc(dve_setup.sem, 1)
                dve.wait_ge(dve_setup.sem, n_set[0])

            dve.wait_ge(consts_in.sem, 6 * 16)
            dve.wait_ge(h_in.sem, 16)
            dve.wait_ge(memset_done.sem, 8)
            lam = VEC[:, V_LAM:V_LAM + KT]
            setup(v.tensor_scalar(SP[:, 5, :], lam, -1.0, None, ALU.mult))
            setup(v.tensor_tensor(SP[:, 0, :], lam, SP[:, 5, :], ALU.max))
            setup(v.tensor_scalar(VEC[:, V_BR:V_BR + 2 * KT], VEC[:, V_BR:V_BR + 2 * KT], 0.5, None, ALU.mult))
            dve.wait_ge(act_setup.sem, 1)
            y = SP[:, 1, :]
            setup(v.tensor_scalar(SP[:, 2, :], y, 2.0, None, ALU.add))
            setup(v.reciprocal(SP[:, 2, :], SP[:, 2, :]))
            setup(v.tensor_tensor(SP[:, 2, :], SP[:, 2, :], y, ALU.mult))
            z, z2, q = SP[:, 2, :], SP[:, 3, :], SP[:, 4, :]
            setup(v.tensor_tensor(z2, z, z, ALU.mult))
            setup(v.tensor_scalar(q, z2, 1.0 / 17, None, ALU.mult))
            for d in (15, 13, 11, 9, 7, 5, 3):
                setup(v.scalar_tensor_tensor(q, q, 1.0 / d, z2, ALU.add, ALU.mult))
            setup(v.scalar_tensor_tensor(q, q, 1.0, z, ALU.add, ALU.mult))
            setup(v.tensor_scalar(SP[:, 5, :], SP[:, 5, :], 0.0, None, ALU.max))
            setup(v.scalar_tensor_tensor(q, q, 2.0, SP[:, 5, :], ALU.mult, ALU.add))
            setup(v.tensor_scalar(C1[:, 0, :], q, -4.0, None, ALU.mult))
            setup(v.tensor_scalar(C1[:, 1, :], q, 4.0, None, ALU.mult))
            for n in range(FREE_HEAD):
                v.memset(SP[:, n, :], 0.0).then_inc(proj_free.sem, 1)
            for k in range(KT):
                low(0, "in0", k, Alo, Ahi, XS[:, k % 2, :], V_G0 + k)

            with dve.Fori(0, GROUPS) as g:
                chain[0] = 0
                dve.wait_ge(lo["in0"].sem, lo["in0"].at(g, KT))
                link(g, v.memset(XB[:, :, PREV + TP:PREV + S0], 0.0))
                for c in range(NBLK):
                    kind, m = ORDER[c]
                    if kind == "g":
                        continue
                    if c in RI_BEFORE:
                        recur(g, RI_BEFORE[c])
                    if kind == "X":
                        conv(g, m, PAIR[c])
                    if c == 2:
                        inverse(g, N_FIN, R[:])
                    if kind == "G":
                        half_gate(g, c, m % 2, RN[:])
                        dve.wait_ge(lru_done.sem, lru_done.at(g, m + 1))
                        silu(g, m)
                    if 3 <= c < 7:
                        final(g, 2 * (c - 3))
                        final(g, 2 * (c - 3) + 1)
                    if kind in "Oo":
                        o, V_P, dl, dh = ("pl0", V_P0, Alo, Ahi) if kind == "O" else ("pl1", V_P1, Blo, Bhi)
                        if c == O0:
                            dve.wait_ge(h_in.sem, h_in.at(g, 1))
                        product(g, c)
                        v.tensor_tensor(halves(H[:, m, :]), pair(PAIR[c]), halves(H[:, m, :]), ALU.add)\
                         .then_inc(proj_free.sem, 1)
                        if m:
                            low(g, o, m - 1, dl, dh, H[:, m - 1, :], V_P + m - 1)
                        if m == KT - 1:
                            low(g, o, m, dl, dh, H[:, m, :], V_P + m)
                            l = int(kind == "o")
                            dve.wait_ge(p_hi.sem, p_hi.at(g, l + 1))
                            v.tensor_tensor(Plo[:], PS_[:], Phi[:].bitcast(F32), ALU.subtract).then_inc(p_lo.sem, 1)
                    if kind in "Zz":
                        i = (KT if kind == "Z" else 3 * KT) + m
                        if m == 0:
                            inverse(g, N_PL0 if kind == "Z" else N_PL1, R[:])
                        half_gate(g, c, m % 2, R[:])
                        if kind == "Z" and m:
                            low(g, "in1", m - 1, Blo, Bhi, H[:, m - 1, :], V_G1 + m - 1)
                        if kind == "z":
                            for k in ((0, 1) if m == 0 else (m + 1,)):
                                if k < KT:
                                    low((g, 1), "in0", k, Alo, Ahi, XS[:, k % 2, :], V_G0 + k)
                        embed(g, c, i, m, "in1" if kind == "Z" else "fin")
                        if m == KT - 1 and kind == "Z":
                            low(g, "in1", m, Blo, Bhi, H[:, m, :], V_G1 + m)
                    if kind == "k":
                        if m == 0:
                            inverse(g, N_IN1, R[:])
                            dve.wait_ge(state_out.sem, state_out.at(g, 2))
                        p = PAIR[c]
                        product(g, c)
                        v.tensor_tensor(K[:, m, BLK:BLK + C], PSUM[:, 2 * p, 0:C], R[:, 0:C], ALU.mult)
                        v.tensor_tensor(K[:, m, BLK + C:], PSUM[:, 2 * p + 1, 0:TB], R[:, C:TP], ALU.mult)
                        v.tensor_tensor(KS[:, m, :, WIN:], samples(PSUM[:, 2 * p + 1, TB:C]), samples(R[:, TP:T]),
                                        ALU.mult).then_inc(proj_free.sem, 1)
                    if kind == "v":
                        product(g, c)
                        v.tensor_tensor(halves(VT[:, m, :]), pair(PAIR[c]), halves(R[:]), ALU.mult)\
                         .then_inc(proj_free.sem, 1)
                    if kind == "q":
                        product(g, c)
                        v.scalar_tensor_tensor(halves(Q[:, m, :]), pair(PAIR[c]), HD ** -0.5, halves(R[:]),
                                               ALU.mult, ALU.mult).then_inc(proj_free.sem, 1)
                        if m == KT - 1:
                            dve.wait_ge(proj_free.sem, proj_free.at(g, c + 1))
                            for s in range(SG):
                                ins = v.tensor_copy(
                                    QS[:, s, :, 0:2 * ST].rearrange("p k (j t) -> p k j t", t=ST),
                                    Q[:, :, TP + s * ST:TP + (s + 1) * ST].rearrange("p (k j) t -> p k j t", j=2))
                            ins.then_inc(q_ready.sem, 1)
                    if c == G1 - 1:
                        ss = SC[:, 2].rearrange("p a b -> p (a b)")[:, 0:4 * SW]
                        s4 = ss.rearrange("p (i w) -> p i w", w=SW)
                        dve.wait_ge(s_done.sem, s_done.at(g, 1))
                        v.tensor_tensor(ss.rearrange("p (a w) -> p a w", a=2), PSUM[:, 4:6, 0:SG * SW], TBS[:],
                                        ALU.add).then_inc(s_read.sem, 1)
                        dve.wait_ge(s_read.sem, s_read.at(g, 1))
                        row_max(g, 0, s4, V_SINKS)
                        half_gate(g, G1, 0, R[:])
                        divide(g, 0, s4, SW)
                        scores(g, 0)
                        silu(g, KT)
                        for u in range(NU):
                            kv, b = divmod(u, NB)
                            if u + 1 < NU:
                                scores(g, u + 1)
                            if u == 0:
                                dve.wait_ge(o_done.sem, o_done.at(g, 1))
                                v.tensor_copy(OS[:].rearrange("p a b -> p (a b)"),
                                              PSUM[:, 6, 0:KT * TS]).then_inc(os_read.sem, 1)
                            divide(g, u + 1, SC[:, u % 3], 2 * BLK)
                            if u in WHOLE:
                                j = WHOLE[u]
                                half_gate(g, G1 + j, j % 2, R[:])
                            elif u - 1 in WHOLE:
                                silu(g, KT + WHOLE[u - 1])
                        silu(g, 2 * KT - 1)
                        for t in (K, KX):
                            v.tensor_copy(t[:, :, 0:BLK], t[:, :, TP:TP + BLK])
                        v.tensor_copy(V[:, 0, :], V[:, NB, :])
                        v.tensor_copy(DIST0[:], DIST[:]).then_inc(carry_done.sem, 1)
                assert chain[0] == DVE_CHAIN, chain[0]
            chain[0] = 0
            dve.wait_ge(root_done.sem, root_done.at(GROUPS, 1))
            link(GROUPS, v.reciprocal(R[:], R[:]))
            for k in range(KT):
                final(GROUPS, k)

        @block.tensor
        def _(pe):
            def project(g, c, hi_t, lo_t, ready, k0=0, k1=None):
                nk = 2 if is_small(c) else KT
                k1 = nk if k1 is None else k1
                if k0 == 0:
                    pe.wait_ge(w_lo.sem, w_lo.at(g, c + 1))
                    pe.wait_ge(proj_free.sem, proj_free.at(g, before_in_pair(c) + 1))
                s, p = c % RING, PAIR[c]
                for k in range(k0, k1):
                    if ready is not None:
                        pe.wait_ge(ready.sem, ready.at(g, k + 1))
                    for n, (w, x) in enumerate(((WH, hi_t), (WH, lo_t), (WL, hi_t))):
                        for a in range(2):
                            ins = nc.tensor.matmul(PSUM[:, 2 * p + a, 0:C], w[:, s, k, :], x[:, k, a * C:(a + 1) * C],
                                                   start=(k == 0 and n == 0), stop=(k == nk - 1 and n == 2))
                if k1 == nk:
                    ins.then_inc(proj_done.sem, 1)

            def mean_square(g, o, acc, roots):
                pe.wait_ge(added[o].sem, added[o].at(g, KT - 1))
                if roots:
                    pe.wait_ge(root_done.sem, root_done.at(g, roots))
                for a in range(2):
                    ins = nc.tensor.matmul(PSUM[:, 4 + a, 0:C], ONE[:], acc[:, a * C:(a + 1) * C], start=True, stop=True)
                ins.then_inc(ms_done.sem, 1)

            def final_sum(g):
                pe.wait_ge(added["fin"].sem, added["fin"].at(g, 0))
                pe.wait_ge(proj_free.sem, proj_free.at(g, 0))
                for a in range(2):
                    ins = nc.tensor.matmul(PSUM[:, 6 + a, 0:C], ONE[:], ACC[:, a * C:(a + 1) * C], start=True, stop=True)
                ins.then_inc(ms_done.sem, 1)

            def static_wait():
                pe.wait_ge(memset_done.sem, 8)

            def gate_products(g, n):
                pe.wait_ge(xc_done.sem, xc_done.at(g, n + 1))
                if n == 0:
                    pe.wait_ge(root_done.sem, root_done.at(g, N_FIN + 1))
                else:
                    pe.wait_ge(ri_read.sem, ri_read.at(g, n))
                hw = FLAT // 2
                for w in range(2):
                    for a in range(2):
                        ins = nc.tensor.matmul(PSUM[:, 4 + 2 * w + a, 0:hw], WRI[:, w * KT + n, :],
                                               XC[:, n % 2, a * hw:(a + 1) * hw], start=True, stop=True)
                ins.then_inc(ri_done.sem, 1)

            def turn_values(g, t):
                pe.wait_ge(proj_free.sem, proj_free.at(g, AT["v", t] + 1))
                if t == 0:
                    pe.wait_ge(root_done.sem, root_done.at(g, N_IN1 + 1))
                for b in range(NB):
                    nc.tensor.transpose(PSUM[:, 6 + t, b * 128:(b + 1) * 128], VT[:, t, b * BLK:(b + 1) * BLK], IDN[:])
                for s in range(SG):
                    ins = nc.tensor.matmul(PSUM[0:ST, 4 + t, s * 128:(s + 1) * 128],
                                           VT[:, t, TP + s * ST:TP + (s + 1) * ST], IDN[:], start=True, stop=True)
                ins.then_inc(v_turned.sem, 1)

            def key_half(kv, par):
                return kv % 2 == par

            def unit_scores(g, u):
                kv, b = divmod(u, NB)
                pe.wait_ge(s_read.sem, s_read.at(g, u + 1))
                for j in range(2):
                    for par in range(2):
                        h0 = 64 * par
                        keys = K if key_half(kv, par) else KX
                        ins = nc.tensor.matmul(PSUM[:, 4 + par, j * 2 * BLK:(j + 1) * 2 * BLK],
                                               Q[h0:h0 + 64, 2 * kv + j, b * BLK:(b + 1) * BLK],
                                               keys[h0:h0 + 64, kv // 2, b * BLK:(b + 2) * BLK], start=True, stop=True)
                ins.then_inc(s_done.sem, 1)

            def unit_turn(g, u):
                pe.wait_ge(p_ready.sem, p_ready.at(g, u + 2))
                if u:
                    pe.wait_ge(o_read.sem, o_read.at(g, u))
                else:
                    pe.wait_ge(os_read.sem, os_read.at(g, 1))
                for h in range(2):
                    for i in range(4):
                        ins = nc.tensor.transpose(PSUM[:, 6 + h, i * BLK:(i + 1) * BLK],
                                                  SC[:, u % 3, i, h * BLK:(h + 1) * BLK], IDN[:])
                ins.then_inc(t_done.sem, 1)

            def unit_values(g, u):
                kv, b = divmod(u, NB)
                pe.wait_ge(pt_ready.sem, pt_ready.at(g, u + 2))
                static_wait()
                for par in range(2):
                    for h in range(2):
                        ins = nc.tensor.matmul(PSUM[64 * par:64 * par + 64, 6, 0:2 * BLK],
                                               V[:, b + h, kv * HD:(kv + 1) * HD],
                                               PT[:, h, 2 * par * BLK:2 * (par + 1) * BLK], start=(h == 0), stop=(h == 1))
                ins.then_inc(o_done.sem, 1)

            def sample_scores(g):
                for kv in range(NKV):
                    for s in range(SG):
                        for par in range(2):
                            h0 = 64 * par
                            keys = KS if key_half(kv, par) else KSX
                            ins = nc.tensor.matmul(PSUM[32 * kv:32 * kv + 32, 4 + par, s * SW:(s + 1) * SW],
                                                   QS[h0:h0 + 64, s, kv, :], keys[h0:h0 + 64, kv // 2, s, :],
                                                   start=True, stop=True)
                ins.then_inc(s_done.sem, 1)

            def sample_turn(g):
                pe.wait_ge(p_ready.sem, p_ready.at(g, 1))
                ss = SC[:, 2].rearrange("p a b -> p (a b)")
                for i in range(4):
                    nc.tensor.transpose(PSUM[:, 6, i * 128:(i + 1) * 128], ss[:, i * SW:i * SW + WIN], IDN[:])
                for i in range(4):
                    ins = nc.tensor.matmul(PSUM[0:ST, 7, i * 128:(i + 1) * 128], ss[:, i * SW + WIN:(i + 1) * SW],
                                           IDN[:], start=True, stop=True)
                ins.then_inc(t_done.sem, 1)

            def sample_values(g):
                pe.wait_ge(pt_ready.sem, pt_ready.at(g, 1))
                static_wait()
                out = PSUM[:, 6, 0:KT * TS].rearrange("p (m s t) -> p m s t", m=KT, s=SG)
                for par in range(2):
                    for s in range(SG):
                        for kv in range(NKV):
                            i = SG * par + s
                            o = out[64 * par:64 * par + 64, 2 * kv:2 * kv + 2, s, :]
                            cols = slice(i * 128 + 32 * kv, i * 128 + 32 * kv + 2 * ST)
                            nc.tensor.matmul(o, VS[:, s, kv * HD:(kv + 1) * HD], PT[:, 0, cols], start=True, stop=False)
                            ins = nc.tensor.matmul(o, VN[0:ST, s, kv * HD:(kv + 1) * HD], PT[0:ST, 1, cols],
                                                   start=False, stop=True)
                ins.then_inc(o_done.sem, 1)

            pe.wait_ge(consts_in.sem, 6 * 16)
            pe.wait_ge(memset_done.sem, 8)
            nc.tensor.matmul(PSUM[:, 0, 0:128], ONE[:], ONE[:], start=True, stop=True).then_inc(proj_done.sem, 1)
            with pe.Fori(0, GROUPS) as g:
                for c in range(NBLK):
                    kind, m = ORDER[c]
                    if c in RI_BEFORE:
                        gate_products(g, RI_BEFORE[c])
                    if c == G1 - 1:
                        pe.wait_ge(k_swapped.sem, k_swapped.at(g, 4))
                        pe.wait_ge(ks_in.sem, ks_in.at(g, 3))
                        pe.wait_ge(v_ready.sem, v_ready.at(g, 2))
                    if c < 2:
                        ready = None if c else lo["in0"]
                        project(g, c, Ahi, Alo, ready, 0, KT // 2)
                        if c:
                            final_sum(g)
                        else:
                            mean_square(g, "in0", ACCN, 0)
                        project(g, c, Ahi, Alo, ready, KT // 2)
                    elif kind in "XG":
                        project(g, c, Ahi, Alo, None)
                    elif kind in "Oo":
                        a, b, o = (Bhi, Blo, "y0") if kind == "O" else (Ahi, Alo, "y1")
                        if m == 0:
                            for k0, k1 in ((0, KT - 2), (KT - 2, KT)):
                                project(g, c, a, b, lo[o], k0, k1)
                                project(g, c + 1, a, b, None, k0, k1)
                        if m > 1:
                            project(g, c, a, b, None)
                    elif kind in "Pp":
                        if m == 0:
                            pe.wait_ge(p_lo.sem, p_lo.at(g, 1 + (kind == "p")))
                        project(g, c, Phi, Plo, None)
                    elif kind in "Zzkvq":
                        a, b, o = (Ahi, Alo, "pl0") if kind == "Z" else (Bhi, Blo, "pl1" if kind == "z" else "in1")
                        if c == L1:
                            project(g, c, a, b, lo[o], 0, KT - 2)
                            project(g, c + 1, a, b, None, 0, KT - 2)
                            project(g, c, a, b, lo[o], KT - 2)
                            mean_square(g, o, ACC, N_IN1)
                            project(g, c + 1, a, b, None, KT - 2)
                        elif c in (Z0, Z1):
                            project(g, c, a, b, lo[o])
                            mean_square(g, o, ACC, {Z0: N_PL0, Z1: N_PL1}[c])
                        elif c != L1 + 1:
                            project(g, c, a, b, None)
                    if c == Q1:
                        turn_values(g, 0)
                    if c == Q1 + 1:
                        turn_values(g, 1)
                    if c == G1 - 1:
                        project(g, G1, Bhi, Blo, None, 0, KT // 2)
                        pe.wait_ge(q_ready.sem, q_ready.at(g, 1))
                        project(g, G1, Bhi, Blo, None, KT // 2)
                        sample_scores(g)
                        project(g, G1 + 1, Bhi, Blo, None, 0, KT // 2)
                        unit_scores(g, 0)
                        project(g, G1 + 1, Bhi, Blo, None, KT // 2)
                        sample_turn(g)
                        unit_scores(g, 1)
                        sample_values(g)
                        for u in range(NU):
                            if u + 2 < NU:
                                unit_scores(g, u + 2)
                            unit_turn(g, u)
                            k = 2 * KT + FILL * u
                            end = k + FILL
                            while k < end:
                                stop = min(end, (k // KT + 1) * KT)
                                project(g, G1 + k // KT, Bhi, Blo, None, k % KT, stop - k // KT * KT)
                                k = stop
                            unit_values(g, u)
            final_sum(GROUPS)


def kernel(**inputs):
    import numpy as np
    import concourse.bacc as bacc
    from concourse.bass_utils import run_bass_kernel_spmd

    i = {k: np.ascontiguousarray(v) for k, v in inputs.items()}

    def by_group(prompt, sample, extra=0):
        f = prompt.shape[-1]
        out = np.zeros((GROUPS + extra, T, f), np.float32)
        out[:GROUPS, :TP] = prompt.reshape(GROUPS, TP, f)
        out[:GROUPS, TP:] = sample.reshape(GROUPS, TS, f)
        return np.ascontiguousarray(out.reshape(-1, T, f // 128, 128).transpose(0, 3, 2, 1))

    def w_block(w, m):
        return w[:, m * 128:(m + 1) * 128].reshape(-1, 128, 128).transpose(1, 0, 2)

    win_a, win_b = i["w_in_a"][0], i["w_in_b"][0]
    take = {"X": (win_a, 0), "G": (win_a, KT), "O": (i["w_out_a"][0], 0), "Z": (i["w_ple_gate"][0], 0),
            "P": (i["w_ple_proj"][0], 0), "q": (win_b, 0), "k": (win_b, KT), "v": (win_b, KT + 2),
            "g": (win_b, KT + 4), "o": (i["w_out_b"][0], 0), "z": (i["w_ple_gate"][1], 0),
            "p": (i["w_ple_proj"][1], 0)}
    big = np.stack([w_block(take[k][0], take[k][1] + m) for k, m in ORDER if k not in "Pp"])
    small = np.stack([w_block(take[k][0], m) for k in "Pp" for m in range(KT)])

    def cols(v):
        return v.reshape(KT, 128).T

    heads = np.array([4 * kv + 2 * j + par for kv in range(NKV) for par in range(2) for j in range(2)])
    sinks = i["sinks"][0]
    row_head = np.zeros((128, 2), np.int64)
    bias_s = np.zeros((128, 2, SG, SW), np.float32)
    key = np.arange(SW)
    for kv in range(NKV):
        for j in range(2):
            for t in range(ST):
                r = 32 * kv + ST * j + t
                dist = WIN + t - key
                for par in range(2):
                    h = 4 * kv + 2 * j + par
                    row_head[r, par] = h
                    bias_s[r, par] = np.where((dist >= 0) & (dist < WIN), -slope(h) * dist, -1e30)
    vec = np.concatenate(
        [cols(i["norm_g"][0]), cols(i["norm_g"][1]), cols(i["ple_norm_g"][0]), cols(i["ple_norm_g"][1]),
         cols(i["final_norm_g"])] + [cols(i["conv_w_a"][0][k]) for k in range(TAPS)]
        + [cols(i[n][0]) for n in ("conv_b_a", "b_rgate", "b_igate", "lru_lambda")]
        + [np.broadcast_to(sinks[heads], (128, NH)), np.repeat(sinks[row_head], SG, axis=1)], axis=1)
    q, s = np.arange(BLK)[:, None], np.arange(2 * BLK)[None]
    d = BLK + q - s
    dist = np.where((d >= 0) & (d < WIN), d, MASKED).astype(np.float32)
    first = np.where(s < BLK, MASKED, dist).astype(np.float32)
    w_ri = np.concatenate([i["w_rgate"][0], i["w_igate"][0]]).transpose(1, 0, 2)
    ck, cv = (i[n][0].reshape(GROUPS, SG, WIN, NKV * HD) for n in ("cache_k", "cache_v"))
    k_cache = ck.reshape(GROUPS, SG, WIN, 2, 128).transpose(0, 4, 3, 1, 2)
    arrays = {
        "x": by_group(i["x_prompt"][0], i["x_sample"], 1),
        "p0": by_group(i["p_prompt"][0, 0], i["p_sample"][0]),
        "p1": by_group(i["p_prompt"][1, 0], i["p_sample"][1]),
        "w_big": big, "w_small": small, "w_ri": w_ri, "vec": vec,
        "dist": np.stack([dist, first]), "bias_s": bias_s.reshape(128, 2, SG * SW),
        "ident": np.eye(128, dtype=np.float32),
        "h_state": i["state_lru_h"][0].reshape(GROUPS, SG, KT, 128).transpose(0, 3, 2, 1),
        "conv_state": i["state_conv"][0].reshape(GROUPS, SG, PREV, KT, 128).transpose(0, 4, 3, 1, 2),
        "k_cache": k_cache, "k_cache_x": np.roll(k_cache, 64, axis=1),
        "v_cache": cv.transpose(0, 2, 1, 3),
    }
    arrays = {k: np.ascontiguousarray(v) for k, v in arrays.items()}
    outs = {
        "y_out": (GROUPS + 1, 128, KT, T), "h_out": (128, KT), "conv_out": (128, KT, PREV),
        "k_out": (128, 2, BLK), "v_out": (BLK, NKV * HD), "h_state_out": (GROUPS, 128, KT, SG),
        "conv_state_out": (GROUPS, 128, KT, SG, PREV), "ks_out": (GROUPS, 128, 2, SG, WIN),
        "vs_out": (GROUPS, WIN, SG, NKV * HD),
    }
    nc = bacc.Bacc("TRN2", target_bir_lowering=False, num_devices=1)
    aps = {k: nc.dram_tensor(k, v.shape, F32, kind="ExternalInput").ap() for k, v in arrays.items()}
    aps.update({k: nc.dram_tensor(k, v, F32, kind="ExternalOutput").ap() for k, v in outs.items()})
    build(nc, aps)
    r = run_bass_kernel_spmd(nc, [arrays], core_ids=[0]).results[0]
    y = r["y_out"][1:].transpose(0, 3, 2, 1).reshape(GROUPS, T, D)
    return (
        y[:, :TP].reshape(1, SEQ, D),
        y[:, TP:].reshape(NSEQ, ST, D),
        r["h_out"].T.reshape(1, 1, D),
        r["conv_out"].transpose(2, 1, 0).reshape(1, 1, PREV, D),
        r["k_out"].transpose(2, 1, 0).reshape(1, 1, WIN, NKV, HD),
        r["v_out"].reshape(1, 1, WIN, NKV, HD),
        r["h_state_out"].transpose(0, 3, 2, 1).reshape(1, NSEQ, D),
        r["conv_state_out"].transpose(0, 3, 4, 2, 1).reshape(1, NSEQ, PREV, D),
        r["ks_out"].transpose(0, 3, 4, 2, 1).reshape(1, NSEQ, WIN, NKV, HD),
        r["vs_out"].transpose(0, 2, 1, 3).reshape(1, NSEQ, WIN, NKV, HD),
    )
```

```python
from contextlib import ExitStack

import concourse.bass as bass
from concourse import mybir

F32 = mybir.dt.float32
F32R = mybir.dt.float32r
ALU = mybir.AluOpType
ACT = mybir.ActivationFunctionType
AX_X = mybir.AxisListType.X

D = 1024
KT = D // 128
SEQ = 2048
GROUPS = 4
TP = SEQ // GROUPS
NSEQ, ST = 8, 4
SG = NSEQ // GROUPS
TS = SG * ST
T = TP + TS
C = T // 2
TB = C - TS
TAPS = 4
PREV = TAPS - 1
SEG = PREV + ST
PAD = 2
FLAT = TP + PAD + SG * SEG
XBW = FLAT + PREV
S0 = TP + PAD
NH, HD, NKV = 16, 64, 4
WIN = 128
BLK = 128
NB = TP // BLK
NU = NB * NKV
SW = WIN + ST
EPS = 1e-6
MASKED = 1e33

ORDER = [("X", 0), ("X", 1), ("X", 2)]
for _n in range(5):
    ORDER += [("G", _n), ("X", _n + 3)]
ORDER += [("G", 5), ("G", 6), ("G", 7)]
O0 = len(ORDER)
ORDER += [("O", m) for m in range(KT)]
Z0 = len(ORDER)
for _m in range(KT):
    ORDER += [("Z", _m), ("P", _m)]
L1 = len(ORDER)
ORDER += [("k", 0), ("k", 1), ("v", 0), ("v", 1)]
Q1 = len(ORDER)
ORDER += [("q", m) for m in range(KT)]
G1 = len(ORDER)
ORDER += [("g", m) for m in range(KT)]
O1 = len(ORDER)
ORDER += [("o", m) for m in range(KT)]
Z1 = len(ORDER)
for _m in range(KT):
    ORDER += [("z", _m), ("p", _m)]
NBLK = len(ORDER)
AT = {b: c for c, b in enumerate(ORDER)}
RING, STAGE = 4, 2
AHEAD = RING - 1
assert NBLK % RING == 0 and (NBLK - 2 * KT) % STAGE == 0
X_PARTS = 4

FILL = (KT - 2) * KT // NU
WHOLE = {max(0, -(-KT * (j - 1) // FILL) - 1): j for j in range(1, KT)}

RI_BEFORE = {2: 0, 3: 1}
RI_BEFORE.update({2 * n: n for n in range(2, KT)})
RI_FIRST = min(RI_BEFORE)
RI_INSIDE = (0, 2, 3, 4, 5, 6)
RECUR_AT = {c + (1 < n < KT - 1): n for c, n in RI_BEFORE.items()}
CONSTS = 4

PAIR = []
_turn = 0
for _b in ORDER:
    if _b[0] in "Pp" or _b == ("v", 0):
        PAIR.append(3)
    else:
        PAIR.append(_turn)
        _turn ^= 1


def before_in_pair(c):
    return next(p for p in range(c - 1, c - NBLK - 1, -1) if PAIR[p % NBLK] == PAIR[c])


FREE_HEAD = 4


def is_small(c):
    return ORDER[c % NBLK][0] in "Pp"


SIZE_INDEX = [sum(is_small(p) == is_small(c) for p in range(c)) for c in range(NBLK)]


def before_in_stage(j):
    same = [p for p in range(j - 1, j - NBLK - 1, -1) if is_small(p) == is_small(j)]
    return max(same[0 if is_small(j) else STAGE - 1], j - 2 * STAGE)


def head_at(tile, par):
    return 4 * (2 * (tile // 4) + par) + tile % 4


def slope(head):
    return 2.0 ** (-8.0 * (head + 1) / NH)


V_G0, V_G1, V_P0, V_P1, V_FIN = 0, 8, 16, 24, 32
V_CW, V_CB, V_BR, V_BI, V_LAM, V_SINK, V_SINKS = 40, 72, 80, 88, 96, 104, 120
NVEC = 124

N_IN0, N_FIN, N_PL0, N_IN1, N_PL1 = range(5)
NORMS = 5

DVE_CHAIN, ACT_CHAIN = 130, 8


class Stage:

    def __init__(self, nc, ctx, name, per, head=0, step=1):
        self.sem = ctx.enter_context(nc.semaphore(name))
        self.per, self.head, self.step = per, head, step

    def at(self, g, n):
        if isinstance(g, tuple):
            g, n = g[0], n + g[1] * self.per
        assert (isinstance(g, int) and g) or self.head + n > 0
        return g * (self.per * self.step) + (self.head + n) * self.step


def build(nc, A):
    ctx = ExitStack()
    with ctx:
        base = 16512
        place = [base]

        def sb_at(name, shape, dt, offset):
            return nc.alloc_sbuf_tensor_at(name, [128] + list(shape), dt, offset=offset)

        def sb(name, shape, dt=F32):
            n = 4
            for s in shape:
                n *= s
            off = place[0]
            place[0] += (n + 31) // 32 * 32
            return sb_at(name, shape, dt, off)

        H = sb("resid", [KT, T])
        a_at = place[0]
        Ahi = sb("a_hi", [KT, T], F32R)
        Alo = sb("a_lo", [KT, T], F32R)
        Bhi = sb("b_hi", [KT, T], F32R)
        Blo = sb("b_lo", [KT, T], F32R)
        Q = sb_at("q", [KT, T], F32, a_at + 4 * KT * T)
        LR = sb("lru_or_o", [4, FLAT])
        p_at = place[0]
        Phi = sb("p_hi", [2, T], F32R)
        Plo = sb("p_lo", [2, T], F32R)
        KS = sb_at("ks", [2, SG, SW], F32, p_at)
        VS = sb_at("vs", [SG, NKV * HD], F32, p_at + 4 * 2 * SG * SW)
        VN = sb_at("vs_new", [SG, NKV * HD], F32, p_at + 4 * 2 * SG * SW + 4 * SG * NKV * HD)
        assert 4 * 2 * SG * SW + 8 * SG * NKV * HD <= 16 * T
        WH = sb("w_hi", [RING, KT, 128], F32R)
        WL = sb("w_lo", [RING, KT, 128], F32R)
        WS = sb("w_stage", [STAGE, KT, 128])
        WSS = sb("w_stage_small", [2, 128])
        WRI = sb("w_ri", [2 * KT, 128])
        Khi = sb("k_hi", [2, BLK + TP], F32R)
        Klo = sb("k_lo", [2, BLK + TP], F32R)
        V = sb("v", [1 + NB, NKV * HD])
        t_at = place[0]
        XB = sb("conv_in", [2, XBW])
        XC = sb("conv_out", [2, FLAT])
        TR = sb("gate_r", [FLAT])
        AA = sb("decay", [FLAT])
        TH = sb("decay_th", [FLAT])
        TI = sb("gate_i", [FLAT])
        SC = sb_at("scores", [3, 4, 2 * BLK], F32, t_at)
        PT = sb_at("probs_t", [2, 4 * BLK], F32, t_at + 12288)
        VT = sb_at("v_t", [2, T], F32, t_at)
        K = sb_at("k", [2, TP], F32, t_at + 8 * T)
        PS_ = sb_at("p_stage", [2, T], F32, t_at)
        XS = sb_at("x_stage", [2, T], F32, t_at + 8 * T)
        assert 16384 <= place[0] - t_at and 16 * T <= place[0] - t_at
        GH = sb("gate_half", [2, T])
        TG = sb("gate_tanh", [3, T])
        R = sb("inv_rms", [T])
        RN = sb("inv_rms_in0", [T])
        SQ = sb("square", [2, T])
        ACC = sb("square_sum", [T])
        ACCN = sb("square_sum_in0", [T])
        DIST = sb("dist", [3, BLK])
        TBS = sb("bias_s", [2, SG * SW])
        IDN = sb("identity", [128])
        ONE = sb("ones", [128])
        VEC = sb("vec", [NVEC])
        C1 = sb("lru_c", [2, KT])
        EPT = sb("eps", [1])
        QS = sb("qs", [SG, NKV, 32])
        OS = sb("os", [KT, TS])
        HC = sb("h_carry", [KT])
        HST = sb("h_state", [KT, SG])
        HSO = sb("h_state_out", [KT, SG])
        CC = sb("conv_carry", [KT, PREV])
        CST = sb("conv_state", [KT, SG, PREV])
        CSO = sb("conv_state_out", [KT, SG, PREV])
        MX = sb("row_max", [4, 4])
        NM = sb("row_max_neg", [4, 4])
        ES = sb("sink_exp", [4, 4])
        DEN = sb("row_sum", [4, 4])
        SP = sb_at("softplus_tmp", [6, KT], F32, t_at)
        assert place[0] <= nc.sbuf_usable_end, place[0]

        PSUM = ctx.enter_context(nc.psum_tensor("psum", [128, 8, 512], F32))

        def pair(p):
            return PSUM[:, 2 * p:2 * p + 2, 0:C]

        def halves(ap):
            return ap.rearrange("p (a c) -> p a c", a=2)

        def samples(ap):
            return ap.rearrange("p (s t) -> p s t", t=ST)

        def segments(ap):
            return ap.rearrange("p (s w) -> p s w", w=SEG)

        def staged(j):
            return WSS[:] if is_small(j) else WS[:, SIZE_INDEX[j % NBLK] % STAGE, :, :]

        def square_of(o, k):
            return LR[:, k % 2, 0:T] if o == "in0" else SQ[:, k % 2, :]

        def stage(name, per, head=0, step=1):
            return Stage(nc, ctx, name, per, head, step)

        consts_in = stage("consts_in", 0, step=16)
        memset_done = stage("memset_done", 0)
        dve_setup = stage("dve_setup", 0)
        act_setup = stage("act_setup", 0)
        w_in = [stage(f"w_in{i}", (NBLK - 2 * KT) // STAGE, step=16) for i in range(STAGE)]
        w_small_in = stage("w_small_in", 2 * KT, step=16)
        w_hi = stage("w_hi_done", NBLK)
        w_lo = stage("w_lo_done", NBLK)
        proj_done = stage("proj_done", NBLK, head=1)
        proj_free = stage("proj_free", NBLK, head=FREE_HEAD)
        x_in = [stage(f"x_in{i}", KT // 2, step=16) for i in range(2)]
        h_in = stage("h_in", 1, step=16)
        vec_in = stage("vec_in", 0, step=16)
        first_in = [stage(f"first_in{i}", 0, step=16) for i in range(X_PARTS)]
        state_in = stage("state_in", 2, step=16)
        state_out = stage("state_out", 2, step=16)
        p_in = stage("p_in", 2, step=16)
        ks_in = stage("ks_in", 2, step=16)
        kv_out = stage("kv_out", 3, step=16)
        k_out = stage("k_out", 1, step=16)
        y_out = stage("y_out", 1, step=16)
        end_out = stage("end_out", 0, step=16)
        ops = ("in0", "y0", "pl0", "in1", "y1", "pl1")
        hi = {o: stage(o + "_hi", KT) for o in ops}
        lo = {o: stage(o + "_lo", KT) for o in ops}
        p_hi, p_lo = stage("p_hi_done", 2), stage("p_lo_done", 2)
        norms = ("in0", "fin", "pl0", "in1", "pl1")
        squared = {o: stage("sq_" + o, KT) for o in norms}
        added = {o: stage("add_" + o, KT - 1, head=int(o == "fin")) for o in norms}
        ms_done = stage("ms_done", NORMS)
        root_done = stage("root_done", NORMS)
        h_new = {o: stage("h_" + o, KT) for o in ("in1", "fin")}
        y_fin = stage("y_fin", KT)
        xc_done = stage("xc_done", KT)
        ri_done = stage("ri_done", KT)
        ri_read = stage("ri_read", KT)
        decay_done = stage("decay_done", KT)
        q2_done = stage("q2_done", KT)
        q2_root = stage("q2_root", KT)
        lru_done = stage("lru_done", KT)
        tanh_done = stage("tanh_done", 4 * KT)
        y_val = {o: stage(o + "_val", KT) for o in ("y0", "y1")}
        v_turned = stage("v_turned", 2)
        v_ready = stage("v_ready", 2)
        q_ready = stage("q_ready", 1)
        k_hi, k_lo = stage("k_hi_done", 2), stage("k_lo_done", 2)
        q_hi, q_lo = stage("q_hi_done", KT), stage("q_lo_done", KT)
        s_done = stage("s_done", NU + 1)
        s_read = stage("s_read", NU + 1)
        nm_ready = stage("nm_ready", NU + 1)
        exp_done = stage("exp_done", NU + 1)
        p_ready = stage("p_ready", NU + 1)
        t_done = stage("t_done", NU + 1)
        pt_ready = stage("pt_ready", NU + 1)
        o_done = stage("o_done", NU + 1)
        o_read = stage("o_read", NU)
        silu_done = stage("silu_done", 2 * KT)
        os_read = stage("os_read", 1)
        carry_done = stage("carry_done", 1)
        dve_chain = stage("dve_chain", DVE_CHAIN)
        act_chain = stage("act_chain", ACT_CHAIN)

        block = ctx.enter_context(nc.Block())

        @block.sync
        def _(sp):
            def load_weights(g, j):
                if not (isinstance(g, int) and j < STAGE):
                    sp.wait_ge(w_lo.sem, w_lo.at(g, before_in_stage(j) + 1))
                c = j % NBLK
                if is_small(c):
                    sp.dma_start(WSS[:], A["w_small"][SIZE_INDEX[c]]).then_inc(w_small_in.sem, 16)
                else:
                    s = SIZE_INDEX[c] % STAGE
                    sp.dma_start(WS[:, s, :, :], A["w_big"][SIZE_INDEX[c]]).then_inc(w_in[s].sem, 16)

            def group_of(ap, g):
                if isinstance(g, int):
                    return ap[g]
                v = ap[bass.ds(g, 1)]
                if len(ap.shape) == 3:
                    return v.rearrange("a p x -> (a p) x")
                if len(ap.shape) == 4:
                    return v.rearrange("a p x y -> (a p) x y")
                return v.rearrange("a p x y z -> (a p) x y z")

            def load_x(g, k):
                if k >= 2:
                    sp.wait_ge(lo["in0"].sem, lo["in0"].at((g, 1), k - 1))
                sp.dma_start(XS[:, k % 2, :], group_of(A["x"], g + 1)[:, k, :]).then_inc(x_in[k % 2].sem, 16)

            sp.dma_start(VEC[:], A["vec"]).then_inc(vec_in.sem, 16)
            load_weights(0, 0)
            for i in range(X_PARTS):
                sp.dma_start(H[:, 2 * i:2 * i + 2, :], A["x"][0][:, 2 * i:2 * i + 2, :]).then_inc(first_in[i].sem, 16)
            load_weights(0, 1)
            for dst, src in ((DIST[:], A["dist"]),
                             (TBS[:], A["bias_s"]), (IDN[:], A["ident"]), (WRI[:], A["w_ri"])):
                sp.dma_start(dst, src).then_inc(consts_in.sem, 16)
            for j in range(STAGE, AHEAD):
                load_weights(0, j)

            with sp.Fori(0, GROUPS) as g:
                for c in range(NBLK):
                    load_weights(g, c + AHEAD)
                    if c == 0:
                        sp.dma_start(CST[:], group_of(A["conv_state"], g)).then_inc(state_in.sem, 16)
                        sp.dma_start(HST[:], group_of(A["h_state"], g)).then_inc(state_in.sem, 16)
                    if c == 11:
                        sp.wait_ge(y_fin.sem, y_fin.at(g, KT))
                        sp.dma_start(group_of(A["y_out"], g), H[:]).then_inc(y_out.sem, 16)
                    if c == 14:
                        sp.wait_ge(y_out.sem, y_out.at(g, 1))
                        sp.dma_start(H[:], group_of(A["x"], g)).then_inc(h_in.sem, 16)
                    if c == O0 + 4:
                        sp.wait_ge(proj_done.sem, proj_done.at(g, O0 + 1))
                        sp.dma_start(PS_[:], group_of(A["p0"], g)).then_inc(p_in.sem, 16)
                        sp.dma_start(group_of(A["h_state_out"], g), HSO[:]).then_inc(state_out.sem, 16)
                        sp.dma_start(group_of(A["conv_state_out"], g), CSO[:]).then_inc(state_out.sem, 16)
                    if c == L1 + 3:
                        sp.wait_ge(proj_done.sem, proj_done.at(g, L1))
                        sp.dma_start(KS[:, :, :, 0:WIN], group_of(A["k_cache"], g)).then_inc(ks_in.sem, 16)
                        sp.dma_start(VS[:], group_of(A["v_cache"], g)).then_inc(ks_in.sem, 16)
                    if c == Q1:
                        sp.wait_ge(proj_free.sem, proj_free.at(g, AT["k", 1] + 1))
                        sp.dma_start(group_of(A["k_out"], g), K[:, :, TP - BLK:]).then_inc(k_out.sem, 16)
                    if c == Q1 + 6:
                        sp.wait_ge(ks_in.sem, ks_in.at(g, 2))
                        sp.wait_ge(v_ready.sem, v_ready.at(g, 2))
                        sp.dma_start(group_of(A["ks_out"], g),
                                     KS[:, :, :, ST:]).then_inc(kv_out.sem, 16)
                        vo = group_of(A["vs_out"], g)
                        sp.dma_start(vo[0:WIN - ST], VS[ST:]).then_inc(kv_out.sem, 16)
                        sp.dma_start(vo[WIN - ST:], VN[0:ST]).then_inc(kv_out.sem, 16)
                    if c == O1 + 4:
                        sp.wait_ge(proj_done.sem, proj_done.at(g, O1 + 1))
                        sp.dma_start(PS_[:], group_of(A["p1"], g)).then_inc(p_in.sem, 16)
                    if c == O1 + 5:
                        load_x(g, 0)
                        load_x(g, 1)
                    if c > Z1 and (c - Z1) % 2 and (c - Z1) // 2 + 2 < KT:
                        load_x(g, (c - Z1) // 2 + 2)

            sp.wait_ge(carry_done.sem, carry_done.at(GROUPS, 0))
            sp.dma_start(A["h_out"], HC[:]).then_inc(end_out.sem, 16)
            sp.dma_start(A["conv_out"], CC[:]).then_inc(end_out.sem, 16)
            sp.dma_start(A["v_out"], V[:, 0, :]).then_inc(end_out.sem, 16)
            for i in range(X_PARTS):
                sp.wait_ge(y_fin.sem, y_fin.at(GROUPS, 2 * i + 2))
                sp.dma_start(A["y_out"][GROUPS][:, 2 * i:2 * i + 2, :], H[:, 2 * i:2 * i + 2, :]).then_inc(end_out.sem, 16)
            sp.wait_ge(end_out.sem, (3 + X_PARTS) * 16)
            sp.wait_ge(y_out.sem, y_out.at(GROUPS, 0))
            sp.wait_ge(state_out.sem, state_out.at(GROUPS, 0))
            sp.wait_ge(kv_out.sem, kv_out.at(GROUPS, 0))
            sp.wait_ge(k_out.sem, k_out.at(GROUPS, 0))
            for j in range(AHEAD):
                sp.wait_ge(w_in[j % STAGE].sem, w_in[j % STAGE].at(GROUPS, j // STAGE + 1))

        @block.gpsimd
        def _(pool):
            def split_low(g, j):
                n = 2 if is_small(j) else KT
                pool.wait_ge(w_hi.sem, w_hi.at(g, j + 1))
                nc.gpsimd.tensor_tensor(WL[:, j % RING, 0:n, :], staged(j),
                                        WH[:, j % RING, 0:n, :].bitcast(F32), ALU.subtract).then_inc(w_lo.sem, 1)

            def add_square(g, o, k):
                acc = ACCN if o == "in0" else ACC
                pool.wait_ge(squared[o].sem, squared[o].at(g, k + 1))
                if k >= 2:
                    pool.wait_ge(added[o].sem, added[o].at(g, k - 1))
                nc.gpsimd.tensor_tensor(acc[:], acc[:], square_of(o, k), ALU.add).then_inc(added[o].sem, 1)

            def y_value(g, o, i, t):
                pool.wait_ge(silu_done.sem, silu_done.at(g, i + 1))
                tg = TG[:, t % 3]
                if o == "y0":
                    nc.gpsimd.tensor_tensor(tg[:, 0:TP], tg[:, 0:TP], LR[:, t % 4, 0:TP], ALU.mult)
                    ins = nc.gpsimd.tensor_tensor(samples(tg[:, TP:T]), samples(tg[:, TP:T]),
                                                  segments(LR[:, t % 4, S0:])[:, :, PREV:], ALU.mult)
                else:
                    pool.wait_ge(o_read.sem, o_read.at(g, 4 * (t // 2) + NB))
                    nc.gpsimd.tensor_tensor(tg[:, 0:TP], tg[:, 0:TP], LR[:, t % 4, 0:TP], ALU.mult)
                    ins = nc.gpsimd.tensor_tensor(tg[:, TP:T], tg[:, TP:T], OS[:, t, :], ALU.mult)
                ins.then_inc(y_val[o].sem, 1)

            def y_low(g, o, t, dst_lo, dst_hi):
                pool.wait_ge(hi[o].sem, hi[o].at(g, t + 1))
                nc.gpsimd.tensor_tensor(dst_lo[:, t, :], TG[:, t % 3, :], dst_hi[:, t, :].bitcast(F32),
                                        ALU.subtract).then_inc(lo[o].sem, 1)

            nc.gpsimd.memset(ONE[:], 1.0).then_inc(memset_done.sem, 1)
            for t in (HC[:], CC[:], Khi[:].bitcast(F32), Klo[:].bitcast(F32), V[:], QS[:]):
                nc.gpsimd.memset(t, 0.0).then_inc(memset_done.sem, 1)
            nc.gpsimd.memset(ACC[:], 0.0).then_inc(added["fin"].sem, 1)
            nc.gpsimd.memset(EPT[:], EPS).then_inc(memset_done.sem, 1)
            split_low(0, 0)
            for k in range(1, KT):
                add_square(0, "in0", k)
            for j in range(1, AHEAD):
                split_low(0, j)

            with pool.Fori(0, GROUPS) as g:
                for c in range(NBLK):
                    kind, m = ORDER[c - 1] if c else ("-", 0)
                    if kind == "G":
                        y_value(g, "y0", m, m)
                        split_low(g, c + AHEAD)
                        y_low(g, "y0", m, Blo, Bhi)
                        continue
                    if kind == "g":
                        split_low(g, c + AHEAD)
                        if m in (1, 3, 4, 6):
                            quad = (1, 3, 4, 6).index(m)
                            for t in (2 * quad, 2 * quad + 1):
                                y_value(g, "y1", KT + t, t)
                            for t in (2 * quad, 2 * quad + 1):
                                y_low(g, "y1", t, Alo, Ahi)
                        continue
                    sum_first = m and kind in "Oo" or kind in "Pp" or kind in "Zz" and m == KT - 1
                    if not sum_first:
                        split_low(g, c + AHEAD)
                    if m and kind in "Oo":
                        add_square(g, "pl0" if kind == "O" else "pl1", m)
                    if kind == "P" and 1 < m < KT - 1:
                        add_square(g, "in1", m - 1)
                    if kind == "P" and m == KT - 1:
                        add_square(g, "in1", m)
                    if kind in "Zz" and m == KT - 1:
                        add_square(g, "in1" if kind == "Z" else "fin", m - 1)
                    if kind == "p":
                        if 1 < m < KT - 1:
                            add_square(g, "fin", m - 1)
                        if m < KT - 1:
                            add_square((g, 1), "in0", m + 1)
                    if sum_first:
                        split_low(g, c + AHEAD)
                    if kind == "k":
                        pool.wait_ge(k_hi.sem, k_hi.at(g, m + 1))
                        nc.gpsimd.tensor_tensor(Klo[:, m, BLK:], K[:, m, :], Khi[:, m, BLK:].bitcast(F32),
                                                ALU.subtract).then_inc(k_lo.sem, 1)
                    if kind == "q":
                        pool.wait_ge(q_hi.sem, q_hi.at(g, m + 1))
                        nc.gpsimd.tensor_tensor(Alo[:, m, 0:TP], Q[:, m, 0:TP], Ahi[:, m, 0:TP].bitcast(F32),
                                                ALU.subtract).then_inc(q_lo.sem, 1)
                add_square(g, "fin", KT - 1)

        @block.scalar
        def _(act):
            chain = [0]

            def link(g, ins):
                chain[0] += 1
                ins.then_inc(act_chain.sem, 1)
                act.wait_ge(act_chain.sem, act_chain.at(g, chain[0]))

            def split_high(g, j):
                k = SIZE_INDEX[j % NBLK]
                if is_small(j):
                    act.wait_ge(w_small_in.sem, w_small_in.at(g, k + 1))
                else:
                    s, past = k % STAGE, j // NBLK * (NBLK - 2 * KT)
                    act.wait_ge(w_in[s].sem, w_in[s].at(g, (k + past) // STAGE + 1))
                if not (isinstance(g, int) and j < RING):
                    act.wait_ge(proj_done.sem, proj_done.at(g, j - RING + 1))
                n = 2 if is_small(j) else KT
                nc.scalar.activation(WH[:, j % RING, 0:n, :], staged(j), ACT.Copy).then_inc(w_hi.sem, 1)

            def square(g, o, k, src):
                acc = ACCN if o == "in0" else ACC
                if k > 2:
                    act.wait_ge(added[o].sem, added[o].at(g, k - 2))
                nc.scalar.activation(acc[:] if k == 0 else square_of(o, k), src, ACT.Square).then_inc(squared[o].sem, 1)

            def scaled_high(g, o, k, dst, src, col):
                nc.scalar.activation(dst, src, ACT.Copy, scale=VEC[:, col:col + 1]).then_inc(hi[o].sem, 1)

            def x_tile(g, k):
                if isinstance(g, int):
                    act.wait_ge(first_in[k // 2].sem, 16)
                    src = H[:, k, :]
                else:
                    act.wait_ge(x_in[k % 2].sem, x_in[k % 2].at(g[0], k // 2 + 1))
                    src = XS[:, k % 2, :]
                square(g, "in0", k, src)
                scaled_high(g, "in0", k, Ahi[:, k, :], src, V_G0 + k)

            def root(g, n, banks, dst):
                act.wait_ge(ms_done.sem, ms_done.at(g, n + 1))
                nc.scalar.activation(halves(dst), PSUM[:, banks:banks + 2, 0:C], ACT.Sqrt, scale=1.0 / D,
                                     bias=EPT[:, 0:1]).then_inc(root_done.sem, 1)

            def gate_tanh(g, c, o=None):
                t = ORDER[c][1]
                act.wait_ge(proj_free.sem, proj_free.at(g, c + 1))
                if o and t >= 3:
                    act.wait_ge(lo[o].sem, lo[o].at(g, t - 2))
                nc.scalar.activation(TG[:, t % 3 if o else t % 2, :], GH[:, t % 2, :], ACT.Tanh).then_inc(tanh_done.sem, 1)

            def gates(g, n):
                act.wait_ge(ri_done.sem, ri_done.at(g, n + 1))
                if n:
                    act.wait_ge(lru_done.sem, lru_done.at(g, n))
                hw = FLAT // 2
                two = lambda ap: ap.rearrange("p (a c) -> p a c", a=2)
                nc.scalar.activation(two(TI[:]), PSUM[:, 6:8, 0:hw], ACT.Tanh, scale=0.5,
                                     bias=VEC[:, V_BI + n:V_BI + n + 1])
                nc.scalar.activation(two(TR[:]), PSUM[:, 4:6, 0:hw], ACT.Tanh, scale=0.5,
                                     bias=VEC[:, V_BR + n:V_BR + n + 1]).then_inc(ri_read.sem, 1)
                act.wait_ge(ri_read.sem, ri_read.at(g, n + 1))
                nc.scalar.activation(TH[:], TR[:], ACT.Tanh, scale=C1[:, 1, n:n + 1], bias=C1[:, 1, n:n + 1])
                link(g, nc.scalar.activation(AA[:], TR[:], ACT.Exp, scale=C1[:, 0, n:n + 1], bias=C1[:, 0, n:n + 1]))
                nc.scalar.activation(TR[:], AA[:], ACT.Square).then_inc(decay_done.sem, 1)

            def decay_root(g, n):
                act.wait_ge(q2_done.sem, q2_done.at(g, n + 1))
                nc.scalar.activation(TR[:], TR[:], ACT.Sqrt, scale=0.25).then_inc(q2_root.sem, 1)

            def y_high(g, o, t, dst):
                act.wait_ge(y_val[o].sem, y_val[o].at(g, t + 1))
                nc.scalar.activation(dst[:, t, :], TG[:, t % 3, :], ACT.Copy).then_inc(hi[o].sem, 1)

            def exps(g, ev, sc, width):
                s = ev if ev == 0 else 1 + (ev - 1) % 3
                act.wait_ge(nm_ready.sem, nm_ready.at(g, ev + 1))
                for i in range(4):
                    nc.scalar.activation(sc[:, i, 0:width], sc[:, i, 0:width], ACT.Exp, bias=NM[:, s, i:i + 1],
                                         accum_out=DEN[:, s, i:i + 1])
                nc.scalar.activation(ES[:, s, :], ES[:, s, :], ACT.Exp).then_inc(exp_done.sem, 1)

            act.wait_ge(dve_setup.sem, 2)
            nc.scalar.activation(SP[:, 1, :], SP[:, 0, :], ACT.Exp, scale=-1.0).then_inc(act_setup.sem, 1)
            act.wait_ge(dve_setup.sem, 3)
            act.wait_ge(memset_done.sem, 8)
            act.wait_ge(vec_in.sem, 16)
            split_high(0, 0)
            for k in range(KT):
                x_tile(0, k)
            for j in range(1, AHEAD):
                split_high(0, j)

            with act.Fori(0, GROUPS) as g:
                chain[0] = 0
                for c in range(NBLK):
                    kind, m = ORDER[c]
                    if kind == "g":
                        continue
                    if c == 0:
                        root(g, N_IN0, 4, RN[:])
                    if c == 1:
                        root(g, N_FIN, 6, R[:])
                    split_high(g, c + AHEAD)
                    if c in RI_BEFORE:
                        gates(g, RI_BEFORE[c])
                    if c in RECUR_AT:
                        decay_root(g, RECUR_AT[c])
                    if c and ORDER[c - 1][0] == "G":
                        y_high(g, "y0", ORDER[c - 1][1], Bhi)
                    if kind == "G":
                        gate_tanh(g, c, "y0")
                    if kind in "Oo":
                        o, V_P, dst = ("pl0", V_P0, Ahi) if kind == "O" else ("pl1", V_P1, Bhi)
                        act.wait_ge(proj_free.sem, proj_free.at(g, c + 1))
                        square(g, o, m, H[:, m, :])
                        scaled_high(g, o, m, dst[:, m, :], H[:, m, :], V_P + m)
                        if m == 6:
                            l = int(kind == "o")
                            act.wait_ge(p_in.sem, p_in.at(g, l + 1))
                            if l:
                                act.wait_ge(kv_out.sem, kv_out.at(g, 3))
                            nc.scalar.activation(Phi[:], PS_[:], ACT.Copy).then_inc(p_hi.sem, 1)
                    if c in (Z0, L1, Z1):
                        root(g, {Z0: N_PL0, L1: N_IN1, Z1: N_PL1}[c], 4, R[:])
                    if kind in "Zz":
                        if kind == "z":
                            if m == 0:
                                x_tile((g, 1), 0)
                            if m < KT - 1:
                                x_tile((g, 1), m + 1)
                        gate_tanh(g, c)
                    if kind == "P":
                        act.wait_ge(h_new["in1"].sem, h_new["in1"].at(g, m + 1))
                        square(g, "in1", m, H[:, m, :])
                        scaled_high(g, "in1", m, Bhi[:, m, :], H[:, m, :], V_G1 + m)
                    if kind == "p":
                        act.wait_ge(h_new["fin"].sem, h_new["fin"].at(g, m + 1))
                        square(g, "fin", m, H[:, m, :])
                    if kind == "k":
                        act.wait_ge(proj_free.sem, proj_free.at(g, c + 1))
                        nc.scalar.activation(Khi[:, m, BLK:], K[:, m, :], ACT.Copy).then_inc(k_hi.sem, 1)
                    if kind == "q":
                        act.wait_ge(proj_free.sem, proj_free.at(g, c + 1))
                        nc.scalar.activation(Ahi[:, m, 0:TP], Q[:, m, 0:TP], ACT.Copy).then_inc(q_hi.sem, 1)
                    if c in (Q1 + 1, Q1 + 2):
                        t = c - Q1 - 1
                        act.wait_ge(v_turned.sem, v_turned.at(g, t + 1))
                        nc.scalar.activation(V[:, 1:, t * 128:(t + 1) * 128],
                                             PSUM[:, 6 + t, :].rearrange("p (b f) -> p b f", f=128), ACT.Copy)
                        nc.scalar.activation(VN[0:ST, :, t * 128:(t + 1) * 128],
                                             PSUM[0:ST, 4 + t, 0:SG * 128].rearrange("p (s f) -> p s f", f=128),
                                             ACT.Copy).then_inc(v_ready.sem, 1)
                    if c == G1 - 1:
                        split_high(g, G1 + AHEAD)
                        exps(g, 0, SC[:, 2].rearrange("p a b -> p (a b)")[:, 0:4 * SW].rearrange(
                            "p (i w) -> p i w", w=SW), SW)
                        gate_tanh(g, G1, "y1")
                        act.wait_ge(t_done.sem, t_done.at(g, 1))
                        nc.scalar.activation(PT[:, 0, :], PSUM[:, 6, :], ACT.Copy)
                        nc.scalar.activation(PT[0:ST, 1, :], PSUM[0:ST, 7, :], ACT.Copy).then_inc(pt_ready.sem, 1)
                        exps(g, 1, SC[:, 0], 2 * BLK)
                        for u in range(NU):
                            quad, b = divmod(u, NB)
                            if u + 1 < NU:
                                exps(g, u + 2, SC[:, (u + 1) % 3], 2 * BLK)
                            act.wait_ge(t_done.sem, t_done.at(g, u + 2))
                            nc.scalar.activation(PT[:], PSUM[:, 6:8, :], ACT.Copy).then_inc(pt_ready.sem, 1)
                            if u in WHOLE:
                                split_high(g, G1 + WHOLE[u] + AHEAD)
                            act.wait_ge(o_done.sem, o_done.at(g, u + 2))
                            s = 2 * (quad % 2)
                            nc.scalar.activation(LR[:, s:s + 2, b * BLK:(b + 1) * BLK],
                                                 PSUM[:, 6, 0:2 * BLK].rearrange("p (j q) -> p j q", j=2),
                                                 ACT.Copy).then_inc(o_read.sem, 1)
                            if b == 0 and u:
                                for t in (2 * quad - 2, 2 * quad - 1):
                                    y_high(g, "y1", t, Ahi)
                            if u - 1 in WHOLE:
                                gate_tanh(g, G1 + WHOLE[u - 1], "y1")
                        gate_tanh(g, G1 + KT - 1, "y1")
                        y_high(g, "y1", KT - 2, Ahi)
                        y_high(g, "y1", KT - 1, Ahi)
                assert chain[0] == ACT_CHAIN, chain[0]
            act.wait_ge(ms_done.sem, ms_done.at(GROUPS, 1))
            nc.scalar.activation(halves(R[:]), PSUM[:, 6:8, 0:C], ACT.Sqrt, scale=1.0 / D,
                                 bias=EPT[:, 0:1]).then_inc(root_done.sem, 1)

        @block.vector
        def _(dve):
            v = nc.vector
            chain = [0]

            def link(g, ins):
                chain[0] += 1
                ins.then_inc(dve_chain.sem, 1)
                dve.wait_ge(dve_chain.sem, dve_chain.at(g, chain[0]))

            def product(g, c):
                dve.wait_ge(proj_done.sem, proj_done.at(g, c + 1))

            def low(g, o, k, dst_lo, dst_hi, src, col):
                dve.wait_ge(hi[o].sem, hi[o].at(g, k + 1))
                v.scalar_tensor_tensor(dst_lo[:, k, :], src, VEC[:, col:col + 1], dst_hi[:, k, :].bitcast(F32),
                                       ALU.mult, ALU.subtract).then_inc(lo[o].sem, 1)

            def inverse(g, n, dst):
                dve.wait_ge(root_done.sem, root_done.at(g, n + 1))
                link(g, v.reciprocal(dst, dst))

            def conv(g, n, p):
                xb = XB[:, n % 2, :]
                product(g, AT["X", n])
                seg = segments(xb[:, S0 + PREV:])
                if n == 0:
                    dve.wait_ge(state_in.sem, state_in.at(g, 2))
                    inverse(g, N_IN0, RN[:])
                v.tensor_copy(seg[:, :, 0:PREV], CST[:, n])
                v.tensor_copy(xb[:, 0:PREV], CC[:, n])
                v.tensor_tensor(xb[:, PREV:PREV + C], PSUM[:, 2 * p, 0:C], RN[:, 0:C], ALU.mult)
                v.tensor_tensor(xb[:, PREV + C:PREV + TP], PSUM[:, 2 * p + 1, 0:TB], RN[:, C:TP], ALU.mult)
                v.tensor_tensor(seg[:, :, PREV:], samples(PSUM[:, 2 * p + 1, TB:C]), samples(RN[:, TP:T]),
                                ALU.mult).then_inc(proj_free.sem, 1)
                dve.wait_ge(proj_free.sem, proj_free.at(g, AT["X", n] + 1))
                xc = XC[:, n % 2, :]
                link(g, v.tensor_scalar(xc, xb[:, 0:FLAT], VEC[:, V_CW + n:V_CW + n + 1],
                                        VEC[:, V_CB + n:V_CB + n + 1], ALU.mult, ALU.add))
                for k in range(1, TAPS):
                    w = V_CW + KT * k + n
                    ins = v.scalar_tensor_tensor(xc, xb[:, k:k + FLAT], VEC[:, w:w + 1], xc, ALU.mult, ALU.add)
                    if k < PREV:
                        link(g, ins)
                    else:
                        ins.then_inc(xc_done.sem, 1)
                v.tensor_copy(CC[:, n], xb[:, TP:TP + PREV])
                v.tensor_copy(CSO[:, n], seg[:, :, SEG - PREV:])

            def gated_input(g, n):
                dve.wait_ge(decay_done.sem, decay_done.at(g, n + 1))
                v.scalar_tensor_tensor(TR[:], TR[:], 1.0, TH[:], ALU.add, ALU.mult).then_inc(q2_done.sem, 1)
                dve.wait_ge(xc_done.sem, xc_done.at(g, n + 1))
                v.scalar_tensor_tensor(TI[:], TI[:], 1.0, XC[:, n % 2, :], ALU.add, ALU.mult)
                link(g, v.memset(segments(AA[:, S0:])[:, :, PREV - 1], 0.0))

            def recur(g, n):
                dve.wait_ge(q2_root.sem, q2_root.at(g, n + 1))
                link(g, v.tensor_tensor(TI[:], TI[:], TR[:], ALU.mult))
                link(g, v.tensor_copy(segments(TI[:, S0:])[:, :, PREV - 1], HST[:, n]))
                if n >= 4:
                    dve.wait_ge(y_val["y0"].sem, y_val["y0"].at(g, n - 3))
                link(g, v.tensor_tensor_scan(LR[:, n % 4, :], AA[:], TI[:], HC[:, n:n + 1], ALU.mult, ALU.add))
                v.tensor_copy(HSO[:, n], segments(LR[:, n % 4, S0:])[:, :, SEG - 1])
                v.tensor_copy(HC[:, n:n + 1], LR[:, n % 4, TP - 1:TP]).then_inc(lru_done.sem, 1)

            def half_gate(g, c, slot, r):
                product(g, c)
                v.scalar_tensor_tensor(halves(GH[:, slot, :]), pair(PAIR[c]), 0.5, halves(r), ALU.mult,
                                       ALU.mult).then_inc(proj_free.sem, 1)

            def silu(g, i):
                if i < KT:
                    dve.wait_ge(lru_done.sem, lru_done.at(g, i + 1))
                dve.wait_ge(tanh_done.sem, tanh_done.at(g, (i if i < KT else i + KT) + 1))
                tg = TG[:, i % KT % 3, :]
                v.scalar_tensor_tensor(tg, tg, 1.0, GH[:, i % 2, :], ALU.add, ALU.mult)\
                 .then_inc(silu_done.sem, 1)

            def embed(g, c, i, m, o):
                s = m % 2
                dve.wait_ge(tanh_done.sem, tanh_done.at(g, i + 1))
                product(g, c + 1)
                v.scalar_tensor_tensor(halves(GH[:, s, :]), halves(TG[:, s, :]), 1.0, pair(3), ALU.add,
                                       ALU.mult).then_inc(proj_free.sem, 1)
                dve.wait_ge(proj_free.sem, proj_free.at(g, c + 2))
                v.scalar_tensor_tensor(H[:, m, :], GH[:, s, :], 0.5, H[:, m, :], ALU.mult, ALU.add)\
                 .then_inc(h_new[o].sem, 1)

            def final(g, k):
                v.scalar_tensor_tensor(H[:, k, :], H[:, k, :], VEC[:, V_FIN + k:V_FIN + k + 1], R[:], ALU.mult,
                                       ALU.mult).then_inc(y_fin.sem, 1)

            def row_max(g, ev, sc, sink):
                s = ev if ev == 0 else 1 + (ev - 1) % 3
                link(g, v.tensor_reduce(MX[:, s, :], sc, AX_X, ALU.max))
                link(g, v.tensor_tensor(MX[:, s, :], MX[:, s, :], VEC[:, sink:sink + 4], ALU.max))
                v.tensor_scalar(NM[:, s, :], MX[:, s, :], -1.0, None, ALU.mult)
                v.tensor_tensor(ES[:, s, :], VEC[:, sink:sink + 4], MX[:, s, :], ALU.subtract).then_inc(nm_ready.sem, 1)

            def scores(g, u):
                quad, b = divmod(u, NB)
                sc = SC[:, u % 3]
                dve.wait_ge(s_done.sem, s_done.at(g, u + 2))
                for i in range(4):
                    ins = v.scalar_tensor_tensor(sc[:, i, :].rearrange("p (h k) -> p h k", h=2),
                                                 DIST[:, 1:3, :] if b else DIST[:, 0:3:2, :],
                                                 -slope(head_at(2 * quad + i % 2, i // 2)),
                                                 PSUM[:, 4 + i // 2, (i % 2) * 2 * BLK:(i % 2 + 1) * 2 * BLK]
                                                 .rearrange("p (h k) -> p h k", h=2),
                                                 ALU.mult, ALU.add)
                ins.then_inc(s_read.sem, 1)
                dve.wait_ge(s_read.sem, s_read.at(g, u + 2))
                row_max(g, u + 1, sc, V_SINK + 4 * quad)

            def divide(g, ev, sc, width):
                s = ev if ev == 0 else 1 + (ev - 1) % 3
                dve.wait_ge(exp_done.sem, exp_done.at(g, ev + 1))
                link(g, v.tensor_tensor(DEN[:, s, :], DEN[:, s, :], ES[:, s, :], ALU.add))
                link(g, v.reciprocal(DEN[:, s, :], DEN[:, s, :]))
                for i in range(4):
                    ins = v.tensor_scalar(sc[:, i, 0:width], sc[:, i, 0:width], DEN[:, s, i:i + 1], None, ALU.mult)
                ins.then_inc(p_ready.sem, 1)

            n_set = [0]

            def setup(ins):
                n_set[0] += 1
                ins.then_inc(dve_setup.sem, 1)
                dve.wait_ge(dve_setup.sem, n_set[0])

            for n in range(FREE_HEAD):
                v.memset(MX[:, n, :], 0.0).then_inc(proj_free.sem, 1)
            dve.wait_ge(vec_in.sem, 16)
            lam = VEC[:, V_LAM:V_LAM + KT]
            setup(v.tensor_scalar(SP[:, 5, :], lam, -1.0, None, ALU.mult))
            setup(v.tensor_tensor(SP[:, 0, :], lam, SP[:, 5, :], ALU.max))
            setup(v.tensor_scalar(VEC[:, V_BR:V_BR + 2 * KT], VEC[:, V_BR:V_BR + 2 * KT], 0.5, None, ALU.mult))
            dve.wait_ge(act_setup.sem, 1)
            for k in range(KT):
                low(0, "in0", k, Alo, Ahi, H[:, k, :], V_G0 + k)
            y = SP[:, 1, :]
            setup(v.tensor_scalar(SP[:, 2, :], y, 2.0, None, ALU.add))
            setup(v.reciprocal(SP[:, 2, :], SP[:, 2, :]))
            setup(v.tensor_tensor(SP[:, 2, :], SP[:, 2, :], y, ALU.mult))
            z, z2, q = SP[:, 2, :], SP[:, 3, :], SP[:, 4, :]
            setup(v.tensor_tensor(z2, z, z, ALU.mult))
            setup(v.tensor_scalar(q, z2, 1.0 / 17, None, ALU.mult))
            for d in (15, 13, 11, 9, 7, 5, 3):
                setup(v.scalar_tensor_tensor(q, q, 1.0 / d, z2, ALU.add, ALU.mult))
            setup(v.scalar_tensor_tensor(q, q, 1.0, z, ALU.add, ALU.mult))
            setup(v.tensor_scalar(SP[:, 5, :], SP[:, 5, :], 0.0, None, ALU.max))
            setup(v.scalar_tensor_tensor(q, q, 2.0, SP[:, 5, :], ALU.mult, ALU.add))
            setup(v.tensor_scalar(C1[:, 0, :], q, -4.0, None, ALU.mult))
            setup(v.tensor_scalar(C1[:, 1, :], q, 4.0, None, ALU.mult))
            dve.wait_ge(memset_done.sem, 8)
            with dve.Fori(0, GROUPS) as g:
                chain[0] = 0
                dve.wait_ge(lo["in0"].sem, lo["in0"].at(g, KT))
                link(g, v.memset(XB[:, :, PREV + TP:PREV + S0], 0.0))
                for c in range(NBLK):
                    kind, m = ORDER[c]
                    if kind == "g":
                        continue
                    if c == 0:
                        dve.wait_ge(consts_in.sem, CONSTS * 16)
                    if c and ORDER[c - 1][0] == "G":
                        silu(g, ORDER[c - 1][1])
                    if c in RI_BEFORE and c in RECUR_AT:
                        gated_input(g, RI_BEFORE[c])
                    if kind == "X":
                        conv(g, m, PAIR[c])
                    if c in RI_BEFORE and c not in RECUR_AT:
                        gated_input(g, RI_BEFORE[c])
                    if c == 4:
                        inverse(g, N_FIN, R[:])
                    if kind == "G":
                        half_gate(g, c, m % 2, RN[:])
                    if c in RECUR_AT:
                        recur(g, RECUR_AT[c])
                    if 5 <= c < 9:
                        final(g, 2 * (c - 5))
                        final(g, 2 * (c - 5) + 1)
                    if kind in "Oo":
                        o, V_P, dl, dh = ("pl0", V_P0, Alo, Ahi) if kind == "O" else ("pl1", V_P1, Blo, Bhi)
                        if c == O0:
                            dve.wait_ge(h_in.sem, h_in.at(g, 1))
                        product(g, c)
                        v.tensor_tensor(halves(H[:, m, :]), pair(PAIR[c]), halves(H[:, m, :]), ALU.add)\
                         .then_inc(proj_free.sem, 1)
                        if m:
                            low(g, o, m - 1, dl, dh, H[:, m - 1, :], V_P + m - 1)
                        if m == KT - 1:
                            low(g, o, m, dl, dh, H[:, m, :], V_P + m)
                            l = int(kind == "o")
                            dve.wait_ge(p_hi.sem, p_hi.at(g, l + 1))
                            v.tensor_tensor(Plo[:], PS_[:], Phi[:].bitcast(F32), ALU.subtract).then_inc(p_lo.sem, 1)
                    if kind in "Zz":
                        i = (KT if kind == "Z" else 3 * KT) + m
                        if m == 0:
                            inverse(g, N_PL0 if kind == "Z" else N_PL1, R[:])
                        half_gate(g, c, m % 2, R[:])
                        if kind == "Z" and m:
                            low(g, "in1", m - 1, Blo, Bhi, H[:, m - 1, :], V_G1 + m - 1)
                        if kind == "z":
                            for k in ((0, 1) if m == 0 else (m + 1,)):
                                if k < KT:
                                    low((g, 1), "in0", k, Alo, Ahi, XS[:, k % 2, :], V_G0 + k)
                        embed(g, c, i, m, "in1" if kind == "Z" else "fin")
                        if m == KT - 1 and kind == "Z":
                            low(g, "in1", m, Blo, Bhi, H[:, m, :], V_G1 + m)
                    if kind == "k":
                        if m == 0:
                            inverse(g, N_IN1, R[:])
                            dve.wait_ge(state_out.sem, state_out.at(g, 2))
                        p = PAIR[c]
                        product(g, c)
                        v.tensor_tensor(K[:, m, 0:C], PSUM[:, 2 * p, 0:C], R[:, 0:C], ALU.mult)
                        v.tensor_tensor(K[:, m, C:TP], PSUM[:, 2 * p + 1, 0:TB], R[:, C:TP], ALU.mult)
                        v.tensor_tensor(KS[:, m, :, WIN:], samples(PSUM[:, 2 * p + 1, TB:C]), samples(R[:, TP:T]),
                                        ALU.mult).then_inc(proj_free.sem, 1)
                    if kind == "v":
                        product(g, c)
                        v.tensor_tensor(halves(VT[:, m, :]), pair(PAIR[c]), halves(R[:]), ALU.mult)\
                         .then_inc(proj_free.sem, 1)
                    if kind == "q":
                        product(g, c)
                        v.scalar_tensor_tensor(halves(Q[:, m, :]), pair(PAIR[c]), HD ** -0.5, halves(R[:]),
                                               ALU.mult, ALU.mult).then_inc(proj_free.sem, 1)
                        if m == KT - 1:
                            dve.wait_ge(proj_free.sem, proj_free.at(g, c + 1))
                            for s in range(SG):
                                ins = v.tensor_copy(
                                    QS[:, s, :, 0:2 * ST].rearrange("p k (j t) -> p k j t", t=ST),
                                    Q[:, :, TP + s * ST:TP + (s + 1) * ST].rearrange("p (k j) t -> p k j t", j=2))
                            ins.then_inc(q_ready.sem, 1)
                    if c == G1 - 1:
                        dve.wait_ge(k_out.sem, k_out.at(g, 1))
                        ss = SC[:, 2].rearrange("p a b -> p (a b)")[:, 0:4 * SW]
                        s4 = ss.rearrange("p (i w) -> p i w", w=SW)
                        dve.wait_ge(s_done.sem, s_done.at(g, 1))
                        v.tensor_tensor(ss.rearrange("p (a w) -> p a w", a=2), PSUM[:, 4:6, 0:SG * SW], TBS[:],
                                        ALU.add).then_inc(s_read.sem, 1)
                        dve.wait_ge(s_read.sem, s_read.at(g, 1))
                        row_max(g, 0, s4, V_SINKS)
                        half_gate(g, G1, 0, R[:])
                        divide(g, 0, s4, SW)
                        scores(g, 0)
                        silu(g, KT)
                        for u in range(NU):
                            quad, b = divmod(u, NB)
                            if u + 1 < NU:
                                scores(g, u + 1)
                            if u == 0:
                                dve.wait_ge(o_done.sem, o_done.at(g, 1))
                                v.tensor_copy(OS[:].rearrange("p a b -> p (a b)"),
                                              PSUM[:, 6, 0:KT * TS]).then_inc(os_read.sem, 1)
                            divide(g, u + 1, SC[:, u % 3], 2 * BLK)
                            if u - 2 in WHOLE:
                                silu(g, KT + WHOLE[u - 2])
                            if u - 1 in WHOLE:
                                j = WHOLE[u - 1]
                                half_gate(g, G1 + j, j % 2, R[:])
                        half_gate(g, G1 + KT - 1, 1, R[:])
                        silu(g, 2 * KT - 1)
                        for t in (Khi, Klo):
                            v.tensor_copy(t[:, :, 0:BLK], t[:, :, TP:TP + BLK])
                        v.tensor_copy(V[:, 0, :], V[:, NB, :])
                        v.tensor_copy(DIST[:, 0, :], DIST[:, 1, :]).then_inc(carry_done.sem, 1)
                assert chain[0] == DVE_CHAIN, chain[0]
            chain[0] = 0
            dve.wait_ge(root_done.sem, root_done.at(GROUPS, 1))
            link(GROUPS, v.reciprocal(R[:], R[:]))
            for k in range(KT):
                final(GROUPS, k)

        @block.tensor
        def _(pe):
            def project(g, c, hi_t, lo_t, ready, k0=0, k1=None):
                nk = 2 if is_small(c) else KT
                k1 = nk if k1 is None else k1
                if k0 == 0:
                    pe.wait_ge(w_lo.sem, w_lo.at(g, c + 1))
                    pe.wait_ge(proj_free.sem, proj_free.at(g, before_in_pair(c) + 1))
                s, p = c % RING, PAIR[c]
                for k in range(k0, k1):
                    if ready is not None:
                        pe.wait_ge(ready.sem, ready.at(g, k + 1))
                    for n, (w, x) in enumerate(((WH, hi_t), (WH, lo_t), (WL, hi_t))):
                        for a in range(2):
                            ins = nc.tensor.matmul(PSUM[:, 2 * p + a, 0:C], w[:, s, k, :], x[:, k, a * C:(a + 1) * C],
                                                   start=(k == 0 and n == 0), stop=(k == nk - 1 and n == 2))
                if k1 == nk:
                    ins.then_inc(proj_done.sem, 1)

            def mean_square(g, o, acc, roots):
                pe.wait_ge(added[o].sem, added[o].at(g, KT - 1))
                if roots:
                    pe.wait_ge(root_done.sem, root_done.at(g, roots))
                for a in range(2):
                    ins = nc.tensor.matmul(PSUM[:, 4 + a, 0:C], ONE[:], acc[:, a * C:(a + 1) * C], start=True, stop=True)
                ins.then_inc(ms_done.sem, 1)

            def final_sum(g):
                pe.wait_ge(added["fin"].sem, added["fin"].at(g, 0))
                pe.wait_ge(proj_free.sem, proj_free.at(g, 0))
                for a in range(2):
                    ins = nc.tensor.matmul(PSUM[:, 6 + a, 0:C], ONE[:], ACC[:, a * C:(a + 1) * C], start=True, stop=True)
                ins.then_inc(ms_done.sem, 1)

            def static_wait():
                pe.wait_ge(memset_done.sem, 8)

            def gate_products(g, n):
                pe.wait_ge(xc_done.sem, xc_done.at(g, n + 1))
                if n == 0:
                    pe.wait_ge(root_done.sem, root_done.at(g, N_FIN + 1))
                else:
                    pe.wait_ge(ri_read.sem, ri_read.at(g, n))
                hw = FLAT // 2
                for w in range(2):
                    for a in range(2):
                        ins = nc.tensor.matmul(PSUM[:, 4 + 2 * w + a, 0:hw], WRI[:, w * KT + n, :],
                                               XC[:, n % 2, a * hw:(a + 1) * hw], start=True, stop=True)
                ins.then_inc(ri_done.sem, 1)

            def turn_values(g, t):
                pe.wait_ge(proj_free.sem, proj_free.at(g, AT["v", t] + 1))
                if t == 0:
                    pe.wait_ge(root_done.sem, root_done.at(g, N_IN1 + 1))
                for b in range(NB):
                    nc.tensor.transpose(PSUM[:, 6 + t, b * 128:(b + 1) * 128], VT[:, t, b * BLK:(b + 1) * BLK], IDN[:])
                for s in range(SG):
                    ins = nc.tensor.matmul(PSUM[0:ST, 4 + t, s * 128:(s + 1) * 128],
                                           VT[:, t, TP + s * ST:TP + (s + 1) * ST], IDN[:], start=True, stop=True)
                ins.then_inc(v_turned.sem, 1)

            def unit_scores(g, u):
                quad, b = divmod(u, NB)
                pe.wait_ge(s_read.sem, s_read.at(g, u + 1))
                for j in range(2):
                    for par in range(2):
                        h0 = 64 * par
                        for n, (q, keys) in enumerate(((Ahi, Khi), (Ahi, Klo), (Alo, Khi))):
                            ins = nc.tensor.matmul(PSUM[:, 4 + par, j * 2 * BLK:(j + 1) * 2 * BLK],
                                                   q[h0:h0 + 64, 2 * quad + j, b * BLK:(b + 1) * BLK],
                                                   keys[h0:h0 + 64, quad // 2, b * BLK:(b + 2) * BLK],
                                                   start=(n == 0), stop=(n == 2))
                ins.then_inc(s_done.sem, 1)

            def unit_turn(g, u):
                pe.wait_ge(p_ready.sem, p_ready.at(g, u + 2))
                if u:
                    pe.wait_ge(o_read.sem, o_read.at(g, u))
                else:
                    pe.wait_ge(os_read.sem, os_read.at(g, 1))
                for h in range(2):
                    for i in range(4):
                        ins = nc.tensor.transpose(PSUM[:, 6 + h, i * BLK:(i + 1) * BLK],
                                                  SC[:, u % 3, i, h * BLK:(h + 1) * BLK], IDN[:])
                ins.then_inc(t_done.sem, 1)

            def unit_values(g, u):
                quad, b = divmod(u, NB)
                pe.wait_ge(pt_ready.sem, pt_ready.at(g, u + 2))
                static_wait()
                for par in range(2):
                    kv = 2 * (quad // 2) + par
                    for h in range(2):
                        ins = nc.tensor.matmul(PSUM[64 * par:64 * par + 64, 6, 0:2 * BLK],
                                               V[:, b + h, kv * HD:(kv + 1) * HD],
                                               PT[:, h, 2 * par * BLK:2 * (par + 1) * BLK], start=(h == 0), stop=(h == 1))
                ins.then_inc(o_done.sem, 1)

            def sample_scores(g):
                for quad in range(NKV):
                    for s in range(SG):
                        for par in range(2):
                            h0 = 64 * par
                            ins = nc.tensor.matmul(PSUM[32 * quad:32 * quad + 32, 4 + par, s * SW:(s + 1) * SW],
                                                   QS[h0:h0 + 64, s, quad, :], KS[h0:h0 + 64, quad // 2, s, :],
                                                   start=True, stop=True)
                ins.then_inc(s_done.sem, 1)

            def sample_turn(g):
                pe.wait_ge(p_ready.sem, p_ready.at(g, 1))
                ss = SC[:, 2].rearrange("p a b -> p (a b)")
                for i in range(4):
                    nc.tensor.transpose(PSUM[:, 6, i * 128:(i + 1) * 128], ss[:, i * SW:i * SW + WIN], IDN[:])
                for i in range(4):
                    ins = nc.tensor.matmul(PSUM[0:ST, 7, i * 128:(i + 1) * 128], ss[:, i * SW + WIN:(i + 1) * SW],
                                           IDN[:], start=True, stop=True)
                ins.then_inc(t_done.sem, 1)

            def sample_values(g):
                pe.wait_ge(pt_ready.sem, pt_ready.at(g, 1))
                static_wait()
                out = PSUM[:, 6, 0:KT * TS].rearrange("p (m s t) -> p m s t", m=KT, s=SG)
                for par in range(2):
                    for s in range(SG):
                        for quad in range(NKV):
                            i, kv = SG * par + s, 2 * (quad // 2) + par
                            o = out[64 * par:64 * par + 64, 2 * quad:2 * quad + 2, s, :]
                            cols = slice(i * 128 + 32 * quad, i * 128 + 32 * quad + 2 * ST)
                            nc.tensor.matmul(o, VS[:, s, kv * HD:(kv + 1) * HD], PT[:, 0, cols], start=True, stop=False)
                            ins = nc.tensor.matmul(o, VN[0:ST, s, kv * HD:(kv + 1) * HD], PT[0:ST, 1, cols],
                                                   start=False, stop=True)
                ins.then_inc(o_done.sem, 1)

            pe.wait_ge(memset_done.sem, 8)
            nc.tensor.matmul(PSUM[:, 0, 0:128], ONE[:], ONE[:], start=True, stop=True).then_inc(proj_done.sem, 1)
            with pe.Fori(0, GROUPS) as g:
                for c in range(NBLK):
                    kind, m = ORDER[c]
                    if c == RI_FIRST:
                        pe.wait_ge(consts_in.sem, CONSTS * 16)
                    if c in RI_BEFORE and RI_BEFORE[c] not in RI_INSIDE:
                        gate_products(g, RI_BEFORE[c])
                    if c == G1 - 1:
                        pe.wait_ge(k_lo.sem, k_lo.at(g, 2))
                        pe.wait_ge(ks_in.sem, ks_in.at(g, 2))
                        pe.wait_ge(v_ready.sem, v_ready.at(g, 2))
                    if c < 2:
                        ready = None if c else lo["in0"]
                        project(g, c, Ahi, Alo, ready, 0, KT // 2)
                        if c:
                            final_sum(g)
                        else:
                            mean_square(g, "in0", ACCN, 0)
                        project(g, c, Ahi, Alo, ready, KT // 2)
                    elif RI_BEFORE.get(c) in RI_INSIDE:
                        project(g, c, Ahi, Alo, None, 0, KT // 2)
                        gate_products(g, RI_BEFORE[c])
                        project(g, c, Ahi, Alo, None, KT // 2)
                    elif kind in "XG":
                        project(g, c, Ahi, Alo, None)
                    elif kind in "Oo":
                        a, b, o = (Bhi, Blo, "y0") if kind == "O" else (Ahi, Alo, "y1")
                        if m == 0:
                            for k0, k1 in ((0, KT - 2), (KT - 2, KT)):
                                project(g, c, a, b, lo[o], k0, k1)
                                project(g, c + 1, a, b, None, k0, k1)
                        if m > 1:
                            project(g, c, a, b, None)
                    elif kind in "Pp":
                        if m == 0:
                            pe.wait_ge(p_lo.sem, p_lo.at(g, 1 + (kind == "p")))
                        project(g, c, Phi, Plo, None)
                    elif kind in "Zzkvq":
                        a, b, o = (Ahi, Alo, "pl0") if kind == "Z" else (Bhi, Blo, "pl1" if kind == "z" else "in1")
                        if c == L1:
                            project(g, c, a, b, lo[o], 0, KT - 2)
                            project(g, c + 1, a, b, None, 0, KT - 2)
                            project(g, c, a, b, lo[o], KT - 2)
                            mean_square(g, o, ACC, N_IN1)
                            project(g, c + 1, a, b, None, KT - 2)
                        elif c in (Z0, Z1):
                            project(g, c, a, b, lo[o])
                            mean_square(g, o, ACC, {Z0: N_PL0, Z1: N_PL1}[c])
                        elif c != L1 + 1:
                            project(g, c, a, b, None)
                    if c == Q1:
                        turn_values(g, 0)
                    if c == Q1 + 1:
                        turn_values(g, 1)
                    if c == G1 - 1:
                        project(g, G1, Bhi, Blo, None, 0, KT // 2)
                        pe.wait_ge(q_ready.sem, q_ready.at(g, 1))
                        project(g, G1, Bhi, Blo, None, KT // 2)
                        sample_scores(g)
                        project(g, G1 + 1, Bhi, Blo, None, 0, KT // 2)
                        pe.wait_ge(q_lo.sem, q_lo.at(g, KT))
                        unit_scores(g, 0)
                        project(g, G1 + 1, Bhi, Blo, None, KT // 2)
                        sample_turn(g)
                        unit_scores(g, 1)
                        sample_values(g)
                        for u in range(NU):
                            if u + 2 < NU:
                                unit_scores(g, u + 2)
                            unit_turn(g, u)
                            k = 2 * KT + FILL * u
                            end = k + FILL
                            while k < end:
                                stop = min(end, (k // KT + 1) * KT)
                                project(g, G1 + k // KT, Bhi, Blo, None, k % KT, stop - k // KT * KT)
                                k = stop
                            unit_values(g, u)
            final_sum(GROUPS)


def kernel(**inputs):
    import numpy as np
    import concourse.bacc as bacc
    from concourse.bass_utils import run_bass_kernel_spmd

    i = {k: np.ascontiguousarray(v) for k, v in inputs.items()}

    def by_group(prompt, sample, extra=0):
        f = prompt.shape[-1]
        out = np.zeros((GROUPS + extra, T, f), np.float32)
        out[:GROUPS, :TP] = prompt.reshape(GROUPS, TP, f)
        out[:GROUPS, TP:] = sample.reshape(GROUPS, TS, f)
        return np.ascontiguousarray(out.reshape(-1, T, f // 128, 128).transpose(0, 3, 2, 1))

    def w_block(w, m):
        return w[:, m * 128:(m + 1) * 128].reshape(-1, 128, 128).transpose(1, 0, 2)

    win_a, win_b = i["w_in_a"][0], i["w_in_b"][0]
    order = np.concatenate([head_at(t, par) * HD + np.arange(HD) for t in range(KT) for par in range(2)])
    att = D + 2 * NKV * HD
    win_b = np.concatenate([win_b[:, order], win_b[:, D:att], win_b[:, att + order]], axis=1)
    take = {"X": (win_a, 0), "G": (win_a, KT), "O": (i["w_out_a"][0], 0), "Z": (i["w_ple_gate"][0], 0),
            "P": (i["w_ple_proj"][0], 0), "q": (win_b, 0), "k": (win_b, KT), "v": (win_b, KT + 2),
            "g": (win_b, KT + 4), "o": (i["w_out_b"][0][order], 0), "z": (i["w_ple_gate"][1], 0),
            "p": (i["w_ple_proj"][1], 0)}
    big = np.stack([w_block(take[k][0], take[k][1] + m) for k, m in ORDER if k not in "Pp"])
    small = np.stack([w_block(take[k][0], m) for k in "Pp" for m in range(KT)])

    def cols(v):
        return v.reshape(KT, 128).T

    heads = np.array([head_at(2 * quad + j, par) for quad in range(NKV) for par in range(2) for j in range(2)])
    sinks = i["sinks"][0]
    row_head = np.zeros((128, 2), np.int64)
    bias_s = np.zeros((128, 2, SG, SW), np.float32)
    key = np.arange(SW)
    for quad in range(NKV):
        for j in range(2):
            for t in range(ST):
                r = 32 * quad + ST * j + t
                dist = WIN + t - key
                for par in range(2):
                    h = head_at(2 * quad + j, par)
                    row_head[r, par] = h
                    bias_s[r, par] = np.where((dist >= 0) & (dist < WIN), -slope(h) * dist, -1e30)
    vec = np.concatenate(
        [cols(i["norm_g"][0]), cols(i["norm_g"][1]), cols(i["ple_norm_g"][0]), cols(i["ple_norm_g"][1]),
         cols(i["final_norm_g"])] + [cols(i["conv_w_a"][0][k]) for k in range(TAPS)]
        + [cols(i[n][0]) for n in ("conv_b_a", "b_rgate", "b_igate", "lru_lambda")]
        + [np.broadcast_to(sinks[heads], (128, NH)), np.repeat(sinks[row_head], SG, axis=1)], axis=1)
    q, s = np.arange(BLK)[:, None], np.arange(2 * BLK)[None]
    d = BLK + q - s
    dist = np.where((d >= 0) & (d < WIN), d, MASKED).astype(np.float32)
    w_ri = np.concatenate([i["w_rgate"][0], i["w_igate"][0]]).transpose(1, 0, 2)
    ck, cv = (i[n][0].reshape(GROUPS, SG, WIN, NKV * HD) for n in ("cache_k", "cache_v"))
    k_cache = ck.reshape(GROUPS, SG, WIN, 2, 128).transpose(0, 4, 3, 1, 2)
    arrays = {
        "x": by_group(i["x_prompt"][0], i["x_sample"], 1),
        "p0": by_group(i["p_prompt"][0, 0], i["p_sample"][0]),
        "p1": by_group(i["p_prompt"][1, 0], i["p_sample"][1]),
        "w_big": big, "w_small": small, "w_ri": w_ri, "vec": vec,
        "dist": np.stack([np.full((BLK, BLK), MASKED, np.float32), dist[:, :BLK], dist[:, BLK:]], axis=1),
        "bias_s": bias_s.reshape(128, 2, SG * SW),
        "ident": np.eye(128, dtype=np.float32),
        "h_state": i["state_lru_h"][0].reshape(GROUPS, SG, KT, 128).transpose(0, 3, 2, 1),
        "conv_state": i["state_conv"][0].reshape(GROUPS, SG, PREV, KT, 128).transpose(0, 4, 3, 1, 2),
        "k_cache": k_cache,
        "v_cache": cv.transpose(0, 2, 1, 3),
    }
    arrays = {k: np.ascontiguousarray(v) for k, v in arrays.items()}
    outs = {
        "y_out": (GROUPS + 1, 128, KT, T), "h_out": (128, KT), "conv_out": (128, KT, PREV),
        "k_out": (GROUPS, 128, 2, BLK), "v_out": (BLK, NKV * HD), "h_state_out": (GROUPS, 128, KT, SG),
        "conv_state_out": (GROUPS, 128, KT, SG, PREV), "ks_out": (GROUPS, 128, 2, SG, WIN),
        "vs_out": (GROUPS, WIN, SG, NKV * HD),
    }
    nc = bacc.Bacc("TRN2", target_bir_lowering=False, num_devices=1)
    aps = {k: nc.dram_tensor(k, v.shape, F32, kind="ExternalInput").ap() for k, v in arrays.items()}
    aps.update({k: nc.dram_tensor(k, v, F32, kind="ExternalOutput").ap() for k, v in outs.items()})
    build(nc, aps)
    r = run_bass_kernel_spmd(nc, [arrays], core_ids=[0]).results[0]
    y = r["y_out"][1:].transpose(0, 3, 2, 1).reshape(GROUPS, T, D)
    return (
        y[:, :TP].reshape(1, SEQ, D),
        y[:, TP:].reshape(NSEQ, ST, D),
        r["h_out"].T.reshape(1, 1, D),
        r["conv_out"].transpose(2, 1, 0).reshape(1, 1, PREV, D),
        r["k_out"][-1].transpose(2, 1, 0).reshape(1, 1, WIN, NKV, HD),
        r["v_out"].reshape(1, 1, WIN, NKV, HD),
        r["h_state_out"].transpose(0, 3, 2, 1).reshape(1, NSEQ, D),
        r["conv_state_out"].transpose(0, 3, 4, 2, 1).reshape(1, NSEQ, PREV, D),
        r["ks_out"].transpose(0, 3, 4, 2, 1).reshape(1, NSEQ, WIN, NKV, HD),
        r["vs_out"].transpose(0, 2, 1, 3).reshape(1, NSEQ, WIN, NKV, HD),
    )
```
